# Optimizing a Trainium2 kernel written in Bass

```python
import math
import jax, jax.numpy as jnp
from jax import lax
import numpy as np

D_MODEL = 1024
BATCH = 1
SEQ = 128
DEPTH = 2
DEC_BATCH = 1
DEC_SEQ = 256
PAST_LEN = 128

GRID_W = 64
N_AB = (DEPTH + 1) // 2
N_C = DEPTH // 2
EPS = 1e-6
RW_HEADS = 8
RW_HEAD = 64
RW_DIM = RW_HEADS * RW_HEAD
W_LORA = 64
A_LORA = 64
G_LORA = 128
LNX_EPS = 64e-5
RW_IN = 3 * RW_DIM + W_LORA + A_LORA + G_LORA
RW_SPLITS = (RW_DIM, 2 * RW_DIM, 3 * RW_DIM, 3 * RW_DIM + W_LORA, 3 * RW_DIM + W_LORA + A_LORA)
MLA_HEADS = 4
QK_NOPE = 128
QK_ROPE = 64
QK_HEAD = QK_NOPE + QK_ROPE
V_HEAD = 128
Q_LORA = 256
KV_LORA = 128
MLA_DIM = MLA_HEADS * V_HEAD
MLA_IN = Q_LORA + KV_LORA + QK_ROPE
AB_IN = RW_IN + MLA_IN
ROPE_THETA = 10000.0
Q_BLOCK = 128
HY_SHORT = 3
HY_BANDS = 16
HY_EMB = 1 + 2 * HY_BANDS
HY_HIDDEN = 64
HY_TARGET = 1e-2
HY_FAST = 0.3
HY_SLOW = 1.5
PEER_KEYS = 128
PEER_N = PEER_KEYS * PEER_KEYS
PEER_HEADS = 8
PEER_DKEY = 256
PEER_TOPK = 16
TOKEN_BLOCK = 128

kernel_name = 'rwkv7_mla_hyena_peer_prefix_diffusion_step'

def rmsnorm(x, g):
    xf = x.astype(jnp.float32)
    y = xf * lax.rsqrt(jnp.mean(xf * xf, axis=-1, keepdims=True) + EPS)
    return (y * g.astype(jnp.float32)).astype(x.dtype)

def modulate(h, shift, scale):
    return h * (1.0 + scale) + shift

def centred_shift(x):
    prev = jnp.pad(x[:, :-1], ((0, 0), (1, 0), (0, 0)))
    nxt = jnp.pad(x[:, 1:], ((0, 0), (0, 1), (0, 0)))
    return 0.5 * (prev + nxt)

def centred_dwconv3(u, w, b):
    prev = jnp.pad(u[:, :-1], ((0, 0), (1, 0), (0, 0)))
    nxt = jnp.pad(u[:, 1:], ((0, 0), (0, 1), (0, 0)))
    return prev * w[0] + u * w[1] + nxt * w[2] + b

def axial_rope(L):
    rows = L // GRID_W
    row = jnp.repeat(jnp.arange(rows, dtype=jnp.float32), GRID_W)
    col = jnp.tile(jnp.arange(GRID_W, dtype=jnp.float32), rows)
    n_freq = QK_ROPE // 4
    inv = ROPE_THETA ** (-jnp.arange(n_freq, dtype=jnp.float32) / n_freq)
    ang = jnp.concatenate([row[:, None] * inv, col[:, None] * inv], axis=-1)
    return jnp.cos(ang), jnp.sin(ang)

def rope_tail(x, cos, sin):
    xn, xr = x[..., :QK_NOPE], x[..., QK_NOPE:]
    x1, x2 = xr[..., 0::2], xr[..., 1::2]
    cs = cos[None, :, None, :].astype(x.dtype)
    sn = sin[None, :, None, :].astype(x.dtype)
    rot = jnp.stack([x1 * cs - x2 * sn, x1 * sn + x2 * cs], axis=-1).reshape(xr.shape)
    return jnp.concatenate([xn, rot], axis=-1)

def attend(q, k, v):
    B, Lq, H, Dh = q.shape
    nb = Lq // Q_BLOCK
    qb = q.reshape(B, nb, Q_BLOCK, H, Dh).transpose(1, 0, 2, 3, 4)
    scale = Dh ** -0.5

    def blk(qi):
        s = jnp.einsum('bqhd,bkhd->bhqk', qi, k).astype(jnp.float32) * scale
        p = jax.nn.softmax(s, axis=-1).astype(v.dtype)
        return jnp.einsum('bhqk,bkhd->bqhd', p, v)

    o = lax.map(blk, qb)
    return o.transpose(1, 0, 2, 3, 4).reshape(B, Lq, H * v.shape[-1])

def rwkv7_scan(r, w, k, v, a, b, s0, reverse):
    def step(s, inp):
        r_t, w_t, k_t, v_t, a_t, b_t = inp
        sa = jnp.einsum('bhvk,bhk->bhv', s, a_t)
        s = s * w_t[:, :, None, :] + sa[..., None] * b_t[:, :, None, :] + v_t[..., None] * k_t[:, :, None, :]
        return s, jnp.einsum('bhvk,bhk->bhv', s, r_t)

    xs = tuple(jnp.swapaxes(t.astype(jnp.float32), 0, 1) for t in (r, w, k, v, a, b))
    s_fin, ys = lax.scan(step, s0.astype(jnp.float32), xs, reverse=reverse)
    return jnp.swapaxes(ys, 0, 1), s_fin

def mla_keys(ckv, k_pe, kv_up, kn):
    B, L, _ = ckv.shape
    kv = (ckv @ kv_up).reshape(B, L, MLA_HEADS, QK_NOPE + V_HEAD)
    k_rope = jnp.broadcast_to(k_pe[:, :, None, :], (B, L, MLA_HEADS, QK_ROPE))
    k = rmsnorm(jnp.concatenate([kv[..., :QK_NOPE], k_rope], axis=-1), kn)
    return k, kv[..., QK_NOPE:]

def rwkv_mla_mixer(h, ctx, p):
    (w_in, mu, w0, w2, a0, a2, g2, k_k, k_a, r_k, lnx_g, lnx_b,
     q_norm, q_up, kv_norm, kv_up, qn, kn, w_out) = p
    B, L, _ = h.shape
    f32 = jnp.float32
    proj = h @ w_in
    rw, mla = proj[..., :RW_IN], proj[..., RW_IN:]
    rw = rw + mu * (centred_shift(rw) - rw)
    r, k, v, wd, ad, gd = jnp.split(rw, RW_SPLITS, axis=-1)
    heads = lambda t: t.reshape(B, L, RW_HEADS, RW_HEAD)
    rh, vh = heads(r.astype(f32)), heads(v.astype(f32))
    kk = heads((k * k_k).astype(f32))
    kk = kk / jnp.maximum(jnp.linalg.norm(kk, axis=-1, keepdims=True), 1e-12)
    if ctx is None:
        z = jnp.zeros((B, RW_HEADS, RW_HEAD, RW_HEAD), f32)
        s0s = (z, z)
    else:
        s0s = (ctx[0], ctx[1])
    ys, finals, bonus = [], [], []
    for d in range(2):
        w_raw = (w0[d] + jnp.tanh(wd) @ w2[d]).astype(f32)
        decay = jnp.exp(-jnp.exp(-jax.nn.softplus(-w_raw) - 0.5))
        lr = jax.nn.sigmoid((a0[d] + ad @ a2[d]).astype(f32))
        kd = heads(k.astype(f32) * (1.0 + (lr - 1.0) * k_a))
        yd, sd = rwkv7_scan(rh, heads(decay), kd, vh, -kk, kk * heads(lr), s0s[d], d == 1)
        ys.append(yd)
        finals.append(sd)
        bonus.append(jnp.sum(rh * kd * r_k, axis=-1, keepdims=True) * vh)
    y = ys[0] + ys[1]
    mean = jnp.mean(y, axis=-1, keepdims=True)
    var = jnp.mean(jnp.square(y - mean), axis=-1, keepdims=True)
    yn = ((y - mean) * lax.rsqrt(var + LNX_EPS)).reshape(B, L, RW_DIM) * lnx_g + lnx_b
    gate = jax.nn.sigmoid(gd) @ g2
    rw_out = ((yn + (bonus[0] + bonus[1]).reshape(B, L, RW_DIM)) * gate).astype(h.dtype)
    q_c, kv_c, k_pe = jnp.split(mla, (Q_LORA, Q_LORA + KV_LORA), axis=-1)
    q = rmsnorm((rmsnorm(q_c, q_norm) @ q_up).reshape(B, L, MLA_HEADS, QK_HEAD), qn)
    ckv = rmsnorm(kv_c, kv_norm)
    k_own, v_own = mla_keys(ckv, k_pe, kv_up, kn)
    if ctx is None:
        keys, vals = k_own, v_own
    else:
        cos, sin = ctx[4]
        q = rope_tail(q, cos, sin)
        k_own = rope_tail(k_own, cos, sin)
        k_ctx, v_ctx = mla_keys(ctx[2], ctx[3], kv_up, kn)
        keys = jnp.concatenate([k_ctx, k_own], axis=1)
        vals = jnp.concatenate([v_ctx, v_own], axis=1)
    mla_out = attend(q, keys, vals)
    out = jnp.concatenate([rw_out, mla_out.astype(h.dtype)], axis=-1) @ w_out
    return out, finals[0], finals[1], ckv, k_pe

def hyena_filters(L, w1, b1, w2, b2, w3, freq):
    f32 = jnp.float32
    t = jnp.arange(L, dtype=f32)[:, None]
    t_unit = t / (L - 1)
    bands = jnp.linspace(1e-4, HY_BANDS - 1, HY_BANDS, dtype=f32)
    ang = 2.0 * math.pi * t * bands / L
    zpos = jnp.concatenate([t_unit, jnp.cos(ang), -jnp.sin(ang)], axis=-1)
    fr = freq.astype(f32)
    hid = jnp.sin(fr * (zpos @ w1.astype(f32) + b1.astype(f32)))
    hid = jnp.sin(fr * (hid @ w2.astype(f32) + b2.astype(f32)))
    filt = hid @ w3.astype(f32)
    deltas = jnp.linspace(math.log(HY_TARGET) / HY_FAST, math.log(HY_TARGET) / HY_SLOW, D_MODEL, dtype=f32)
    window = jnp.exp(-t_unit * jnp.abs(deltas))
    h_f = filt[:, :D_MODEL] * window
    h_b = filt[:, D_MODEL:] * window
    circ = jnp.concatenate([h_f, jnp.zeros((1, D_MODEL), f32), h_b[:0:-1]], axis=0)
    return circ / jnp.sum(jnp.abs(circ), axis=0, keepdims=True)

def hyena_mixer(h, p):
    w_in, b_in, conv_w, conv_b, f_w1, f_b1, f_w2, f_b2, f_w3, f_freq, bias, w_out = p
    B, L, _ = h.shape
    u = centred_dwconv3(h @ w_in + b_in, conv_w, conv_b)
    x0, x1, v = jnp.split(u, 3, axis=-1)
    zin = (x1 * v).astype(jnp.float32)
    filt_f = jnp.fft.rfft(hyena_filters(L, f_w1, f_b1, f_w2, f_b2, f_w3, f_freq), axis=0)
    conv = jnp.fft.irfft(jnp.fft.rfft(zin, n=2 * L, axis=1) * filt_f, n=2 * L, axis=1)[:, :L]
    y = conv + zin * bias.astype(jnp.float32)
    return (x0 * y.astype(h.dtype)) @ w_out

def peer_ffn(h, w_q, sub_keys, u_tab, v_tab):
    B, L, D = h.shape
    nb = (B * L) // TOKEN_BLOCK

    def blk(xb):
        q = (xb @ w_q).reshape(TOKEN_BLOCK, PEER_HEADS, 2, PEER_DKEY // 2)
        s = jnp.einsum('thpd,hpnd->thpn', q, sub_keys).astype(jnp.float32)
        s1, i1 = lax.top_k(s[:, :, 0], PEER_TOPK)
        s2, i2 = lax.top_k(s[:, :, 1], PEER_TOPK)
        cand = (s1[..., :, None] + s2[..., None, :]).reshape(TOKEN_BLOCK, PEER_HEADS, PEER_TOPK * PEER_TOPK)
        cidx = (i1[..., :, None] * PEER_KEYS + i2[..., None, :]).reshape(TOKEN_BLOCK, PEER_HEADS, PEER_TOPK * PEER_TOPK)
        top_s, pos = lax.top_k(cand, PEER_TOPK)
        idx = jnp.take_along_axis(cidx, pos, axis=-1)
        g = jax.nn.softmax(top_s, axis=-1).astype(xb.dtype)
        act = jax.nn.gelu(jnp.einsum('thkd,td->thk', u_tab[idx], xb))
        return jnp.einsum('thk,thkd->td', g * act, v_tab[idx])

    out = lax.map(blk, h.reshape(nb, TOKEN_BLOCK, D))
    return out.reshape(B, L, D)

def setup_inputs(seed: int = 0) -> dict:
    key = jax.random.key(seed)
    keys = iter(jax.random.split(key, 64))

    def nrm(shape, scale):
        return jax.random.normal(next(keys), shape, jnp.float32) * scale

    def gain(shape):
        return 1.0 + nrm(shape, 0.02)

    D = D_MODEL
    return {
        'x_prompt': nrm((BATCH, SEQ, D), 1.0),
        'x_sample': nrm((DEC_BATCH, DEC_SEQ, D), 1.0),
        'state_rwkv_fwd': nrm((DEC_BATCH, N_AB, RW_HEADS, RW_HEAD, RW_HEAD), 0.5),
        'state_rwkv_bwd': nrm((DEC_BATCH, N_AB, RW_HEADS, RW_HEAD, RW_HEAD), 0.5),
        'cache_mla_ckv': nrm((DEC_BATCH, N_AB, PAST_LEN, KV_LORA), 1.0),
        'cache_mla_kpe': nrm((DEC_BATCH, N_AB, PAST_LEN, QK_ROPE), 1.0),
        'c': nrm((DEC_BATCH, D), 1.0),
        'c_ctx': nrm((D,), 1.0),
        'norm_g': gain((DEPTH, 2, D)),
        'w_mod': nrm((DEPTH, D, 6 * D), D ** -0.5),
        'b_mod': nrm((DEPTH, 6 * D), 0.02),
        'ab_w_in': nrm((N_AB, D, AB_IN), D ** -0.5),
        'rw_mu': jax.random.uniform(next(keys), (N_AB, RW_IN), jnp.float32, 0.1, 0.9),
        'rw_w0': nrm((N_AB, 2, RW_DIM), 0.5),
        'rw_w2': nrm((N_AB, 2, W_LORA, RW_DIM), 0.1),
        'rw_a0': nrm((N_AB, 2, RW_DIM), 0.3),
        'rw_a2': nrm((N_AB, 2, A_LORA, RW_DIM), 0.1),
        'rw_g2': nrm((N_AB, G_LORA, RW_DIM), G_LORA ** -0.5),
        'rw_k_k': 0.85 + nrm((N_AB, RW_DIM), 0.02),
        'rw_k_a': gain((N_AB, RW_DIM)),
        'rw_r_k': nrm((N_AB, RW_HEADS, RW_HEAD), 0.1),
        'rw_lnx_g': gain((N_AB, RW_DIM)),
        'rw_lnx_b': nrm((N_AB, RW_DIM), 0.02),
        'mla_q_norm': gain((N_AB, Q_LORA)),
        'mla_q_up': nrm((N_AB, Q_LORA, MLA_HEADS * QK_HEAD), Q_LORA ** -0.5),
        'mla_kv_norm': gain((N_AB, KV_LORA)),
        'mla_kv_up': nrm((N_AB, KV_LORA, MLA_HEADS * (QK_NOPE + V_HEAD)), KV_LORA ** -0.5),
        'mla_qn': gain((N_AB, QK_HEAD)),
        'mla_kn': gain((N_AB, QK_HEAD)),
        'ab_w_out': nrm((N_AB, RW_DIM + MLA_DIM, D), (RW_DIM + MLA_DIM) ** -0.5),
        'hy_w_in': nrm((N_C, D, 3 * D), D ** -0.5),
        'hy_b_in': nrm((N_C, 3 * D), 0.02),
        'hy_conv_w': nrm((N_C, HY_SHORT, 3 * D), 0.5),
        'hy_conv_b': nrm((N_C, 3 * D), 0.02),
        'hy_f_w1': nrm((N_C, HY_EMB, HY_HIDDEN), HY_EMB ** -0.5),
        'hy_f_b1': nrm((N_C, HY_HIDDEN), 0.1),
        'hy_f_w2': nrm((N_C, HY_HIDDEN, HY_HIDDEN), HY_HIDDEN ** -0.5),
        'hy_f_b2': nrm((N_C, HY_HIDDEN), 0.1),
        'hy_f_w3': nrm((N_C, HY_HIDDEN, 2 * D), HY_HIDDEN ** -0.5),
        'hy_f_freq': gain((N_C, HY_HIDDEN)),
        'hy_bias': nrm((N_C, D), 0.1),
        'hy_w_out': nrm((N_C, D, D), D ** -0.5),
        'peer_w_q': nrm((DEPTH, D, PEER_HEADS * PEER_DKEY), D ** -0.5),
        'peer_keys': nrm((DEPTH, PEER_HEADS, 2, PEER_KEYS, PEER_DKEY // 2), (PEER_DKEY // 2) ** -0.5),
        'peer_u': nrm((DEPTH, PEER_N, D), D ** -0.5),
        'peer_v': nrm((DEPTH, PEER_N, D), 0.05),
    }

def reference(x_prompt, x_sample, state_rwkv_fwd, state_rwkv_bwd, cache_mla_ckv, cache_mla_kpe, c, c_ctx,
              norm_g, w_mod, b_mod, ab_w_in, rw_mu, rw_w0, rw_w2, rw_a0, rw_a2, rw_g2, rw_k_k, rw_k_a, rw_r_k,
              rw_lnx_g, rw_lnx_b, mla_q_norm, mla_q_up, mla_kv_norm, mla_kv_up, mla_qn, mla_kn, ab_w_out,
              hy_w_in, hy_b_in, hy_conv_w, hy_conv_b, hy_f_w1, hy_f_b1, hy_f_w2, hy_f_b2, hy_f_w3, hy_f_freq,
              hy_bias, hy_w_out, peer_w_q, peer_keys, peer_u, peer_v):
    rope = axial_rope(x_sample.shape[1])
    xp, xs = x_prompt, x_sample
    st_f, st_b, st_ckv, st_kpe = [], [], [], []
    for li in range(DEPTH):
        j = li // 2
        mp = jnp.split(jax.nn.silu(c_ctx) @ w_mod[li] + b_mod[li], 6, axis=-1)
        ms = [m[:, None, :] for m in jnp.split(jax.nn.silu(c) @ w_mod[li] + b_mod[li], 6, axis=-1)]
        hp = modulate(rmsnorm(xp, norm_g[li, 0]), mp[0], mp[1])
        hs = modulate(rmsnorm(xs, norm_g[li, 0]), ms[0], ms[1])
        if li % 2 == 0:
            p = (ab_w_in[j], rw_mu[j], rw_w0[j], rw_w2[j], rw_a0[j], rw_a2[j], rw_g2[j], rw_k_k[j], rw_k_a[j],
                 rw_r_k[j], rw_lnx_g[j], rw_lnx_b[j], mla_q_norm[j], mla_q_up[j], mla_kv_norm[j], mla_kv_up[j],
                 mla_qn[j], mla_kn[j], ab_w_out[j])
            op, sf, sb, ckv, kpe = rwkv_mla_mixer(hp, None, p)
            ctx = (state_rwkv_fwd[:, j], state_rwkv_bwd[:, j], cache_mla_ckv[:, j], cache_mla_kpe[:, j], rope)
            os_, _, _, _, _ = rwkv_mla_mixer(hs, ctx, p)
            st_f.append(sf)
            st_b.append(sb)
            st_ckv.append(ckv)
            st_kpe.append(kpe)
        else:
            p = (hy_w_in[j], hy_b_in[j], hy_conv_w[j], hy_conv_b[j], hy_f_w1[j], hy_f_b1[j], hy_f_w2[j],
                 hy_f_b2[j], hy_f_w3[j], hy_f_freq[j], hy_bias[j], hy_w_out[j])
            op = hyena_mixer(hp, p)
            os_ = hyena_mixer(hs, p)
        xp = xp + mp[2] * op
        xs = xs + ms[2] * os_
        pp = (peer_w_q[li], peer_keys[li], peer_u[li], peer_v[li])
        xp = xp + mp[5] * peer_ffn(modulate(rmsnorm(xp, norm_g[li, 1]), mp[3], mp[4]), *pp)
        xs = xs + ms[5] * peer_ffn(modulate(rmsnorm(xs, norm_g[li, 1]), ms[3], ms[4]), *pp)
    new_state_rwkv_fwd = jnp.stack(st_f, axis=1).astype(x_prompt.dtype)
    new_state_rwkv_bwd = jnp.stack(st_b, axis=1).astype(x_prompt.dtype)
    new_cache_mla_ckv = jnp.stack(st_ckv, axis=1)
    new_cache_mla_kpe = jnp.stack(st_kpe, axis=1)
    return (xp, xs, new_state_rwkv_fwd, new_state_rwkv_bwd, new_cache_mla_ckv, new_cache_mla_kpe)


_drawn_inputs = setup_inputs


def setup_inputs(seed=0):
    import zlib

    import numpy as np

    out = dict(_drawn_inputs(seed))
    spreads = {}
    factors = {'state_rwkv_fwd': 6.08,
     'state_rwkv_bwd': 6.409,
     'cache_mla_kpe': 4.805,
     'rw_k_k': 9.986,
     'rw_lnx_g': 29.107,
     'rw_lnx_b': 27.112,
     'mla_q_norm': 8.0,
     'mla_kv_norm': 2.991,
     'mla_qn': 8.0,
     'mla_kn': 8.0,
     'hy_b_in': 29.967,
     'hy_conv_b': 26.626,
     'hy_f_freq': 8.0,
     'peer_w_q': 4.759,
     'peer_keys': 4.765,
     'peer_u': 5.329,
     'peer_v': 4.757}
    for name, (base, spread) in spreads.items():
        noise = np.random.default_rng([zlib.crc32(name.encode()), seed]).standard_normal(out[name].shape)
        drawn = base * np.exp(spread * noise) if base else spread * noise
        out[name] = __import__('jax').numpy.asarray(drawn.astype(out[name].dtype))
    for name, factor in factors.items():
        out[name] = (out[name] * factor).astype(out[name].dtype)
    return out
```

```python
from contextlib import ExitStack

import numpy as np

import concourse.bass as bass
from concourse import mybir

F32 = mybir.dt.float32
U32 = mybir.dt.uint32
ALU = mybir.AluOpType
ACT = mybir.ActivationFunctionType
AX = mybir.AxisListType

P = 128
D = 1024
KD = D // P
TILES = 3
T = TILES * P
EPS = 1e-6
LNX_EPS = 64e-5
HEADS = 8
PAIRS = HEADS // 2
CH = 64
NCH = T // CH
MLA_HEADS = 4
QK = 192
KEYTILES = 4
SLOT = 4096
RING = 3
TOPK = 16
SIDES = 16
HALF = 64
UVJOBS = 64

JOB_COUNTS = [[("mod", 12), ("in", 5), ("small", 1), ("out", 2), ("wq", 4), ("keys", 1), ("uv", UVJOBS)],
              [("mod", 12), ("in", 6), ("window", 1), ("filter", 1), ("dft", 1), ("out", 2), ("wq", 4),
               ("keys", 1), ("uv", UVJOBS)]]
JOB = {}
N_JOBS = 0
for _l, _jobs in enumerate(JOB_COUNTS):
    for _name, _n in _jobs:
        JOB[(_name, _l)] = N_JOBS
        N_JOBS += _n

SCAN_GROUPS = 2 * 26
STAGES = [("mod0", 12, 1), ("norm0", 6, 1), ("in0", 17, 1), ("qkvT", 3, 1), ("up", 14, 1), ("headT", 16, 1),
          ("att", 6, MLA_HEADS), ("knorm", 4, 1), ("lora", 20, 1), ("state_in", 4, 1), ("coef", 1, 1),
          ("scanp", SCAN_GROUPS, 2), ("state_out", 2, 1), ("scans", SCAN_GROUPS, 4),
          ("yT", 12, 1), ("gate0", 4, 1), ("out0", 6, 1), ("norm0b", 6, 1), ("wq0", 16, 1), ("keys0", 12, 1),
          ("selT0", 3, 1), ("hot0", 6, 1), ("gate0b", (6, 7, 14, 15), 1),
          ("mod1", 12, 1), ("norm1", 6, 1), ("in1", 24, 1), ("hid", 2, 1), ("filt", 12, 1), ("norm_f", 4, 1),
          ("filtF", 12, 1), ("zT", 6, 1), ("zF", 12, 1), ("conv", 8, 1), ("gate1", 4, 1), ("out1", 6, 1),
          ("norm1b", 6, 1), ("wq1", 16, 1), ("keys1", 12, 1), ("selT1", 3, 1), ("hot1", 6, 1), ("gate1b", (6, 7, 14, 15), 1)]


def plan_banks():
    used, first, groups = [0] * 8, {}, {}
    for stage, gs, n in STAGES:
        first[stage], groups[stage] = list(used), range(gs) if isinstance(gs, int) else gs
        for q in groups[stage]:
            used[q % 8] += n
    return first, groups


FIRST, GROUPS = plan_banks()


def use_of(stage, q, i=0):
    same = [g for g in GROUPS[stage] if g % 8 == q % 8]
    before = FIRST[stage][q % 8] + same.index(q)
    if isinstance(i, int):
        return before + len(same) * i
    return i * len(same) + before


NORM_NO = {"norm0": 0, "norm0b": 1, "norm1": 2, "norm1b": 3}
GATE_NO = {"gate0": 0, "gate0b": 1, "gate1": 2, "gate1b": 3}

COLS = {}
N_COLS = 0
for _name, _n in [("mu", 14), ("k_k", 4), ("k_a", 4), ("r_k", 4), ("w0", 8), ("a0", 8), ("g", 32), ("b_mod", 96),
                  ("b_in", 24), ("conv_w", 72), ("conv_b", 24), ("bias", 8), ("f_b1", 1), ("f_b2", 1), ("freq", 1),
                  ("cond", 16)]:
    COLS[_name] = N_COLS
    N_COLS += _n
ROWS = {"q_norm": (0, 256), "kv_norm": (256, 128), "qn": (384, 192), "kn": (576, 192)}
N_ROWS = 768


def build(nc, io):
    with ExitStack() as ctx:
        def sb(name, shape, dt=F32):
            return ctx.enter_context(nc.sbuf_tensor(name, shape, dt))

        sems = {}

        def s(name):
            if name not in sems:
                sems[name] = ctx.enter_context(nc.semaphore(name))
            return sems[name]

        ring = sb("ring", [P, RING, SLOT])
        x = sb("x", [P, TILES, D])
        hT = sb("hT", [P, KD, T])
        arena = sb("arena", [P, 27648])
        cols = sb("cols", [P, N_COLS])
        modc = sb("modc", [P, 48, 2])
        gsc = sb("gsc", [P, KD, 2])
        condT = sb("condT", [P, KD, 2])
        ident = sb("ident", [P, P])
        stacked = sb("stacked", [P, CH])
        iota = sb("iota", [P, P])
        ones = sb("ones", [P, P])
        headones = sb("headones", [P, P])
        stat = sb("stat", [P, 64])
        shared = sb("shared", [P, 2048 + 640])
        masks = shared[:, 0:2048].rearrange("p (m c) -> p m c", m=16)
        sel = shared[:, 0:3 * T].rearrange("p (m t) -> p m t", m=3)
        gel = shared[:, 3 * T:5 * T].rearrange("p (b t) -> p b t", b=2)
        gw = shared[:, 5 * T:7 * T].rearrange("p (b t) -> p b t", b=2)
        psum = ctx.enter_context(nc.psum_tensor("psum", [P, 8, 512], F32))

        def area(off, *shape):
            n = 1
            for d in shape:
                n *= d
            assert off + n <= 27648, (off, shape)
            a = arena[:, off:off + n]
            if len(shape) == 1:
                return a
            names = "abcd"[:len(shape)]
            return a.rearrange("p (%s) -> p %s" % (" ".join(names), " ".join(names)),
                               **{names[k]: shape[k] for k in range(len(shape) - 1)})

        rkv = area(0, 12, T)
        wdad = area(4608, T)
        gd = area(4992, T)
        mla0 = 5376
        mla = area(mla0, 3, 448)
        ckv = area(mla0 + 1344, KEYTILES, 128)
        kpe = area(mla0 + 1856, KEYTILES, 64)
        qc = area(mla0 + 2112, 3, 256)
        qcT = area(mla0 + 2880, 2, T)
        ckvT = area(mla0 + 3648, KEYTILES * P)
        q = area(mla0 + 4160, 3, MLA_HEADS, QK)
        kx = area(mla0 + 6464, KEYTILES, MLA_HEADS, QK)
        vx = area(mla0 + 9536, KEYTILES, MLA_HEADS, P)
        qTn = area(mla0 + 11584, MLA_HEADS, T)
        qTr = area(mla0 + 13120, MLA_HEADS, T)
        kTn = area(mla0 + 14656, MLA_HEADS, 4 * P)
        kTr = area(mla0 + 16704, MLA_HEADS, 4 * P)
        sq = area(mla0 + 14656, 3072)
        prob = area(mla0 + 0, 7, P)
        probT = area(mla0 + 2112, 7, P)
        rows = area(mla0 + 18752, N_ROWS)
        rope = area(mla0 + 19520, 2, 2, 32)
        rtmp = area(mla0 + 19648, 4, 2, MLA_HEADS, 32)
        assert mla0 + 19648 + 1024 <= 27648
        tilde = area(5376, 8, PAIRS, T)
        gateT = area(17664, PAIRS, T)
        kk = area(19200, PAIRS, T)
        ld = area(20736, PAIRS, T)
        cum = area(22272, PAIRS, T)
        cumx = area(23808, PAIRS, T)
        lr = area(25344, PAIRS, T)
        tr0 = 19200
        ex = area(tr0, 5, PAIRS, P)
        NT = area(tr0 + 2560, 512)
        NTm = area(tr0 + 3072, 512)
        Tm = area(tr0 + 3584, 512)
        TT = area(tr0 + 4096, 512)
        Pm = area(tr0 + 4608, 512)
        KT = area(tr0 + 5120, 512)
        RkT = area(tr0 + 5632, 512)
        RbT = area(tr0 + 6144, 512)
        ktok = area(tr0 + 6656, 512)
        btok = area(tr0 + 7168, 512)
        Vt = area(tr0 + 7680, 256)
        Xt = area(tr0 + 7936, 256)
        SA = area(tr0 + 8192, 256)
        y = area(1536, NCH, PAIRS, CH)
        ST = sb("ST", [P, 2, 2, PAIRS, CH])
        lora_rhs = area(26880, 2, T)
        bexp = area(26880, 2, P)
        bonus_w = area(0, PAIRS, T)
        elast = sb("elast", [P, 2, PAIRS, NCH])
        coef = sb("coef", [P, PAIRS, NCH])
        s0 = sb("s0", [64, 2, HEADS, 64])
        scanmask = sb("scanmask", [P, T])
        lnx = area(tr0, 2, PAIRS, CH)
        yc = area(tr0 + 512, NCH, PAIRS, CH)
        ysq = area(tr0 + 2048, NCH, PAIRS, CH)
        zexp = area(tr0 + 3584, 2, PAIRS, P)
        vtok = area(tr0 + 4608, NCH, PAIRS, CH)
        pad = area(mla0 + 20736, 2, 388)
        padt = area(mla0 + 21512, 388)
        xn = area(24576, 1024)
        xn2 = area(25600, 1024)
        junk = area(26624, 1024)
        gate_row = area(20480, 2, D)
        x0T = area(0, KD, T)
        zinT = area(3072, KD, T)
        filtF = area(6144, 6, D)
        zF = area(12288, 6, D)
        filt = area(12288, 3, 2 * D)
        z = area(18432, 3, D)
        absf = area(6144, 12, 512)
        rnorm = area(18432, 2, D)
        hid = area(22528, 2, T)
        htmp = area(23296, 2, T)
        prod = area(21504, 2, D)
        pad1 = area(24576, 2, 388)
        padt1 = area(25352, 388)
        vtmp = area(25740, T)
        gate_bc = area(9216, 16, P)
        qT = area(0, SIDES, T)
        sc = area(6144, SIDES, TILES, P)
        top = area(12288, TILES, SIDES, TOPK)
        topi = area(13056, TILES, SIDES, TOPK)
        topif = area(13824, TILES, SIDES, TOPK)
        cand = area(14592, HEADS, 256)
        tops = area(16640, HEADS, TOPK)
        posu = area(16768, HEADS, TOPK)
        hi = area(16896, HEADS, TOPK)
        lo = area(17024, HEADS, TOPK)
        oh = area(17152, HEADS, TOPK, TOPK)
        pick = area(19200, 3, P)
        wd = area(0, T, HALF)
        ohA = area(24576, 2, 8, P)
        ohB = area(26624, 2, 8, HALF)

        block = ctx.enter_context(nc.Block())

        def slot(job):
            return ring[:, job % RING, :]

        def landed(eng, job):
            eng.wait_ge(s("landed%d" % (job % RING)), 16 * (job // RING + 1))

        def bank_free(eng, stage, g, i=0):
            u = use_of(stage, g, i)
            if not (isinstance(u, int) and u == 0):
                eng.wait_ge(s("bank_free%d" % (g % 8)), u)
            return psum[:, g % 8, :]

        def bank_full(eng, stage, g, i=0):
            eng.wait_ge(s("bank_full%d" % (g % 8)), use_of(stage, g, i) + 1)
            return psum[:, g % 8, :]

        def full(ins, g):
            ins.then_inc(s("bank_full%d" % (g % 8)), 1)

        def copied(eng, stage, g, i=0):
            eng.wait_ge(s("bank_free%d" % (g % 8)), use_of(stage, g, i) + 1)

        def free(ins, g):
            ins.then_inc(s("bank_free%d" % (g % 8)), 1)

        def chain(eng, name):
            at = {"base": 0, "n": 0}

            def link(ins):
                ins.then_inc(s(name), 1)
                at["n"] += 1
                eng.wait_ge(s(name), at["base"] + at["n"])

            def enter(base):
                done = at["n"]
                at["base"], at["n"] = base, 0
                return done

            return link, enter

        def tell(eng, ins, name, value):
            ins.then_inc(s(name), 1)
            eng.wait_ge(s(name), value)

        def bc(ap, n):
            return ap.unsqueeze(2).to_broadcast([ap.shape[0], ap.shape[1], n])

        def head_bc(ap, n, k):
            return ap.unsqueeze(1).to_broadcast([ap.shape[0], k, n])

        def blocks(ap):
            return ap.rearrange("p (m c) -> p m c", m=PAIRS)

        def col(name, k=0):
            return cols[:, COLS[name] + k:COLS[name] + k + 1]

        @block.sync
        def _(sp):
            for ap, src in [(x[:, 0, :], io["x_prompt"][0]),
                            (x[:, 1:3, :], io["x_sample"][0].rearrange("(a p) d -> p a d", p=P)),
                            (cols[:], io["cols"]), (ident[:], io["consts"][:, 0:128]),
                            (headones[:], io["consts"][:, 128:256]), (stacked[:], io["consts"][:, 256:320]),
                            (scanmask[:], io["consts"][:, 320:704]), (iota[:], io["consts"][:, 704:832])]:
                sp.dma_start(ap, src).then_inc(s("inputs"), 16)

            def job_load(j, k, wait):
                if wait is not None:
                    sp.wait_ge(s("slot_used"), wait)
                sp.dma_start(ring[:, k, :], io["stream"][j]).then_inc(s("landed%d" % k), 16)
            for k in range(RING):
                job_load(k, k, None)
            with sp.Fori(1, N_JOBS // RING) as i:
                for k in range(RING):
                    job_load(i * RING + k, k, i * RING + (k - RING + 1))
            for j in range(N_JOBS // RING * RING, N_JOBS):
                job_load(j, j % RING, j - RING + 1)

        @block.gpsimd
        def _(pool):
            bank_full(pool, "norm0", 5)
            for ap, src in [(masks, io["masks"]), (rows, io["rows"].to_broadcast([P, N_ROWS])),
                            (rope[:, 0], io["rope"][0].rearrange("(a p) f -> p a f", p=P)),
                            (rope[:, 1], io["rope"][1].rearrange("(a p) f -> p a f", p=P)),
                            (ckv[:, 1, :], io["cache_mla_ckv"][0, 0]), (kpe[:, 1, :], io["cache_mla_kpe"][0, 0]),
                            (s0[:, 0], io["state_rwkv_fwd"][0, 0].rearrange("h v k -> v h k")),
                            (s0[:, 1], io["state_rwkv_bwd"][0, 0].rearrange("h v k -> v h k"))]:
                pool.dma_start(ap, src).then_inc(s("mixer_params"), 16)
            pool.wait_ge(s("latents"), 1)
            pool.dma_start(io["o_ckv"][0, 0], ckv[:, 0, :]).then_inc(s("stored"), 16)
            pool.dma_start(io["o_kpe"][0, 0], kpe[:, 0, :]).then_inc(s("stored"), 16)

            def block_masks(stage, i, d, first):
                it = first + d
                copied(pool, stage, 26 * d + 1, i)
                for lev in range(1, 6):
                    if lev > 1:
                        bank_full(pool, stage, 26 * d + 8 + 3 * (lev - 2), i)
                    m = masks[:, lev + 6 * d, :].unsqueeze(1).to_broadcast([P, PAIRS, P])
                    nc.gpsimd.tensor_tensor(blocks(NTm), blocks(NT), m, ALU.mult).then_inc(s("ntm_ready"), 1)
            with pool.Fori(0, 2) as i:
                for d in range(2):
                    block_masks("scanp", i, d, i * 2)
            pool.wait_ge(s("state_copied"), 2)
            for d, name in enumerate(("o_fwd", "o_bwd")):
                pool.dma_start(io[name][0, 0].rearrange("h v k -> v h k"), s0[:, d]).then_inc(s("stored"), 16)
            with pool.Fori(0, 4) as i:
                for d in range(2):
                    block_masks("scans", i, d, i * 2 + 4)
            pool.wait_ge(s("scan_done"), 1)
            for h in range(2):
                for m, name in enumerate(("lnx_g", "lnx_b")):
                    pool.dma_start(lnx[64 * h:64 * h + 64, m],
                                   io[name][h:h + 1].to_broadcast([64, PAIRS, CH])).then_inc(s("lnx_loaded"), 16)
            pool.wait_ge(s("y_done"), 1)
            pool.dma_start(io["o_prompt"][0], x[:, 0, :]).then_inc(s("stored"), 16)
            pool.dma_start(io["o_sample"][0].rearrange("(a p) d -> p a d", p=P), x[:, 1:3, :]).then_inc(s("stored"), 16)
            pool.wait_ge(s("stored"), 16 * 6)

        @block.tensor
        def _(pe):
            mm = nc.tensor.matmul

            def hand_back(ins, jobs=1):
                ins.then_inc(s("slot_used"), jobs)

            def adaln(l):
                pe.wait_ge(s("cond_ready"), 1)
                for j in range(12):
                    job = JOB[("mod", l)] + j
                    w = slot(job).rearrange("p (k n) -> p k n", k=KD)
                    landed(pe, job)
                    b = bank_free(pe, "mod%d" % l, j)
                    for m in range(4):
                        for k in range(KD):
                            ins = mm(b[:, 2 * m:2 * m + 2], w[:, k, m * P:(m + 1) * P], condT[:, k, :],
                                     start=k == 0, stop=k == KD - 1)
                            if j > 0 and m == 0 and k == 0:
                                hand_back(ins)
                    full(ins, j)

            def norm_transposes(stage):
                for t in range(TILES):
                    pe.wait_ge(s("normed"), NORM_NO[stage] * TILES + t + 1)
                    for h in range(2):
                        b = bank_free(pe, stage, 2 * t + h)
                        for k in range(4):
                            ins = nc.tensor.transpose(b[:, k * P:(k + 1) * P],
                                                      (xn, xn2)[t % 2][:, (4 * h + k) * P:(4 * h + k + 1) * P], ident[:])
                            if t == 0 and h == 0 and k == 0:
                                hand_back(ins)
                        full(ins, 2 * t + h)

            def feature_product(stage, g, w, cols_, back=False):
                b = bank_free(pe, stage, g)
                for k in range(KD):
                    ins = mm(b[:, 0:T], w[:, k, cols_], hT[:, k, :], start=k == 0, stop=k == KD - 1)
                    if back and k == 0:
                        hand_back(ins)
                full(ins, g)

            def token_product(stage, g, w, n, t, back=False):
                b = bank_free(pe, stage, g)
                for k in range(KD):
                    ins = mm(b[:, 0:n], hT[:, k, t * P:(t + 1) * P], w[:, k, 0:n], start=k == 0, stop=k == KD - 1)
                    if back and k == 0:
                        hand_back(ins)
                full(ins, g)

            def out_product(l):
                for j in range(2):
                    job = JOB[("out", l)] + j
                    landed(pe, job)
                    w = slot(job).rearrange("p (k n) -> p k n", k=KD)
                    for t in range(TILES):
                        token_product("out%d" % l, 3 * j + t, w, 512, t, back=j == 1 and t == 0)

            def gate_rows(stage, l):
                pe.wait_ge(s("gate_cols"), GATE_NO[stage] + 1)
                for c in range(2):
                    for h in range(2):
                        g = GROUPS[stage][2 * c + h]
                        b = bank_free(pe, stage, g)
                        for k in range(4):
                            ins = mm(b[:, k * P:(k + 1) * P], gate_bc[:, 8 * c + 4 * h + k, :], ident[:],
                                     start=True, stop=True)
                            if (c, h, k) == (0, 0, 0) and (stage[-1] == "b" or stage == "gate1"):
                                hand_back(ins)
                        full(ins, g)

            pe.wait_ge(s("inputs"), 16 * 8)
            adaln(0)
            norm_transposes("norm0")
            copied(pe, "norm0", 4)
            copied(pe, "norm0", 5)
            for j in range(4):
                job = JOB[("in", 0)] + j
                landed(pe, job)
                w = slot(job).rearrange("p (k n) -> p k n", k=KD)
                for m in range(4 if j < 3 else 2):
                    feature_product("in0", 4 * j + m, w, slice(m * P, (m + 1) * P), back=j > 0 and m == 0)
            job = JOB[("in", 0)] + 4
            landed(pe, job)
            for t in range(TILES):
                token_product("in0", 14 + t, slot(job).rearrange("p (k n) -> p k n", k=KD), 448, t, back=t == 0)

            small = slot(JOB[("small", 0)])
            q_up = small[:, 0:1536].rearrange("p (k n) -> p k n", k=2)
            kv_up = small[:, 1536:2560]
            w2a2 = small[:, 2560:3584].rearrange("p (d n) -> p d n", d=2)
            g2 = small[:, 3584:4096]
            pe.wait_ge(s("latents"), 1)
            for k in range(2):
                b = bank_free(pe, "qkvT", k)
                for t in range(TILES):
                    ins = nc.tensor.transpose(b[:, t * P:(t + 1) * P], qc[:, t, k * P:(k + 1) * P], ident[:])
                    if k == 0 and t == 0:
                        hand_back(ins)
                full(ins, k)
            b = bank_free(pe, "qkvT", 2)
            for t in range(KEYTILES):
                ins = nc.tensor.transpose(b[:, t * P:(t + 1) * P], ckv[:, t, :], ident[:])
            full(ins, 2)
            landed(pe, JOB[("small", 0)])
            for g in range(3):
                copied(pe, "qkvT", g)
            for t in range(TILES):
                for h in range(2):
                    b = bank_free(pe, "up", 2 * t + h)
                    for k in range(2):
                        ins = mm(b[:, 0:384], qcT[:, k, t * P:(t + 1) * P], q_up[:, k, 384 * h:384 * h + 384],
                                 start=k == 0, stop=k == 1)
                    full(ins, 2 * t + h)
            for t in range(KEYTILES):
                for h in range(2):
                    b = bank_free(pe, "up", 6 + 2 * t + h)
                    full(mm(b, ckvT[:, t * P:(t + 1) * P], kv_up[:, 512 * h:512 * h + 512], start=True, stop=True),
                         6 + 2 * t + h)
            pe.wait_ge(s("heads_ready"), 1)
            for h in range(MLA_HEADS):
                for part, (src, n) in enumerate(((q, TILES), (q, TILES), (kx, KEYTILES), (kx, KEYTILES))):
                    g = 4 * h + part
                    b = bank_free(pe, "headT", g)
                    for t in range(n):
                        if part % 2 == 0:
                            ins = nc.tensor.transpose(b[:, t * P:(t + 1) * P], src[:, t, h, 0:P], ident[:])
                        else:
                            ins = nc.tensor.transpose(b[0:64, t * P:(t + 1) * P], src[:, t, h, P:QK], ident[:])
                    full(ins, g)
            for h in range(MLA_HEADS):
                if h == 0:
                    for g in range(8, 16):
                        copied(pe, "headT", g)
                for t in range(TILES):
                    keys = slice(0, P) if t == 0 else slice(P, 4 * P)
                    n = keys.stop - keys.start
                    b = bank_free(pe, "att", t, h)
                    mm(b[:, 0:n], qTn[:, h, t * P:(t + 1) * P], kTn[:, h, keys], start=True, stop=False)
                    full(mm(b[:, 0:n], qTr[0:64, h, t * P:(t + 1) * P], kTr[0:64, h, keys], start=False, stop=True), t)
                pe.wait_ge(s("probs"), h + 1)
                b = bank_free(pe, "att", 3, h)
                for n in range(4):
                    ins = nc.tensor.transpose(b[:, n * P:(n + 1) * P], prob[:, n, :], ident[:])
                full(ins, 3)
                b = bank_free(pe, "att", 4, h)
                for n in range(3):
                    ins = nc.tensor.transpose(b[:, n * P:(n + 1) * P], prob[:, 4 + n, :], ident[:])
                full(ins, 4)
                copied(pe, "att", 3, h)
                copied(pe, "att", 4, h)
                b = bank_free(pe, "att", 5, h)
                mm(b[:, 0:P], vx[:, 0, h, :], probT[:, 0, :], start=True, stop=True)
                for t in range(1, 3):
                    for n in range(3):
                        ins = mm(b[:, t * P:(t + 1) * P], vx[:, 1 + n, h, :], probT[:, 3 * t - 2 + n, :],
                                 start=n == 0, stop=n == 2)
                full(ins, 5)

            pe.wait_ge(s("kk_squares"), 1)
            for m in range(PAIRS):
                b = bank_free(pe, "knorm", m)
                full(mm(b[:, 0:T], headones[:], ld[:, m, :], start=True, stop=True), m)
            pe.wait_ge(s("lora_in"), 3)
            for d in range(2):
                for part in range(2):
                    for m in range(PAIRS):
                        g = 8 * d + 4 * part + m
                        b = bank_free(pe, "lora", g)
                        full(mm(b[:, 0:T], w2a2[:, d, m * P:(m + 1) * P], lora_rhs[:, part, :],
                                start=True, stop=True), g)
            for m in range(PAIRS):
                b = bank_free(pe, "lora", 16 + m)
                full(mm(b[:, 0:T], g2[:, m * P:(m + 1) * P], gd, start=True, stop=True), 16 + m)
            pe.wait_ge(s("mixer_params"), 16 * 8)
            for d in range(2):
                for h in range(2):
                    b = bank_free(pe, "state_in", 2 * d + h)
                    for n in range(2):
                        m = 2 * h + n
                        ins = nc.tensor.transpose(b[:, n * 64:(n + 1) * 64],
                                                  s0[:, d, 2 * m:2 * m + 2, :].rearrange("v h k -> v (h k)"),
                                                  ident[0:64, 0:64])
                        if (d, h, n) == (0, 0, 0):
                            hand_back(ins)
                    full(ins, 2 * d + h)
            b = bank_free(pe, "coef", 0)
            for n in range(PAIRS * NCH):
                pe.wait_ge(s("bonus_exp"), n + 1)
                ins = mm(b[:, n:n + 1], bexp[:, n % 2, :], ones[:, 0:1], start=True, stop=True)
                if n < PAIRS * NCH - 1:
                    ins.then_inc(s("bonus_mm"), 1)
            full(ins, 0)

            def scan_item(stage, i, d, first):
                r_, a_, b_, k_, v_ = (ex[:, n] for n in range(5))
                g0 = 26 * d
                it = first + d
                S = ST[:, 0 if stage == "scanp" else 1, d]

                def pairs(g, lhsT, rhs, n=P):
                    b = bank_free(pe, stage, g0 + g, i)
                    for m in range(PAIRS):
                        ins = mm(b[:, m * n:(m + 1) * n], lhsT(m), rhs(m), start=True, stop=True)
                    full(ins, g0 + g)

                def sl(ap, n=P):
                    return lambda m: ap[:, m * n:(m + 1) * n]

                def pr(ap):
                    return lambda m: ap[:, m, :]
                pe.wait_ge(s("expanded"), it * 5 + 5)
                pairs(0, pr(a_), pr(b_))
                pairs(1, pr(b_), pr(a_))
                pairs(2, pr(k_), pr(a_))
                pairs(3, pr(k_), pr(r_))
                pairs(4, pr(b_), pr(r_))
                b = bank_free(pe, stage, g0 + 5, i)
                for m in range(PAIRS):
                    ins = nc.tensor.transpose(b[:, m * P:(m + 1) * P], k_[:, m, :], ident[:])
                full(ins, g0 + 5)
                b = bank_free(pe, stage, g0 + 6, i)
                for m in range(PAIRS):
                    ins = nc.tensor.transpose(b[:, m * P:(m + 1) * P], b_[:, m, :], ident[:])
                full(ins, g0 + 6)
                pairs(7, pr(v_), lambda m: stacked[:], CH)
                g = 8
                for lev in range(1, 6):
                    pe.wait_ge(s("ntm_ready"), it * 5 + lev)
                    pe.wait_ge(s("t_ready"), it * 6 + lev)
                    pairs(g, sl(NTm), sl(Tm))
                    copied(pe, stage, g0 + g, i)
                    if lev < 5:
                        pairs(g + 1, sl(TT), sl(Pm))
                        pairs(g + 2, sl(Pm), sl(TT))
                        g += 3
                    else:
                        pairs(g + 1, sl(Pm), sl(TT))
                        g += 2
                pe.wait_ge(s("state_ready"), it + 1)
                if d == 1:
                    pe.wait_ge(s("state_scaled"), i + (1 if stage == "scanp" else 3))
                copied(pe, stage, g0 + 7, i)
                copied(pe, stage, g0 + 2, i)
                b = bank_free(pe, stage, g0 + 22, i)
                for m in range(PAIRS):
                    o = b[:, m * CH:(m + 1) * CH]
                    mm(o, a_[:, m, :], S[:, m, :], start=True, stop=False)
                    ins = mm(o, KT[:, m * P:(m + 1) * P], Vt[:, m * CH:(m + 1) * CH], start=False, stop=True)
                full(ins, g0 + 22)
                pe.wait_ge(s("t_ready"), it * 6 + 6)
                copied(pe, stage, g0 + 22, i)
                pairs(23, sl(TT), sl(Xt, CH), CH)
                copied(pe, stage, g0 + 23, i)
                for g in range(3, 7):
                    copied(pe, stage, g0 + g, i)
                b = bank_free(pe, stage, g0 + 24, i)
                for m in range(PAIRS):
                    o = b[:, m * CH:(m + 1) * CH]
                    mm(o, r_[:, m, :], S[:, m, :], start=True, stop=False)
                    mm(o, RkT[:, m * P:(m + 1) * P], Vt[:, m * CH:(m + 1) * CH], start=False, stop=False)
                    ins = mm(o, RbT[:, m * P:(m + 1) * P], SA[:, m * CH:(m + 1) * CH], start=False, stop=True)
                full(ins, g0 + 24)
                b = bank_free(pe, stage, g0 + 25, i)
                for m in range(PAIRS):
                    o = b[:, m * CH:(m + 1) * CH]
                    mm(o, ktok[:, m * P:(m + 1) * P], Vt[:, m * CH:(m + 1) * CH], start=True, stop=False)
                    ins = mm(o, btok[:, m * P:(m + 1) * P], SA[:, m * CH:(m + 1) * CH], start=False, stop=True)
                full(ins, g0 + 25)

            pe.wait_ge(s("state_ready"), 2)
            with pe.Fori(0, 2) as i:
                for d in range(2):
                    scan_item("scanp", i, d, i * 2)
            pe.wait_ge(s("state_ready"), 6)
            for d in range(2):
                b = bank_free(pe, "state_out", d)
                for m in range(PAIRS):
                    ins = nc.tensor.transpose(b[0:64, m * P:(m + 1) * P], ST[:, 0, d, m, :], ident[:])
                full(ins, d)
            with pe.Fori(0, 4) as i:
                for d in range(2):
                    scan_item("scans", i, d, i * 2 + 4)
            for part, name in enumerate(("vexp_ready", "yexp_ready")):
                for c in range(NCH):
                    pe.wait_ge(s(name), c + 1)
                    b = bank_free(pe, "yT", NCH * part + c)
                    for m in range(PAIRS):
                        ins = mm(b[:, m * CH:(m + 1) * CH], zexp[:, part, m, :], stacked[:], start=True, stop=True)
                    full(ins, NCH * part + c)
            gate_rows("gate0", 0)
            for g in range(NCH, 2 * NCH):
                copied(pe, "yT", g)
            copied(pe, "att", 5, MLA_HEADS - 1)
            out_product(0)

            def peer(l):
                norm_transposes("norm%db" % l)
                copied(pe, "norm%db" % l, 4)
                copied(pe, "norm%db" % l, 5)
                for j in range(4):
                    job = JOB[("wq", l)] + j
                    landed(pe, job)
                    w = slot(job).rearrange("p (k n) -> p k n", k=KD)
                    for m in range(4):
                        feature_product("wq%d" % l, 4 * j + m, w, slice(m * P, (m + 1) * P), back=j > 0 and m == 0)
                job = JOB[("keys", l)]
                landed(pe, job)
                w = slot(job)[:, 0:2048]
                for t in range(TILES):
                    for g in range(4):
                        if t == 0:
                            copied(pe, "wq%d" % l, 4 * g + 2)
                            copied(pe, "wq%d" % l, 4 * g + 3)
                        b = bank_free(pe, "keys%d" % l, 4 * t + g)
                        for k in range(4):
                            side = 4 * g + k
                            ins = mm(b[:, k * P:(k + 1) * P], qT[:, side, t * P:(t + 1) * P],
                                     w[:, side * P:(side + 1) * P], start=True, stop=True)
                            if t == 0 and g == 0 and k == 0:
                                hand_back(ins)
                        full(ins, 4 * t + g)
                for t in range(TILES):
                    pe.wait_ge(s("picked%d" % l), t + 1)
                    b = bank_free(pe, "selT%d" % l, t)
                    for n in range(3):
                        ins = nc.tensor.transpose(b[:, n * P:(n + 1) * P], pick[:, n, :], ident[:])
                        if t == 0 and n == 0:
                            hand_back(ins)
                    full(ins, t)
                for g in range(6):
                    bank_free(pe, "hot%d" % l, g)
                for g in (6, 7):
                    pe.wait_ge(s("bank_free%d" % g), FIRST["hot%d" % l][g])
                for half in range(2):
                    wbuild(l, half)
                    hot(l, half)

            def wbuild(l, half):
                base = (2 * l + half) * 48
                if half == 1:
                    pe.wait_ge(s("gelu_done"), 128 * l + 64)

                def group(g, par):
                    pe.wait_ge(s("onehots"), g + 1)
                    if not isinstance(g, int) or g > 1:
                        pe.wait_ge(s("w_copied"), g - 1)
                    for u in range(8):
                        ins = mm(psum[:, 6 + par, u * HALF:(u + 1) * HALF], ohA[:, par, u, :], ohB[:, par, u, :],
                                 start=True, stop=True)
                    ins.then_inc(s("w_ready"), 1)
                group(base, 0)
                group(base + 1, 1)
                with pe.Fori(1, 24) as i:
                    for par in range(2):
                        group(i * 2 + (base + par), par)

            def hot(l, half):
                j0 = JOB[("uv", l)] + 32 * half
                c0 = 128 * l + 64 * half
                pe.wait_ge(s("w_copied"), (2 * l + half + 1) * 48)

                def h_part(c, i):
                    job = j0 + c // 2
                    u = ring[:, job % RING, (c % 2) * 1024:(c % 2) * 1024 + 1024]
                    if c % 2 == 0:
                        pe.wait_ge(s("landed%d" % (job % RING)), i * 16 + 16 * (job // RING + 1))
                    if not (isinstance(i, int) and i * 6 + c0 + c < 2):
                        pe.wait_ge(s("gelu_done"), i * 6 + (c0 + c - 1))
                    for k in range(KD):
                        ins = mm(psum[:, 6 + c % 2, 0:T], u[:, k * P:(k + 1) * P], hT[:, k, :],
                                 start=k == 0, stop=k == KD - 1)
                    ins.then_inc(s("h_ready"), 1)

                def v_part(c, i, start=False, stop=False):
                    job = j0 + c // 2
                    v = ring[:, job % RING, 2048 + (c % 2) * 1024:3072 + (c % 2) * 1024]
                    pe.wait_ge(s("g_done"), i * 6 + (c0 + c + 1))
                    for t in range(TILES):
                        for h in range(2):
                            ins = mm(psum[:, 2 * t + h, :], gw[:, c % 2, t * P:(t + 1) * P], v[:, 512 * h:512 * h + 512],
                                     start=start, stop=stop, skip_group_check=True)
                            if stop:
                                full(ins, 2 * t + h)
                    if c % 2 == 1 and not stop:
                        ins.then_inc(s("slot_used"), 1)
                h_part(0, 0)
                for c in range(6):
                    h_part(c + 1, 0)
                    v_part(c, 0, start=half == 0 and c == 0)
                with pe.Fori(1, 10) as i:
                    for c in range(6):
                        h_part(c + 1, i)
                        v_part(c, i)
                for c in range(60, 64):
                    if c < 63:
                        h_part(c + 1, 0)
                    v_part(c, 0, stop=half == 1 and c == 63)

            peer(0)
            gate_rows("gate0b", 0)

            adaln(1)
            norm_transposes("norm1")
            copied(pe, "norm1", 4)
            copied(pe, "norm1", 5)
            for j in range(6):
                job = JOB[("in", 1)] + j
                landed(pe, job)
                w = slot(job).rearrange("p (k n) -> p k n", k=KD)
                for m in range(4):
                    feature_product("in1", 4 * j + m, w, slice(m * P, (m + 1) * P), back=j > 0 and m == 0)
            job_f, job_d = JOB[("filter", 1)], JOB[("dft", 1)]
            fw = slot(job_f)
            w3, zpos, w1, w2 = fw[0:64, 0:2048], fw[0:33, 2048:2432], fw[0:33, 2432:2496], fw[0:64, 2496:2560]
            landed(pe, job_f)
            b = bank_free(pe, "hid", 0)
            full(mm(b[0:64, 0:T], w1, zpos, start=True, stop=True), 0)
            pe.wait_ge(s("hid_ready"), 1)
            b = bank_free(pe, "hid", 1)
            full(mm(b[0:64, 0:T], w2, hid[0:64, 0, :], start=True, stop=True), 1)
            pe.wait_ge(s("hid_ready"), 2)
            for t in range(TILES):
                for n in range(4):
                    b = bank_free(pe, "filt", 4 * t + n)
                    full(mm(b, hid[0:64, 1, t * P:(t + 1) * P], w3[:, 512 * n:512 * n + 512], start=True, stop=True),
                         4 * t + n)
            na = 0
            pe.wait_ge(s("abs_ready"), 12)
            for seq, tiles in ((0, (1, 2)), (1, (0,))):
                for h in range(2):
                    b = bank_free(pe, "norm_f", 2 * seq + h)
                    n = 2 * len(tiles)
                    for m in range(n):
                        ins = mm(b, ones[:], absf[:, na, :], start=m == 0, stop=m == n - 1)
                        na += 1
                    full(ins, 2 * seq + h)
            dft = slot(job_d)
            landed(pe, job_d)
            Fz = [dft[:, 0:1024].rearrange("p (a f) -> p a f", a=2), dft[:, 3072:3328].rearrange("p (a f) -> p a f", a=1)]
            Fb = [dft[:, 1024:2048].rearrange("p (a f) -> p a f", a=2), dft[:, 3328:3584].rearrange("p (a f) -> p a f", a=1)]
            Gi = [dft[:, 2048:3072].rearrange("p (a f) -> p a f", a=4), dft[:, 3584:3840].rearrange("p (a f) -> p a f", a=2)]
            SEQ = ((0, (1, 2), 0, 4), (1, (0,), 4, 2))

            def transform(stage, parts):
                for sq_, tiles, f0, nf in SEQ:
                    for f in range(nf):
                        for h in range(2):
                            g = 2 * (f0 + f) + h
                            b = bank_free(pe, stage, g)
                            todo = [(mat[sq_][:, a, f * P:(f + 1) * P], src(t, h)) for mat, src in parts
                                    for a, t in enumerate(tiles)]
                            for n, (lhsT, rhs) in enumerate(todo):
                                ins = mm(b, lhsT, rhs, start=n == 0, stop=n == len(todo) - 1)
                                if stage == "filtF" and g == 0 and n == 0:
                                    hand_back(ins, 2)
                            full(ins, g)
            transform("filtF", [(Fz, lambda t, h: filt[:, t, 512 * h:512 * h + 512]),
                                (Fb, lambda t, h: filt[:, t, D + 512 * h:D + 512 * h + 512])])
            pe.wait_ge(s("zin_ready"), KD)
            copied(pe, "filtF", 11)
            for t in range(TILES):
                for h in range(2):
                    b = bank_free(pe, "zT", 2 * t + h)
                    for k in range(4):
                        ins = nc.tensor.transpose(b[:, k * P:(k + 1) * P], zinT[:, 4 * h + k, t * P:(t + 1) * P], ident[:])
                    full(ins, 2 * t + h)
            for g in range(6):
                copied(pe, "zT", g)
            transform("zF", [(Fz, lambda t, h: z[:, t, 512 * h:512 * h + 512])])
            pe.wait_ge(s("spectra_ready"), 1)
            for k in range(KD):
                b = bank_free(pe, "conv", k)
                for sq_, tiles, f0, nf in SEQ:
                    n = len(tiles) * P
                    o = tiles[0] * P
                    for f in range(nf):
                        ins = mm(b[:, o:o + n], zF[:, f0 + f, k * P:(k + 1) * P], Gi[sq_][:, f, :],
                                 start=f == 0, stop=f == nf - 1)
                full(ins, k)
            gate_rows("gate1", 1)
            pe.wait_ge(s("conv_out"), KD)
            out_product(1)
            peer(1)
            gate_rows("gate1b", 1)

        @block.vector
        def _(dve):
            V = nc.vector
            L, enter = chain(dve, "dve_chain")
            normed = [0]
            x_new = [0]

            def rms(ss, n, count, eps=EPS):
                a = stat[:, ss:ss + n]
                V.tensor_scalar(a, a, 1.0 / count, eps, ALU.mult, ALU.add).then_inc(s("to_root"), 1)
                roots[0] += 1
                dve.wait_ge(s("rooted"), roots[0])
                L(V.reciprocal(a, a))
            roots = [0]

            def adaln(l):
                for j in range(12):
                    b = bank_full(dve, "mod%d" % l, j)
                    o = COLS["b_mod"] + 48 * l + 4 * j
                    free(V.tensor_tensor(modc[:, 4 * j:4 * j + 4, :], b[:, 0:8].rearrange("p (m c) -> p m c", m=4),
                                         bc(cols[:, o:o + 4], 2), ALU.add), j)
                copied(dve, "mod%d" % l, 11)

            def norm(stage, l, part):
                no = NORM_NO[stage]
                o = COLS["g"] + 8 * (2 * l + part)
                L(V.tensor_scalar(gsc[:], modc[:, 24 * part + 8:24 * part + 16, :], 1.0, None, ALU.add))
                tell(dve, V.tensor_tensor(gsc[:], gsc[:], bc(cols[:, o:o + 8], 2), ALU.mult), "gsc_ready", no + 1)
                dve.wait_ge(s("x_squares"), no + 1)
                rms(0, 3, D)
                for t in range(TILES):
                    if t == 2:
                        bank_full(dve, stage, 1)
                    tell(dve, V.tensor_scalar((xn, xn2)[t % 2], x[:, t, :], stat[:, t:t + 1], None, ALU.mult),
                              "normed", no * TILES + t + 1)

            def gate_columns(stage, part):
                for c in range(2):
                    ins = V.tensor_copy(gate_bc[:, 8 * c:8 * c + 8, :], bc(modc[:, 8 * part:8 * part + 8, c], P))
                    if c == 0:
                        L(ins)
                    else:
                        tell(dve, ins, "gate_cols", GATE_NO[stage] + 1)

            def add_out(stage, gate, order):
                for n in (1, 3):
                    copied(dve, gate, GROUPS[gate][n])
                for g, t, h in order:
                    b = bank_full(dve, stage, g)
                    c = 0 if t == 0 else 1
                    tmp = (xn, xn2)[g % 2][:, 0:512]
                    ins = V.tensor_tensor(tmp, b, gate_row[:, c, 512 * h:512 * h + 512], ALU.mult)
                    free(ins, g)
                    copied(dve, stage, g)
                    xs = x[:, t, 512 * h:512 * h + 512]
                    ins = V.tensor_tensor(xs, xs, tmp, ALU.add)
                    if g == 5:
                        x_new[0] += 1
                        tell(dve, ins, "x_new", x_new[0])
                    else:
                        L(ins)

            dve.wait_ge(s("inputs"), 16 * 8)
            L(V.memset(ones[:], 1.0))
            dve.wait_ge(s("cond_sig"), 1)
            cond = cols[:, COLS["cond"]:COLS["cond"] + 16].rearrange("p (k c) -> p k c", k=KD)
            tell(dve, V.tensor_tensor(condT[:], condT[:], cond, ALU.mult), "cond_ready", 1)
            adaln(0)
            norm("norm0", 0, 0)

            bank_full(dve, "norm0", 5)
            tell(dve, V.memset(pad, 0.0), "pad_zero", 1)
            mu = cols[:, COLS["mu"]:COLS["mu"] + 14]
            L(V.tensor_scalar(stat[:, 32:46], mu, 0.5, None, ALU.mult))
            L(V.tensor_scalar(stat[:, 46:60], mu, -1.0, 1.0, ALU.mult, ALU.add))
            for g in range(14):
                dst = rkv[:, g, :] if g < 12 else (wdad, gd)[g - 12]
                pd = pad[:, g % 2, :]
                dve.wait_ge(s("bank_free%d" % (g % 8)), use_of("in0", g) + 1)
                L(V.tensor_tensor(padt[:, 1:386], pd[:, 0:385], pd[:, 2:387], ALU.add))
                L(V.tensor_scalar(padt[:, 1:386], padt[:, 1:386], stat[:, 32 + g:33 + g], None, ALU.mult))
                om = stat[:, 46 + g:47 + g]
                L(V.scalar_tensor_tensor(dst[:, 0:P], pd[:, 1:129], om, padt[:, 1:129], ALU.mult, ALU.add))
                tell(dve, V.scalar_tensor_tensor(dst[:, P:T], pd[:, 130:386], om, padt[:, 130:386], ALU.mult, ALU.add),
                          "shifted", g + 1)

            dve.wait_ge(s("mixer_params"), 16 * 8)
            dve.wait_ge(s("latent_squares"), 1)
            L(V.tensor_scalar(stat[:, 3:6], stat[:, 3:6], 256.0 / 128.0, None, ALU.mult))
            rms(0, 6, 256)
            for t, kt in enumerate((0, 2, 3)):
                L(V.tensor_copy(kpe[:, kt, :], mla[:, t, 384:448]))
                L(V.scalar_tensor_tensor(ckv[:, kt, :], mla[:, t, 256:384], stat[:, 3 + t:4 + t], rows[:, 256:384],
                                         ALU.mult, ALU.mult))
                ins = V.scalar_tensor_tensor(qc[:, t, :], mla[:, t, 0:256], stat[:, t:t + 1], rows[:, 0:256],
                                             ALU.mult, ALU.mult)
                if t < 2:
                    L(ins)
            tell(dve, ins, "latents", 1)
            for t in range(KEYTILES):
                L(V.tensor_copy(kx[:, t, :, P:QK], head_bc(kpe[:, t, :], 64, MLA_HEADS)))
                for h in range(2):
                    g = 6 + 2 * t + h
                    b = bank_full(dve, "up", g).rearrange("p (h n) -> p h n", h=2)
                    L(V.tensor_copy(kx[:, t, 2 * h:2 * h + 2, 0:P], b[:, :, 0:P]))
                    free(V.tensor_copy(vx[:, t, 2 * h:2 * h + 2, :], b[:, :, P:2 * P]), g)
                    copied(dve, "up", g)
            for g in range(6):
                copied(dve, "up", g)
            for buf, n, o, row in ((q, 12, 6, "qn"), (kx, 16, 6, "kn")):
                a = buf.rearrange("p t h c -> p (t h) c")
                sv = sq[:, 0:n * QK].rearrange("p (r c) -> p r c", r=n)
                L(V.tensor_tensor(sv, a, a, ALU.mult))
                L(V.tensor_reduce(stat[:, o:o + n], sv, AX.X, ALU.add))
                rms(o, n, QK)
                L(V.tensor_tensor(a, a, bc(stat[:, o:o + n], QK), ALU.mult))
                r0 = ROWS[row][0]
                L(V.tensor_tensor(a, a, head_bc(rows[:, r0:r0 + QK], QK, n), ALU.mult))
            for n_, (buf, t0) in enumerate(((q, 1), (kx, 2))):
                x1, x2 = (buf[:, t0:t0 + 2, :, P + e:QK:2] for e in range(2))
                cs, sn = (rope[:, e].unsqueeze(2).to_broadcast([P, 2, MLA_HEADS, 32]) for e in range(2))
                for n, (a, w) in enumerate(((x1, cs), (x2, sn), (x1, sn), (x2, cs))):
                    L(V.tensor_tensor(rtmp[:, n], a, w, ALU.mult))
                L(V.tensor_tensor(x1, rtmp[:, 0], rtmp[:, 1], ALU.subtract))
                ins = V.tensor_tensor(x2, rtmp[:, 2], rtmp[:, 3], ALU.add)
                if n_ == 0:
                    L(ins)
            tell(dve, ins, "heads_ready", 1)
            for h in range(MLA_HEADS):
                for part in (2, 3):
                    g = 4 * h + part
                    b = bank_full(dve, "headT", g)
                    if part == 2:
                        free(V.tensor_copy(kTn[:, h, :], b), g)
                    else:
                        free(V.tensor_copy(kTr[0:64, h, :], b[0:64, :]), g)
            scale = float(QK) ** -0.5
            for h in range(MLA_HEADS):
                for t in range(TILES):
                    n = P if t == 0 else 3 * P
                    b = bank_full(dve, "att", t, h)
                    m = stat[:, 3 * h + t:3 * h + t + 1]
                    L(V.tensor_reduce(m, b[:, 0:n], AX.X, ALU.max, negate=True))
                    tell(dve, V.tensor_scalar(m, m, scale, None, ALU.mult), "row_max", 3 * h + t + 1)
                dve.wait_ge(s("exps"), 3 * h + 3)
                r = stat[:, 12 + 3 * h:15 + 3 * h]
                L(V.reciprocal(r, r))
                for t, (o, n) in enumerate(((0, 1), (1, 3), (4, 3))):
                    ins = V.tensor_scalar(prob[:, o:o + n, :], prob[:, o:o + n, :], r[:, t:t + 1], None, ALU.mult)
                    if t < 2:
                        L(ins)
                tell(dve, ins, "probs", h + 1)
                b = bank_full(dve, "att", 4, h)
                free(V.tensor_copy(probT[:, 4:7, :], b[:, 0:384].rearrange("p (n c) -> p n c", n=3)), 4)
                copied(dve, "att", 4, h)

            copied(dve, "att", 5, MLA_HEADS - 1)
            tell(dve, V.memset(lora_rhs, 0.0), "lora_zero", 1)
            for m in range(PAIRS):
                L(V.tensor_scalar(kk[:, m, :], rkv[:, 4 + m, :], col("k_k", m), None, ALU.mult))
            tell(dve, V.tensor_tensor(ld, kk, kk, ALU.mult), "kk_squares", 1)
            for m in range(PAIRS):
                copied(dve, "knorm", m)
            L(V.tensor_scalar(cum, cum, 1e-12, None, ALU.max))
            L(V.reciprocal(cum, cum))
            tell(dve, V.tensor_tensor(kk, kk, cum, ALU.mult), "kk_ready", 1)
            decay = -float(np.exp(np.float64(-0.5)))
            for d in range(2):
                for m in range(PAIRS):
                    copied(dve, "lora", 8 * d + m)
                    copied(dve, "lora", 8 * d + 4 + m)
                L(V.tensor_scalar(ld, ld, decay, None, ALU.mult))
                for m in range(PAIRS):
                    L(V.tensor_tensor_scan(cum[:, m, :], scanmask[:], ld[:, m, :], 0.0, ALU.mult, ALU.add))
                tell(dve, V.tensor_tensor(cumx, cum, ld, ALU.subtract), "cums", d + 1)
                dve.wait_ge(s("decays"), d + 1)
                tr, ta, tb, tk = (tilde[:, 4 * d + n] for n in range(4))
                L(V.tensor_tensor(tr, tr, rkv[:, 0:4, :], ALU.mult))
                L(V.scalar_tensor_tensor(ta, ta, -1.0, kk, ALU.mult, ALU.mult))
                L(V.tensor_copy(tk, tb))
                L(V.tensor_tensor(tb, tb, kk, ALU.mult))
                L(V.tensor_tensor(tb, tb, lr, ALU.mult))
                for m in range(PAIRS):
                    L(V.tensor_scalar(lr[:, m, :], lr[:, m, :], -1.0, col("k_a", m), ALU.add, ALU.mult))
                kd = cum
                L(V.scalar_tensor_tensor(kd, lr, 1.0, rkv[:, 4:8, :], ALU.add, ALU.mult))
                L(V.tensor_tensor(tk, tk, kd, ALU.mult))
                if d == 0:
                    tell(dve, V.tensor_copy(gateT, kd), "dir_done", 1)
                else:
                    L(V.tensor_tensor(gateT, gateT, kd, ALU.add))
            L(V.tensor_tensor(bonus_w, gateT, rkv[:, 0:4, :], ALU.mult))
            L(V.memset(bexp, 0.0))
            for m in range(PAIRS):
                ins = V.tensor_scalar(bonus_w[:, m, :], bonus_w[:, m, :], col("r_k", m), None, ALU.mult)
                if m < PAIRS - 1:
                    L(ins)
            tell(dve, ins, "gate_free", 1)
            tell(dve, V.memset(ST[:, 0], 0.0), "state_ready", 1)
            for g in range(4):
                d, h = g // 2, g % 2
                b = bank_full(dve, "state_in", g)
                free(V.tensor_copy(ST[:, 1, d, 2 * h:2 * h + 2, :], b[:, 0:2 * CH].rearrange("p (m c) -> p m c", m=2)), g)
                copied(dve, "state_in", g)
            L(V.memset(y, 0.0))
            tell(dve, V.memset(ex, 0.0), "state_ready", 2)
            for n in range(PAIRS * NCH):
                m, c = n // NCH, n % NCH
                if n >= 2:
                    dve.wait_ge(s("bonus_mm"), n - 1)
                L(V.tensor_copy(bexp[0:64, n % 2, 0:CH], bonus_w[0:64, m, c * CH:(c + 1) * CH]))
                tell(dve, V.tensor_copy(bexp[64:P, n % 2, CH:P], bonus_w[64:P, m, c * CH:(c + 1) * CH]), "bonus_exp", n + 1)
            b = bank_full(dve, "coef", 0)
            free(V.tensor_copy(coef[:].rearrange("p m c -> p (m c)"), b[:, 0:PAIRS * NCH]), 0)
            copied(dve, "coef", 0)

            def scan_item(stage, i, d, first, chunk, seq):
                g0 = 26 * d
                it = first + d
                S = ST[:, seq, d]
                c = chunk

                def expand(n):
                    src = tilde[:, 4 * d + n]
                    L(V.tensor_copy(ex[0:64, n, :, 0:CH], src[0:64, :, bass.ts(c, CH)]))
                    V.tensor_copy(ex[64:P, n, :, CH:P], src[64:P, :, bass.ts(c, CH)]).then_inc(s("expanded"), 1)
                el = elast[:, d, :, bass.ts(c, 1)].to_broadcast([P, PAIRS, CH])
                for n in range(3):
                    expand(n)
                dve.wait_ge(s("state_ready"), it + 1)
                if d == 1:
                    V.tensor_tensor(S, S, el, ALU.mult).then_inc(s("state_scaled"), 1)
                    dve.wait_ge(s("state_scaled"), i + (1 if stage == "scanp" else 3))
                m0 = head_bc(masks[:, (6, 0)[d], :], P, PAIRS)
                m0T = head_bc(masks[:, (0, 6)[d], :], P, PAIRS)
                eye = head_bc(ident[:], P, PAIRS)
                b = bank_full(dve, stage, g0, i)
                free(V.tensor_tensor(blocks(Tm), blocks(b), m0, ALU.mult), g0)
                copied(dve, stage, g0 + 1, i)
                L(V.tensor_tensor(blocks(TT), blocks(NT), m0T, ALU.mult))
                copied(dve, stage, g0, i)
                L(V.tensor_tensor(blocks(Tm), blocks(Tm), eye, ALU.add))
                V.tensor_tensor(blocks(TT), blocks(TT), eye, ALU.add).then_inc(s("t_ready"), 1)
                for n, (dst, m) in enumerate(((KT, 12 + 2 * d), (RkT, 13 + 2 * d), (RbT, 13 + 2 * d))):
                    b = bank_full(dve, stage, g0 + 2 + n, i)
                    free(V.tensor_tensor(blocks(dst), blocks(b), head_bc(masks[:, m, :], P, PAIRS), ALU.mult), g0 + 2 + n)
                dve.wait_ge(s("t_ready"), it * 6 + 1)
                g = 9
                for lev in range(1, 6):
                    if lev < 5:
                        b = bank_full(dve, stage, g0 + g, i)
                        free(V.tensor_tensor(Tm, Tm, b, ALU.add), g0 + g)
                        copied(dve, stage, g0 + g, i)
                        g += 1
                    b = bank_full(dve, stage, g0 + g, i)
                    free(V.tensor_tensor(TT, TT, b, ALU.add), g0 + g)
                    copied(dve, stage, g0 + g, i)
                    g += 2
                    V.tensor_copy(stat[:, 62:63], ones[:, 0:1]).then_inc(s("t_ready"), 1)
                    dve.wait_ge(s("t_ready"), it * 6 + (lev + 1))
                b = bank_full(dve, stage, g0 + 24, i)
                yv = y[:, bass.ts(c, 1)].rearrange("p o m v -> p (o m v)")
                free(V.tensor_tensor(yv, yv, b[:, 0:256], ALU.add), g0 + 24)
                b = bank_full(dve, stage, g0 + 25, i)
                Sf = S.rearrange("p m v -> p (m v)")
                copied(dve, stage, g0 + 24, i)
                ins = V.tensor_tensor(Sf, Sf, b[:, 0:256], ALU.add)
                free(ins, g0 + 25)
                copied(dve, stage, g0 + 25, i)
                if d == 0:
                    ins = V.tensor_tensor(S, S, el, ALU.mult)
                else:
                    ins = V.tensor_copy(stat[:, 61:62], ones[:, 0:1])
                ins.then_inc(s("state_ready"), 1)

            c0, per = enter(0), 2 * (3 + 2)
            with dve.Fori(0, 2) as i:
                back = dve.snap(1 - i)
                for d in range(2):
                    enter(i * per + (c0 + d * (per // 2)))
                    scan_item("scanp", i, d, i * 2, i if d == 0 else back, 0)
            with dve.Fori(0, 4) as i:
                back = dve.snap(5 - i)
                for d in range(2):
                    enter(i * per + (c0 + 2 * per + d * (per // 2)))
                    scan_item("scans", i, d, i * 2 + 4, i + 2 if d == 0 else back, 1)
            enter(c0 + 6 * per)

            bank_full(dve, "scans", SCAN_GROUPS - 1, 3)
            tell(dve, V.memset(zexp, 0.0), "scan_done", 1)
            yr = y.rearrange("p c m v -> p (c m) v")
            ycr, ysr = (a.rearrange("p c m v -> p (c m) v") for a in (yc, ysq))
            n = NCH * PAIRS
            mean, var = stat[:, 0:n], stat[:, n:2 * n]
            L(V.tensor_reduce(mean, yr, AX.X, ALU.add))
            L(V.tensor_scalar(mean, mean, 1.0 / CH, None, ALU.mult))
            L(V.tensor_tensor(ycr, yr, bc(mean, CH), ALU.subtract))
            L(V.tensor_tensor(ysr, ycr, ycr, ALU.mult))
            L(V.tensor_reduce(var, ysr, AX.X, ALU.add))
            rms(n, n, CH, LNX_EPS)
            L(V.tensor_tensor(ycr, ycr, bc(var, CH), ALU.mult))
            dve.wait_ge(s("lnx_loaded"), 16 * 4)
            for m, op in ((0, ALU.mult), (1, ALU.add)):
                L(V.tensor_tensor(yc, yc, lnx[:, m].unsqueeze(1).to_broadcast([P, NCH, PAIRS, CH]), op))

            def expand_z(part, src, c, name):
                if c > 0:
                    bank_full(dve, "yT", NCH * part + c - 1)
                L(V.tensor_copy(zexp[0:64, part, :, 0:CH], src(0)))
                tell(dve, V.tensor_copy(zexp[64:P, part, :, CH:P], src(1)), name, c + 1)
            for c in range(NCH):
                expand_z(0, lambda h, c=c: rkv[64 * h:64 * h + 64, 8:12, c * CH:(c + 1) * CH], c, "vexp_ready")
            for c in range(NCH):
                b = bank_full(dve, "yT", c)
                cf = coef[:, :, c:c + 1].to_broadcast([P, PAIRS, CH])
                free(V.tensor_tensor(vtok[:, c], b[:, 0:256].rearrange("p (m v) -> p m v", m=PAIRS), cf, ALU.mult), c)
                copied(dve, "yT", c)
                L(V.tensor_tensor(yc[:, c], yc[:, c], vtok[:, c], ALU.add))
            copied(dve, "lora", 19)
            for c in range(NCH):
                expand_z(1, lambda h, c=c: yc[64 * h:64 * h + 64, c], c, "yexp_ready")
                g = NCH + c
                b = bank_full(dve, "yT", g)
                free(V.tensor_tensor(hT[:, 0:4, c * CH:(c + 1) * CH], b[:, 0:256].rearrange("p (m v) -> p m v", m=PAIRS),
                                     gateT[:, :, c * CH:(c + 1) * CH], ALU.mult), g)
            gate_columns("gate0", 2)
            add_out("out0", "gate0", [(3 * j + t, t, j) for j in range(2) for t in range(TILES)])

            def peer(l):
                norm("norm%db" % l, l, 1)
                for t in range(TILES):
                    for g in range(4):
                        copied(dve, "keys%d" % l, 4 * t + g)
                    for a in range(SIDES):
                        v, o, oi = sc[:, a, t, :], top[:, t, a, :], topi[:, t, a, :].bitcast(U32)
                        L(V.max(o[:, 0:8], v))
                        L(V.max_index(oi[:, 0:8], o[:, 0:8], v))
                        L(V.match_replace(v, o[:, 0:8], v, -3.0e38))
                        L(V.max(o[:, 8:16], v))
                        L(V.max_index(oi[:, 8:16], o[:, 8:16], v))
                    L(V.tensor_copy(topif[:, t], topi[:, t].bitcast(U32)))
                    tv = top[:, t].rearrange("p (h e) k -> p h e k", e=2)
                    ti = topif[:, t].rearrange("p (h e) k -> p h e k", e=2)
                    c4 = cand.rearrange("p h (i j) -> p h i j", i=TOPK)
                    sh = [P, HEADS, TOPK, TOPK]
                    L(V.tensor_tensor(c4, tv[:, :, 0, :].unsqueeze(3).to_broadcast(sh),
                                      tv[:, :, 1, :].unsqueeze(2).to_broadcast(sh), ALU.add))
                    for h in range(HEADS):
                        v, o, oi = cand[:, h, :], tops[:, h, :], posu[:, h, :].bitcast(U32)
                        L(V.max(o[:, 0:8], v))
                        L(V.max_index(oi[:, 0:8], o[:, 0:8], v))
                        L(V.match_replace(v, o[:, 0:8], v, -3.0e38))
                        L(V.max(o[:, 8:16], v))
                        L(V.max_index(oi[:, 8:16], o[:, 8:16], v))
                    L(V.tensor_scalar(hi.bitcast(U32), posu.bitcast(U32), 4, None, ALU.logical_shift_right))
                    L(V.tensor_scalar(lo.bitcast(U32), posu.bitcast(U32), 15, None, ALU.bitwise_and))
                    if t > 0:
                        bank_full(dve, "selT%d" % l, t - 1)
                    for e, pos in enumerate((hi, lo)):
                        L(V.tensor_copy(pos, pos.bitcast(U32)))
                        ranks = iota[:, 0:TOPK].unsqueeze(1).unsqueeze(1).to_broadcast(sh)
                        L(V.tensor_tensor(oh, pos.unsqueeze(3).to_broadcast(sh), ranks, ALU.is_equal))
                        L(V.tensor_tensor(oh, oh, ti[:, :, e, :].unsqueeze(2).to_broadcast(sh), ALU.mult))
                        L(V.tensor_reduce(pick[:, e, :], oh.rearrange("p h k m -> p (h k) m"), AX.X, ALU.add))
                    gt = pick[:, 2, :].rearrange("p (h k) -> p h k", h=HEADS)
                    tell(dve, V.tensor_tensor(gt, tops, tops[:, :, 0:1].to_broadcast([P, HEADS, TOPK]), ALU.subtract),
                              "shifted_tops", 3 * l + t + 1)
                    dve.wait_ge(s("tops_exp"), 3 * l + t + 1)
                    L(V.tensor_reduce(stat[:, 0:8], gt, AX.X, ALU.add))
                    L(V.reciprocal(stat[:, 0:8], stat[:, 0:8]))
                    tell(dve, V.tensor_tensor(gt, gt, bc(stat[:, 0:8], TOPK), ALU.mult), "picked%d" % l, t + 1)
                for t in range(TILES):
                    copied(dve, "selT%d" % l, t)
                for half in range(2):
                    base = (2 * l + half) * 48

                    def onehots(g, tok, par, wait):
                        if wait:
                            dve.wait_ge(s("w_ready"), g - 1)
                        for u in range(8):
                            tk = tok + u
                            V.tensor_scalar(ohB[:, par, u, :], iota[:, HALF * half:HALF * half + HALF],
                                            sel[:, 1, bass.ds(tk, 1)], None, ALU.is_equal)
                            ins = V.tensor_scalar(ohA[:, par, u, :], iota[:], sel[:, 0, bass.ds(tk, 1)],
                                                  sel[:, 2, bass.ds(tk, 1)], ALU.is_equal, ALU.mult)
                        ins.then_inc(s("onehots"), 1)
                    for par in range(2):
                        onehots(base + par, 8 * par, par, base > 0)
                    with dve.Fori(1, 24) as i:
                        for par in range(2):
                            onehots(i * 2 + (base + par), i * 16 + 8 * par, par, True)
                    c0_ = 128 * l + 64 * half
                    dve.wait_ge(s("w_copied"), base + 48)

                    def gates(c, local, par):
                        dve.wait_ge(s("gelu_done"), c + 1)
                        V.tensor_tensor(gw[:, par, :], gel[:, par, :],
                                        wd[:, :, bass.ds(local, 1)].rearrange("p t o -> p (t o)"),
                                        ALU.mult).then_inc(s("g_done"), 1)
                    with dve.Fori(0, 32) as i:
                        for par in range(2):
                            gates(i * 2 + (c0_ + par), i * 2 + par, par)
                dve.wait_ge(s("g_done"), 128 * (l + 1))
                gate_columns("gate%db" % l, 5)
                add_out("hot%d" % l, "gate%db" % l, [(2 * t + h, t, h) for t in range(TILES) for h in range(2)])

            bank_full(dve, "out0", 5)
            peer(0)

            adaln(1)
            norm("norm1", 1, 0)
            bank_full(dve, "norm1", 5)
            tell(dve, V.memset(pad1, 0.0), "pad_zero", 2)
            for g in range(24):
                pd = pad1[:, g % 2, :]
                dve.wait_ge(s("bank_free%d" % (g % 8)), use_of("in1", g) + 1)
                k = g % 8
                dst = (x0T[:, k, :], zinT[:, k, :], vtmp)[g // 8]
                L(V.tensor_scalar(padt1[:, 1:386], pd[:, 0:385], col("conv_w", g), col("conv_b", g), ALU.mult, ALU.add))
                L(V.scalar_tensor_tensor(padt1[:, 1:386], pd[:, 1:386], col("conv_w", 24 + g), padt1[:, 1:386],
                                         ALU.mult, ALU.add))
                for (a, b_), o in (((1, 129), 0), ((130, 386), P)):
                    ins = V.scalar_tensor_tensor(dst[:, o:o + b_ - a], pd[:, a + 1:b_ + 1], col("conv_w", 48 + g),
                                                 padt1[:, a:b_], ALU.mult, ALU.add)
                    if o == 0:
                        L(ins)
                tell(dve, ins, "shifted", 14 + g + 1)
                if g >= 16:
                    tell(dve, V.tensor_tensor(zinT[:, k, :], zinT[:, k, :], vtmp, ALU.mult), "zin_ready", k + 1)
            V.tensor_copy(stat[:, 62:63], ones[:, 0:1]).then_inc(s("slot_used"), 1)
            dve.wait_ge(s("slot_used"), JOB[("in", 1)] + 6)

            magic, two_pi = 12582912.0, 2 * np.pi
            c1 = float(np.float32(6.28125))
            c2 = float(np.float32(round((two_pi - c1) * 2 ** 20) / 2 ** 20))
            c3 = float(np.float32(two_pi - c1 - c2))
            for n in range(2):
                b = bank_full(dve, "hid", n)
                a, k_ = htmp[0:64, 0, :], htmp[0:64, 1, :]
                free(V.tensor_scalar(a, b[0:64, 0:T], col("f_b1" if n == 0 else "f_b2")[0:64], col("freq")[0:64],
                                     ALU.add, ALU.mult), n)
                copied(dve, "hid", n)
                L(V.tensor_scalar(k_, a, float(1 / two_pi), magic, ALU.mult, ALU.add))
                L(V.tensor_scalar(k_, k_, -magic, None, ALU.add))
                for c in (c1, c2, c3):
                    L(V.scalar_tensor_tensor(a, k_, -c, a, ALU.mult, ALU.add))
                tell(dve, V.tensor_scalar(a, a, 3.1415925, -3.1415925, ALU.min, ALU.max), "sin_in", n + 1)
            job_w = JOB[("window", 1)]
            landed(dve, job_w)
            win = slot(job_w)[:, 0:3072].rearrange("p (t c) -> p t c", t=3)
            for t in range(TILES):
                for n in range(4):
                    g = 4 * t + n
                    b = bank_full(dve, "filt", g)
                    h = n % 2
                    free(V.tensor_tensor(filt[:, t, 512 * n:512 * n + 512], b, win[:, t, 512 * h:512 * h + 512],
                                         ALU.mult), g)
                    copied(dve, "filt", g)
            L(V.memset(filt[0:1, 0, D:2 * D], 0.0))
            tell(dve, V.memset(filt[0:1, 1, D:2 * D], 0.0), "filters", 1)
            for g in range(4):
                b = bank_full(dve, "norm_f", g)
                free(V.reciprocal(rnorm[:, g // 2, 512 * (g % 2):512 * (g % 2) + 512], b), g)
                copied(dve, "norm_f", g)
            for g in range(12):
                f, h = g // 2, g % 2
                b = bank_full(dve, "filtF", g)
                seq = 0 if f < 4 else 1
                free(V.tensor_tensor(filtF[:, f, 512 * h:512 * h + 512], b, rnorm[:, seq, 512 * h:512 * h + 512],
                                     ALU.mult), g)
                copied(dve, "filtF", g)
            for g in range(12):
                copied(dve, "zF", g)
            for n, (re, im, special) in enumerate(((0, 2, True), (1, 3, False), (4, 5, True))):
                zr, zi, hr, hi_ = zF[:, re], zF[:, im], filtF[:, re], filtF[:, im]
                p0, p1 = prod[:, 0], prod[:, 1]
                L(V.tensor_tensor(p0, zr, hr, ALU.mult))
                L(V.tensor_tensor(p1, zi, hi_, ALU.mult))
                L(V.tensor_tensor(zr, zr, hi_, ALU.mult))
                L(V.tensor_tensor(zi, zi, hr, ALU.mult))
                L(V.tensor_tensor(zi, zi, zr, ALU.add))
                L(V.tensor_tensor(zr, p0, p1, ALU.subtract))
                if special:
                    L(V.tensor_copy(zr[0:1, :], p0[0:1, :]))
                    ins = V.tensor_copy(zi[0:1, :], p1[0:1, :])
                    if n < 2:
                        L(ins)
            tell(dve, ins, "spectra_ready", 1)
            for k in range(KD):
                b = bank_full(dve, "conv", k)
                free(V.scalar_tensor_tensor(zinT[:, k, :], zinT[:, k, :], col("bias", k), b[:, 0:T], ALU.mult, ALU.add), k)
                copied(dve, "conv", k)
                tell(dve, V.tensor_tensor(hT[:, k, :], zinT[:, k, :], x0T[:, k, :], ALU.mult), "conv_out", k + 1)
            gate_columns("gate1", 2)
            add_out("out1", "gate1", [(3 * j + t, t, j) for j in range(2) for t in range(TILES)])
            bank_full(dve, "out1", 5)
            peer(1)
            V.tensor_copy(stat[:, 62:63], ones[:, 0:1]).then_inc(s("y_done"), 1)

        @block.scalar
        def _(act):
            A = nc.scalar.activation
            L, enter = chain(act, "act_chain")
            roots = [0]

            def root(ss, n):
                roots[0] += 1
                act.wait_ge(s("to_root"), roots[0])
                A(stat[:, ss:ss + n], stat[:, ss:ss + n], ACT.Sqrt).then_inc(s("rooted"), 1)

            def norm(stage, l, part):
                no = NORM_NO[stage]
                if no > 0:
                    act.wait_ge(s("x_new"), no)
                for t in range(TILES):
                    ins = A(junk, x[:, t, :], ACT.Square, accum_out=stat[:, t:t + 1])
                    if t < 2:
                        L(ins)
                tell(act, ins, "x_squares", no + 1)
                root(0, 3)
                act.wait_ge(s("gsc_ready"), no + 1)
                for t in range(TILES):
                    c = 0 if t == 0 else 1
                    for h in range(2):
                        b = bank_full(act, stage, 2 * t + h)
                        for j in range(4):
                            k = 4 * h + j
                            ins = A(hT[:, k, t * P:(t + 1) * P], b[:, j * P:(j + 1) * P], ACT.Identity,
                                    bias=modc[:, 24 * part + k, c:c + 1], scale=gsc[:, k, c:c + 1])
                        free(ins, 2 * t + h)

            def gate_rows(stage):
                for c in range(2):
                    for h in range(2):
                        g = GROUPS[stage][2 * c + h]
                        b = bank_full(act, stage, g)
                        free(A(gate_row[:, c, 512 * h:512 * h + 512], b, ACT.Copy), g)

            act.wait_ge(s("inputs"), 16 * 8)
            cond = cols[:, COLS["cond"]:COLS["cond"] + 16].rearrange("p (k c) -> p k c", k=KD)
            A(condT[:], cond, ACT.Sigmoid).then_inc(s("cond_sig"), 1)
            norm("norm0", 0, 0)
            act.wait_ge(s("pad_zero"), 1)
            for g in range(14):
                if g >= 2:
                    act.wait_ge(s("shifted"), g - 1)
                b = bank_full(act, "in0", g)
                L(A(pad[:, g % 2, 1:129], b[:, 0:P], ACT.Copy))
                free(A(pad[:, g % 2, 130:386], b[:, P:T], ACT.Copy), g)
            for t in range(TILES):
                b = bank_full(act, "in0", 14 + t)
                free(A(mla[:, t, :], b[:, 0:448], ACT.Copy), 14 + t)
            for t in range(TILES):
                copied(act, "in0", 14 + t)
            act.wait_ge(s("shifted"), 14)
            for t in range(TILES):
                L(A(padt[:, 0:256], mla[:, t, 0:256], ACT.Square, accum_out=stat[:, t:t + 1]))
                ins = A(padt[:, 0:128], mla[:, t, 256:384], ACT.Square, accum_out=stat[:, 3 + t:4 + t])
                if t < 2:
                    L(ins)
            tell(act, ins, "latent_squares", 1)
            root(0, 6)
            for g in range(3):
                b = bank_full(act, "qkvT", g)
                if g < 2:
                    free(A(qcT[:, g, :], b[:, 0:T], ACT.Copy), g)
                else:
                    free(A(ckvT, b, ACT.Copy), g)
            for t in range(TILES):
                for h in range(2):
                    b = bank_full(act, "up", 2 * t + h)
                    free(A(q[:, t, 2 * h:2 * h + 2, :], b[:, 0:384].rearrange("p (h c) -> p h c", h=2), ACT.Copy), 2 * t + h)
            root(6, 12)
            root(6, 16)
            for h in range(MLA_HEADS):
                b = bank_full(act, "headT", 4 * h)
                free(A(qTn[:, h, :], b[:, 0:T], ACT.Copy), 4 * h)
                b = bank_full(act, "headT", 4 * h + 1)
                free(A(qTr[0:64, h, :], b[0:64, 0:T], ACT.Copy), 4 * h + 1)
            scale = float(QK) ** -0.5
            for h in range(MLA_HEADS):
                if h > 0:
                    bank_full(act, "att", 4, h - 1)
                for t, (o, n) in enumerate(((0, 1), (1, 3), (4, 3))):
                    act.wait_ge(s("row_max"), 3 * h + t + 1)
                    b = bank_full(act, "att", t, h)
                    ins = A(prob[:, o:o + n, :], b[:, 0:n * P].rearrange("p (n c) -> p n c", n=n), ACT.Exp,
                            bias=stat[:, 3 * h + t:3 * h + t + 1], scale=scale,
                            accum_out=stat[:, 12 + 3 * h + t:13 + 3 * h + t])
                    free(ins, t)
                    copied(act, "att", t, h)
                    A(stat[:, 60:61], ones[:, 0:1], ACT.Copy).then_inc(s("exps"), 1)
                    act.wait_ge(s("exps"), 3 * h + t + 1)
                b = bank_full(act, "att", 3, h)
                free(A(probT[:, 0:4, :], blocks(b), ACT.Copy), 3)
                b = bank_full(act, "att", 5, h)
                free(A(hT[:, 4 + h, :], b[:, 0:T], ACT.Copy), 5)
            act.wait_ge(s("lora_zero"), 1)
            A(lora_rhs[0:64, 0, :], wdad[0:64, :], ACT.Tanh).then_inc(s("lora_in"), 1)
            A(lora_rhs[64:P, 1, :], wdad[64:P, :], ACT.Copy).then_inc(s("lora_in"), 1)
            A(gd, gd, ACT.Sigmoid).then_inc(s("lora_in"), 1)
            for m in range(PAIRS):
                b = bank_full(act, "knorm", m)
                free(A(cum[:, m, :], b[:, 0:T], ACT.Sqrt), m)
            for d in range(2):
                if d == 0:
                    act.wait_ge(s("kk_ready"), 1)
                else:
                    act.wait_ge(s("dir_done"), 1)
                for part, (dst, name) in enumerate(((ld, "w0"), (lr, "a0"))):
                    for m in range(PAIRS):
                        g = 8 * d + 4 * part + m
                        b = bank_full(act, "lora", g)
                        free(A(dst[:, m, :], b[:, 0:T], ACT.Sigmoid, bias=col(name, 4 * d + m)), g)
                act.wait_ge(s("cums"), d + 1)
                if d == 0:
                    act.wait_ge(s("stored"), 16 * 2)
                L(A(elast[:, d], cum[:, :, CH - 1:T:CH], ACT.Exp))
                tr, ta, tb = (tilde[:, 4 * d + n] for n in range(3))
                for n, (dst, src, sign) in enumerate((((tr, cum, 1.0), (ta, cumx, 1.0), (tb, cum, -1.0)),
                                                      ((tr, cumx, -1.0), (ta, cum, -1.0), (tb, cumx, 1.0)))[d]):
                    ins = A(dst, src, ACT.Exp, scale=sign)
                    if n < 2:
                        L(ins)
                tell(act, ins, "decays", d + 1)
            act.wait_ge(s("gate_free"), 1)
            for m in range(PAIRS):
                b = bank_full(act, "lora", 16 + m)
                free(A(gateT[:, m, :], b[:, 0:T], ACT.Copy), 16 + m)

            def scan_item(stage, i, d, first, chunk):
                g0 = 26 * d
                it = first + d
                for n, src in ((3, tilde[:, 4 * d + 3]), (4, rkv[:, 8:12, :])):
                    L(A(ex[0:64, n, :, 0:CH], src[0:64, :, bass.ts(chunk, CH)], ACT.Copy))
                    A(ex[64:P, n, :, CH:P], src[64:P, :, bass.ts(chunk, CH)], ACT.Copy).then_inc(s("expanded"), 1)
                for g, dst in ((1, NT), (5, ktok), (6, btok), (7, Vt)):
                    b = bank_full(act, stage, g0 + g, i)
                    free(A(dst, b[:, 0:dst.shape[1]], ACT.Copy), g0 + g)
                g = 8
                for lev in range(1, 6):
                    b = bank_full(act, stage, g0 + g, i)
                    free(A(Pm, b, ACT.Copy), g0 + g)
                    g += 3
                for g, dst in ((22, Xt), (23, SA)):
                    b = bank_full(act, stage, g0 + g, i)
                    free(A(dst, b[:, 0:256], ACT.Copy), g0 + g)

            act.wait_ge(s("state_ready"), 2)
            c0, per = enter(0), 4
            with act.Fori(0, 2) as i:
                back = act.snap(1 - i)
                for d in range(2):
                    enter(i * per + (c0 + 2 * d))
                    scan_item("scanp", i, d, i * 2, i if d == 0 else back)
            for d in range(2):
                b = bank_full(act, "state_out", d)
                free(A(s0[:, d].rearrange("v h k -> v (h k)"), b[0:64, :], ACT.Copy), d)
                copied(act, "state_out", d)
                A(stat[:, 60:61], ones[:, 0:1], ACT.Copy).then_inc(s("state_copied"), 1)
                act.wait_ge(s("state_copied"), d + 1)
            with act.Fori(0, 4) as i:
                back = act.snap(5 - i)
                for d in range(2):
                    enter(i * per + (c0 + 2 * per + 2 * d))
                    scan_item("scans", i, d, i * 2 + 4, i + 2 if d == 0 else back)
            enter(c0 + 6 * per)
            root(24, 24)
            gate_rows("gate0")

            def peer(l):
                norm("norm%db" % l, l, 1)
                for g in range(16):
                    b = bank_full(act, "wq%d" % l, g)
                    free(A(qT[:, g, :], b[:, 0:T], ACT.Copy), g)
                for t in range(TILES):
                    for g in range(4):
                        b = bank_full(act, "keys%d" % l, 4 * t + g)
                        free(A(sc[:, 4 * g:4 * g + 4, t, :], blocks(b), ACT.Copy), 4 * t + g)
                for t in range(TILES):
                    act.wait_ge(s("shifted_tops"), 3 * l + t + 1)
                    A(pick[:, 2, :], pick[:, 2, :], ACT.Exp).then_inc(s("tops_exp"), 1)
                    b = bank_full(act, "selT%d" % l, t)
                    free(A(sel[:, :, t * P:(t + 1) * P], b[:, 0:384].rearrange("p (n c) -> p n c", n=3), ACT.Copy), t)
                for half in range(2):
                    base = (2 * l + half) * 48
                    c0_ = 128 * l + 64 * half
                    if c0_ > 0:
                        act.wait_ge(s("g_done"), c0_)

                    def dense(g, tok, par):
                        act.wait_ge(s("w_ready"), g + 1)
                        A(wd[:, bass.ds(tok, 8), :], psum[:, 6 + par, :].rearrange("p (t c) -> p t c", t=8),
                          ACT.Copy).then_inc(s("w_copied"), 1)
                    with act.Fori(0, 24) as i:
                        for par in range(2):
                            dense(i * 2 + (base + par), i * 16 + 8 * par, par)

                    def gelu(c, par, wait):
                        act.wait_ge(s("h_ready"), c + 1)
                        if wait:
                            act.wait_ge(s("g_done"), c - 1)
                        A(gel[:, par, :], psum[:, 6 + par, 0:T], ACT.Gelu_apprx_tanh).then_inc(s("gelu_done"), 1)
                    for par in range(2):
                        gelu(c0_ + par, par, c0_ > 0)
                    with act.Fori(1, 32) as i:
                        for par in range(2):
                            gelu(i * 2 + (c0_ + par), par, True)
                gate_rows("gate%db" % l)
            peer(0)

            norm("norm1", 1, 0)
            act.wait_ge(s("pad_zero"), 2)
            for g in range(24):
                if g >= 2:
                    act.wait_ge(s("shifted"), 14 + g - 1)
                b = bank_full(act, "in1", g)
                L(A(pad1[:, g % 2, 1:129], b[:, 0:P], ACT.Identity, bias=col("b_in", g)))
                free(A(pad1[:, g % 2, 130:386], b[:, P:T], ACT.Identity, bias=col("b_in", g)), g)
            for n in range(2):
                act.wait_ge(s("sin_in"), n + 1)
                A(hid[0:64, n, :], htmp[0:64, 0, :], ACT.Sin).then_inc(s("hid_ready"), 1)
            act.wait_ge(s("filters"), 1)
            na = 0
            for tiles in ((1, 2), (0,)):
                for h in range(2):
                    for t in tiles:
                        for part in range(2):
                            o = part * D + 512 * h
                            A(absf[:, na, :], filt[:, t, o:o + 512], ACT.Abs).then_inc(s("abs_ready"), 1)
                            na += 1
            copied(act, "filtF", 11)
            for g in range(6):
                b = bank_full(act, "zT", g)
                free(A(z[:, g // 2, 512 * (g % 2):512 * (g % 2) + 512], b, ACT.Copy), g)
            for g in range(12):
                b = bank_full(act, "zF", g)
                free(A(zF[:, g // 2, 512 * (g % 2):512 * (g % 2) + 512], b, ACT.Copy), g)
            gate_rows("gate1")
            peer(1)

    return nc


def weight_jobs(w):
    n = -(-w.shape[1] // 512)
    out = np.zeros((n, P, KD, 512), np.float32)
    for j in range(n):
        part = w[:, 512 * j:512 * (j + 1)]
        out[j, :, :, :part.shape[1]] = part.reshape(KD, P, -1).transpose(1, 0, 2)
    return out.reshape(n, P, SLOT)


def uv_jobs(u, v):
    out = np.empty((UVJOBS, P, 2, 2 * D), np.float32)
    out[:, :, 0, :] = u.reshape(P, UVJOBS, 2, KD, P).transpose(1, 4, 2, 3, 0).reshape(UVJOBS, P, 2 * D)
    out[:, :, 1, :] = v.reshape(P, UVJOBS, 2 * D).transpose(1, 0, 2)
    return out.reshape(UVJOBS, P, SLOT)


def column(v):
    return v.reshape(-1, P).T


def dft_tables(L):
    t, f = np.arange(L)[:, None], np.arange(L)[None, :]
    ang = 2 * np.pi * ((t * f) % (2 * L)) / (2 * L)
    re, im = np.cos(ang), -np.sin(ang)
    ny = np.cos(np.pi * t[:, 0])
    im[:, 0] = ny
    fwd = np.concatenate([re, im], 1)
    imb = np.sin(ang)
    imb[:, 0] = ny
    bwd = np.concatenate([re, imb], 1)
    bwd[0] = 0
    w = np.full(L, 2.0)
    w[0] = 1.0
    inv_re = (w[:, None] * np.cos(ang.T)) / (2 * L)
    inv_im = (-2.0 * np.sin(ang.T)) / (2 * L)
    inv_im[0] = ny / (2 * L)
    inv = np.concatenate([inv_re, inv_im], 0)
    return [a.astype(np.float32) for a in (fwd, bwd, inv)]


def hyena_constants():
    zpos, window = np.zeros((33, T), np.float32), np.zeros((P, 3, D), np.float32)
    f = np.float32
    deltas = np.linspace(np.log(1e-2) / 0.3, np.log(1e-2) / 1.5, D).astype(f)
    bands = np.linspace(1e-4, 15, 16).astype(f)
    for L, o in ((P, 0), (2 * P, P)):
        t = np.arange(L, dtype=f)[:, None]
        unit = t / f(L - 1)
        ang = (f(2.0 * np.pi) * t * bands / f(L)).astype(f)
        zpos[:, o:o + L] = np.concatenate([unit, np.cos(ang), -np.sin(ang)], 1).T
        win = np.exp(-unit * np.abs(deltas))
        window[:, o // P:(o + L) // P, :] = win.reshape(-1, P, D).transpose(1, 0, 2)
    return zpos, window


def scan_masks():
    j, t = np.arange(P)[:, None] % CH, np.arange(P)[None, :] % CH
    out = []
    for d in range(2):
        for lev in range(6):
            b = 1 << lev
            m = (t // (2 * b) == j // (2 * b)) & ((t // b) % 2 == 1) & ((j // b) % 2 == 0)
            if d == 1:
                m = (t // (2 * b) == j // (2 * b)) & ((j // b) % 2 == 1) & ((t // b) % 2 == 0)
            out.append(m)
    out += [j < t, j <= t, j > t, j >= t]
    return np.stack(out, 1).astype(np.float32)


def fill(n):
    return np.zeros((P, n), np.float32)


def kernel(**inputs):
    import concourse.bacc as bacc
    from concourse.bass_utils import run_bass_kernel_spmd

    a = {k: np.ascontiguousarray(v) for k, v in inputs.items()}
    f = np.float32
    zpos, window = hyena_constants()
    jobs = []
    for l in range(2):
        jobs.append(weight_jobs(a["w_mod"][l]))
        if l == 0:
            w = a["ab_w_in"][0]
            jobs += [weight_jobs(w[:, :1792]), weight_jobs(w[:, 1792:])]
            small = fill(SLOT)
            small[:, 0:1536] = a["mla_q_up"][0].reshape(2, P, 768).transpose(1, 0, 2).reshape(P, 1536)
            small[:, 1536:2560] = a["mla_kv_up"][0]
            small[0:64, 2560:3584] = a["rw_w2"][0].transpose(1, 0, 2).reshape(64, 1024)
            small[64:P, 2560:3584] = a["rw_a2"][0].transpose(1, 0, 2).reshape(64, 1024)
            small[:, 3584:4096] = a["rw_g2"][0]
            jobs += [small[None], weight_jobs(a["ab_w_out"][0])]
        else:
            jobs.append(weight_jobs(a["hy_w_in"][0]))
            win, flt, dft = fill(SLOT), fill(SLOT), fill(SLOT)
            win[:, 0:3072] = window.reshape(P, 3072)
            flt[0:64, 0:2048] = a["hy_f_w3"][0]
            flt[0:33, 2048:2432] = zpos
            flt[0:33, 2432:2496] = a["hy_f_w1"][0]
            flt[0:64, 2496:2560] = a["hy_f_w2"][0]
            o = 0
            for L in (2 * P, P):
                for m in dft_tables(L):
                    n = m.size // P
                    dft[:, o:o + n] = m.reshape(-1, P, m.shape[1]).transpose(1, 0, 2).reshape(P, n)
                    o += n
            jobs += [win[None], flt[None], dft[None], weight_jobs(a["hy_w_out"][0])]
        keys = fill(SLOT)
        keys[:, 0:2048] = a["peer_keys"][l].reshape(SIDES, P, P).transpose(2, 0, 1).reshape(P, 2048)
        jobs += [weight_jobs(a["peer_w_q"][l]), keys[None], uv_jobs(a["peer_u"][l], a["peer_v"][l])]
    stream = np.concatenate(jobs)
    assert len(stream) == N_JOBS

    cols = fill(N_COLS)

    def put(name, block):
        cols[:block.shape[0], COLS[name]:COLS[name] + block.shape[1]] = block
    put("mu", column(a["rw_mu"][0]))
    put("k_k", column(a["rw_k_k"][0]))
    put("k_a", column(a["rw_k_a"][0]))
    put("r_k", column(a["rw_r_k"][0]))
    put("w0", column(a["rw_w0"][0]))
    put("a0", column(a["rw_a0"][0]))
    put("g", column(a["norm_g"]))
    put("b_mod", column(a["b_mod"]))
    put("b_in", column(a["hy_b_in"][0]))
    put("conv_w", column(a["hy_conv_w"][0]))
    put("conv_b", column(a["hy_conv_b"][0]))
    put("bias", column(a["hy_bias"][0]))
    put("f_b1", a["hy_f_b1"][0][:, None])
    put("f_b2", a["hy_f_b2"][0][:, None])
    put("freq", a["hy_f_freq"][0][:, None])
    put("cond", np.stack([a["c_ctx"], a["c"][0]], 1).reshape(KD, P, 2).transpose(1, 0, 2).reshape(P, 16))

    consts = fill(832)
    i = np.arange(P)
    consts[:, 0:128] = np.eye(P)
    consts[:, 128:256] = i[:, None] // 64 == i[None, :] // 64
    consts[:, 256:320] = i[:, None] % 64 == np.arange(64)[None, :]
    consts[:, 320:704] = (np.arange(T) % CH != 0)[None, :]
    consts[:, 704:832] = i[None, :]

    pos = np.arange(2 * P)
    inv = (f(10000.0) ** (-np.arange(16, dtype=f) / f(16))).astype(f)
    ang = np.concatenate([(pos // 64)[:, None].astype(f) * inv, (pos % 64)[:, None].astype(f) * inv], 1)
    rope = np.stack([np.cos(ang), np.sin(ang)]).astype(f)

    arrays = {
        "x_prompt": a["x_prompt"], "x_sample": a["x_sample"], "cols": cols, "consts": consts,
        "masks": scan_masks(), "rope": rope, "stream": stream,
        "rows": np.concatenate([a["mla_q_norm"][0], a["mla_kv_norm"][0], a["mla_qn"][0], a["mla_kn"][0]])[None],
        "cache_mla_ckv": a["cache_mla_ckv"], "cache_mla_kpe": a["cache_mla_kpe"],
        "state_rwkv_fwd": a["state_rwkv_fwd"], "state_rwkv_bwd": a["state_rwkv_bwd"],
        "lnx_g": a["rw_lnx_g"][0].reshape(PAIRS, 2, CH).transpose(1, 0, 2).copy(),
        "lnx_b": a["rw_lnx_b"][0].reshape(PAIRS, 2, CH).transpose(1, 0, 2).copy(),
    }
    outs = {"o_prompt": (1, P, D), "o_sample": (1, 2 * P, D), "o_fwd": (1, 1, HEADS, 64, 64),
            "o_bwd": (1, 1, HEADS, 64, 64), "o_ckv": (1, 1, P, 128), "o_kpe": (1, 1, P, 64)}
    nc = bacc.Bacc("TRN2", target_bir_lowering=False, num_devices=1)
    io = {}
    for k, v in arrays.items():
        io[k] = nc.dram_tensor("in_" + k, v.shape, F32, kind="ExternalInput").ap()
    for k, shape in outs.items():
        io[k] = nc.dram_tensor(k, shape, F32, kind="ExternalOutput").ap()
    build(nc, io)
    r = run_bass_kernel_spmd(nc, [{"in_" + k: v for k, v in arrays.items()}], core_ids=[0]).results[0]
    return tuple(r[k] for k in outs)
```

```python
from contextlib import ExitStack
from itertools import zip_longest

import numpy as np

import concourse.bass as bass
from concourse import mybir

F32 = mybir.dt.float32
U32 = mybir.dt.uint32
BF16 = mybir.dt.bfloat16
F32R = mybir.dt.float32r
ALU = mybir.AluOpType
ACT = mybir.ActivationFunctionType
AX = mybir.AxisListType

P = 128
D = 1024
KD = D // P
TILES = 3
T = TILES * P
EPS = 1e-6
LNX_EPS = 64e-5
HEADS = 8
PAIRS = HEADS // 2
CH = 64
NCH = T // CH
MLA_HEADS = 4
QK = 192
KEYTILES = 4
SLOT = 4096
RING = 3
TOPK = 16
SIDES = 16
SLICE = 16
SLICES = P // SLICE
UVRING = 2
STEPS = 2 * UVRING
BLOCKS = SLICE // STEPS
BUILD = 8
PER_STEP = T // BUILD // SLICE
NG = T // BUILD
UVJOBS = 64

JOB_COUNTS = [[("mod", 12), ("in", 5), ("small", 1), ("scratch", 2), ("out", 2), ("keys", 1), ("wq", 4), ("mod1", 12),
               ("uv", UVJOBS)],
              [("in", 6), ("window", 1), ("filter", 1), ("dft", 1), ("out", 2), ("keys", 1),
               ("wq", 4), ("uv", UVJOBS)]]
JOB = {}
N_JOBS = 0
for _l, _jobs in enumerate(JOB_COUNTS):
    for _name, _n in _jobs:
        JOB[("mod", 1) if _name == "mod1" else (_name, _l)] = N_JOBS
        N_JOBS += _n

SLOT_OF, BEFORE, LANDING = [], [], []
SCRATCH = [JOB[("scratch", 0)], JOB[("scratch", 0)] + 1]
for _j in range(N_JOBS):
    _uv = [_j - JOB[("uv", _l)] for _l in range(2) if 0 <= _j - JOB[("uv", _l)] < UVJOBS]
    _slot = _uv[0] % UVRING if _uv else _j % RING
    _same = [_i for _i in range(_j) if SLOT_OF[_i] == _slot]
    SLOT_OF.append(_slot)
    BEFORE.append(_same[-1] if _same else -1)
    LANDING.append(len([_i for _i in _same if _i not in SCRATCH]) + 1)

SCAN_GROUPS = tuple(sorted(8 * (_g // 4) + 4 * _d + _g % 4 for _d in range(2) for _g in range(26)))
STAGES = [("mod0", 8, 3), ("norm0", 6, 1), ("in0", 17, 1), ("qkvT", 3, 1), ("up", 14, 1), ("headT", 16, 1),
          ("att", 6, MLA_HEADS), ("knorm", 4, 1), ("lora", 20, 1), ("state_in", 4, 1), ("coef", 1, 1),
          ("scanp", SCAN_GROUPS, 2), ("state_out", 2, 1), ("scans", SCAN_GROUPS, 4),
          ("yT", 12, 1), ("gate0", 4, 1), ("out0", 6, 1), ("norm0b", 6, 1), ("wk0", 28, 1),
          ("sel0", 9, 3), ("hot0", 6, 1), ("gate0b", (6, 7, 14, 15), 1),
          ("norm1", 6, 1), ("in1", 24, 1), ("hid", 2, 1), ("filt", 12, 1), ("norm_f", 4, 1),
          ("filtF", 12, 1), ("zT", 6, 1), ("zF", 12, 1), ("conv", 8, 1), ("gate1", 4, 1), ("out1", 6, 1),
          ("norm1b", 6, 1), ("wk1", 28, 1), ("sel1", 1, 3), ("hot1", 6, 1), ("gate1b", (6, 7, 14, 15), 1)]


def plan_banks():
    used, first, groups = [0] * 8, {}, {}
    for stage, gs, n in STAGES:
        first[stage], groups[stage] = list(used), range(gs) if isinstance(gs, int) else gs
        for q in groups[stage]:
            used[q % 8] += n
    return first, groups


FIRST, GROUPS = plan_banks()


def use_of(stage, q, i=0):
    same = [g for g in GROUPS[stage] if g % 8 == q % 8]
    before = FIRST[stage][q % 8] + same.index(q)
    if isinstance(i, int):
        return before + len(same) * i
    return i * len(same) + before


def sg(d, g):
    return 8 * (g // 4) + 4 * d + g % 4


WQ = [_g + 3 * max(0, (_g - 1) // 4) for _g in range(16)]
KEYG = [[_f + _t for _f in (5, 12, 19, 25)] for _t in range(3)]
SELG = [8, 0]
NORM_NO = {"norm0": 0, "norm0b": 1, "norm1": 2, "norm1b": 3}
GATE_NO = {"gate0": 0, "gate0b": 1, "gate1": 2, "gate1b": 3}

COLS = {}
N_COLS = 0
for _name, _n in [("mu", 14), ("k_k", 4), ("k_a", 4), ("r_k", 4), ("w0", 8), ("a0", 8), ("g", 32), ("b_mod", 96),
                  ("b_in", 24), ("conv_w", 72), ("conv_b", 24), ("bias", 8), ("f_b1", 1), ("f_b2", 1), ("freq", 1),
                  ("cond", 16)]:
    COLS[_name] = N_COLS
    N_COLS += _n
ROWS = {"q_norm": (0, 256), "kv_norm": (256, 128), "qn": (384, 192), "kn": (576, 192)}
N_ROWS = 768


def build(nc, io):
    with ExitStack() as ctx:
        def sb(name, shape, dt=F32):
            return ctx.enter_context(nc.sbuf_tensor(name, shape, dt))

        sems = {}

        def s(name):
            if name not in sems:
                sems[name] = ctx.enter_context(nc.semaphore(name))
            return sems[name]

        ring = sb("ring", [P, RING, SLOT])
        x = sb("x", [P, TILES, D])
        cols = sb("cols", [P, N_COLS])
        modc = sb("modc", [P, 2, 48, 2])
        gsc = sb("gsc", [P, KD, 2])
        condT = sb("condT", [P, KD, 2])
        ident = sb("ident", [P, P])
        stacked = sb("stacked", [P, CH])
        iota = sb("iota", [P, P])
        rep16 = sb("rep16", [P, P * BUILD], BF16)
        ones = sb("ones", [P, P])
        headones = sb("headones", [P, P])
        stat = sb("stat", [P, 64])
        elast = sb("elast", [P, 2, PAIRS, NCH])
        coef = sb("coef", [P, PAIRS, NCH])
        shared = sb("shared", [P, 4480])
        masks = shared[:, 0:2048].rearrange("p (m c) -> p m c", m=16)
        ST = shared[:, 2048:3072].rearrange("p (s d m v) -> p s d m v", s=2, d=2, m=PAIRS)
        s0 = shared[0:64, 3072:4096].rearrange("v (d h k) -> v d h k", d=2, h=HEADS)
        scanmask = shared[:, 4096:4480]
        sel = shared[:, 0:3 * T].rearrange("p (m t) -> p m t", m=3)
        sel16 = shared[:, 3 * T:11 * T // 2].bitcast(BF16).rearrange("p (m t) -> p m t", m=5)
        gel = shared[:, 6 * T:8 * T].rearrange("p (b t) -> p b t", b=2)
        gw = shared[:, 8 * T:10 * T].rearrange("p (b t) -> p b t", b=2)
        with nc.sbuf_tensor("arena", [P, 27648], F32) as arena, nc.sbuf_tensor("hT", [P, KD, T], F32) as hT:
            pass
        wd = sb("wd", [P, 2, T, SLICE])
        xs = sb("xs", [P, 2, KD, T], F32R)
        us = sb("us", [P, 2, 2, D], F32R)
        vs = sb("vs", [P, 2, 2, D], F32R)
        gs = sb("gs", [P, 2, 2, T], F32R)
        ohA = sb("ohA", [P, 2, P, BUILD], BF16)
        ohE = sb("ohE", [P, SLICE, BUILD], BF16)
        ohB = sb("ohB", [P, 2, 3, SLICE, BUILD], BF16)
        psum = ctx.enter_context(nc.psum_tensor("psum", [P, 8, 512], F32))

        def area(off, *shape):
            n = 1
            for d in shape:
                n *= d
            assert off + n <= 27648, (off, shape)
            a = arena[:, off:off + n]
            if len(shape) == 1:
                return a
            names = "abcd"[:len(shape)]
            return a.rearrange("p (%s) -> p %s" % (" ".join(names), " ".join(names)),
                               **{names[k]: shape[k] for k in range(len(shape) - 1)})

        rkv = area(0, 12, T)
        wdad = area(4608, T)
        gd = area(4992, T)
        mla0 = 5376
        mla = area(mla0, 3, 448)
        ckv = area(mla0 + 1344, KEYTILES, 128)
        kpe = area(mla0 + 1856, KEYTILES, 64)
        qc = area(mla0 + 2112, 3, 256)
        qcT = area(mla0 + 2880, 2, T)
        ckvT = area(mla0 + 3648, KEYTILES * P)
        q = area(mla0 + 4160, 3, MLA_HEADS, QK)
        kx = area(mla0 + 6464, KEYTILES, MLA_HEADS, QK)
        vx = area(mla0 + 9536, KEYTILES, MLA_HEADS, P)
        qTn = area(mla0 + 11584, MLA_HEADS, T)
        qTr = area(mla0 + 13120, MLA_HEADS, T)
        kTn = area(mla0 + 14656, MLA_HEADS, 4 * P)
        kTr = area(mla0 + 16704, MLA_HEADS, 4 * P)
        sq = area(mla0 + 14656, 3072)
        prob = area(mla0 + 0, 7, P)
        probT = area(mla0 + 2112, 7, P)
        rows = area(mla0 + 18752, N_ROWS)
        rope = area(mla0 + 19520, 2, 2, 32)
        rtmp = area(mla0 + 19648, 4, 2, MLA_HEADS, 32)
        assert mla0 + 19648 + 1024 <= 27648
        tilde = area(5376, 8, PAIRS, T)
        gateT = area(17664, PAIRS, T)
        kk = area(19200, PAIRS, T)
        ld = area(20736, PAIRS, T)
        cum = area(22272, PAIRS, T)
        cumx = area(23808, PAIRS, T)
        lr = area(25344, PAIRS, T)
        tr0 = 19200
        flat = ring[:, 0:2, :].rearrange("p s n -> p (s n)")
        assert [SLOT_OF[j] for j in SCRATCH] == [0, 1]

        def transients(base, sa):
            m = [base[:, 2560 + 512 * n:3072 + 512 * n] for n in range(10)]
            return [base[:, 0:2560].rearrange("p (n m c) -> p n m c", n=5, m=PAIRS)] + m + [
                base[:, 7680:7936], base[:, 7936:8192], sa]
        scan_mem = [transients(arena[:, tr0:tr0 + 8192], area(tr0 + 8192, 256)), transients(flat, area(4608, 256))]
        y = area(1536, NCH, PAIRS, CH)
        lora_rhs = area(26880, 2, T)
        bexp = area(26880, 2, P)
        bonus_w = area(0, PAIRS, T)
        lnx = area(tr0, 2, PAIRS, CH)
        yc = area(tr0 + 512, NCH, PAIRS, CH)
        ysq = area(tr0 + 2048, NCH, PAIRS, CH)
        zexp = area(tr0 + 3584, 2, PAIRS, P)
        vtok = area(tr0 + 4608, NCH, PAIRS, CH)
        pad = area(mla0 + 20736, 2, 388)
        padt = area(mla0 + 21512, 388)
        xn = area(24576, 1024)
        xn2 = area(25600, 1024)
        junk = area(26624, 1024)
        gate_row = area(20480, 2, D)
        x0T = area(0, KD, T)
        zinT = area(3072, KD, T)
        filtF = area(6144, 6, D)
        zF = area(12288, 6, D)
        filt = area(12288, 3, 2 * D)
        z = area(18432, 3, D)
        absf = area(6144, 12, 512)
        rnorm = area(18432, 2, D)
        hid = area(22528, 2, T)
        htmp = area(23296, 2, T)
        prod = area(21504, 2, D)
        pad1 = area(24576, 2, 388)
        padt1 = area(25352, 388)
        vtmp = area(25740, T)
        gate_bc = area(9216, 16, P)
        qT = area(0, SIDES, T)
        sc = area(6144, SIDES, TILES, P)
        top = area(12288, TILES, SIDES, TOPK)
        topi = area(13056, TILES, SIDES, TOPK)
        topif = area(13824, TILES, SIDES, TOPK)
        cand = area(14592, HEADS, 256)
        tops = area(16640, HEADS, TOPK)
        posu = area(16768, HEADS, TOPK)
        hi = area(16896, HEADS, TOPK)
        lo = area(17024, HEADS, TOPK)
        oh = area(17152, HEADS, TOPK, TOPK)
        pick = area(19200, 3, P)
        subkeys = area(20480, SIDES, P)
        modrow = area(22528, 2, 512)

        block = ctx.enter_context(nc.Block())

        def slot(job):
            return ring[:, SLOT_OF[job], :]

        def landed(eng, job):
            eng.wait_ge(s("landed%d" % SLOT_OF[job]), 16 * LANDING[job])

        def bank_free(eng, stage, g, i=0):
            u = use_of(stage, g, i)
            if not (isinstance(u, int) and u == 0):
                eng.wait_ge(s("bank_free%d" % (g % 8)), u)
            return psum[:, g % 8, :]

        def bank_full(eng, stage, g, i=0):
            eng.wait_ge(s("bank_full%d" % (g % 8)), use_of(stage, g, i) + 1)
            return psum[:, g % 8, :]

        def full(ins, g):
            ins.then_inc(s("bank_full%d" % (g % 8)), 1)

        def copied(eng, stage, g, i=0):
            eng.wait_ge(s("bank_free%d" % (g % 8)), use_of(stage, g, i) + 1)

        def free(ins, g):
            ins.then_inc(s("bank_free%d" % (g % 8)), 1)

        def chain(eng, name):
            at = {"base": 0, "n": 0}

            def link(ins):
                ins.then_inc(s(name), 1)
                at["n"] += 1
                eng.wait_ge(s(name), at["base"] + at["n"])

            def enter(base):
                done = at["n"]
                at["base"], at["n"] = base, 0
                return done

            return link, enter

        def tell(eng, ins, name, value):
            ins.then_inc(s(name), 1)
            eng.wait_ge(s(name), value)

        def expert_steps(eng, step):
            def block(lin, sl, j, par, start=False, end=False):
                for u in range(STEPS):
                    last = end and u == STEPS - 1
                    step(lin, sl, j, u, par, "first" if start and u == 0 else "end" if last else "")

            block(lambda k, c: c, lambda k, c: c, 0, 0, start=True)
            with eng.Fori(1, BLOCKS) as j:
                block(lambda k, c: j * k + c, lambda k, c: c, j, 0)
            with eng.Fori(0, SLICES // 2 - 1) as i:
                for n in (1, 2):
                    with eng.Fori(0, BLOCKS) as j:
                        block(lambda k, c: i * (2 * BLOCKS * k) + j * k + (n * BLOCKS * k + c),
                              lambda k, c: i * (2 * k) + (n * k + c), j, n % 2)
            m = BLOCKS * (SLICES - 1)
            with eng.Fori(0, BLOCKS - 1) as j:
                block(lambda k, c: j * k + (m * k + c), None, j, 1)
            block(lambda k, c: (m + BLOCKS - 1) * k + c, None, BLOCKS - 1, 1, end=True)

        def table(j0, n):
            d = ring[:, SLOT_OF[j0 + n // 2], :].rearrange("p (m c d) -> p m c d", m=2, c=2)
            return d[:, 0, n % 2, :], d[:, 1, n % 2, :]

        def both(items):
            for _parts in zip_longest(*items):
                pass

        def at_least(eng, name, value):
            if not isinstance(value, int) or value > 0:
                eng.wait_ge(s(name), value)

        def bc(ap, n):
            return ap.unsqueeze(2).to_broadcast([ap.shape[0], ap.shape[1], n])

        def head_bc(ap, n, k):
            return ap.unsqueeze(1).to_broadcast([ap.shape[0], k, n])

        def blocks(ap):
            return ap.rearrange("p (m c) -> p m c", m=PAIRS)

        def col(name, k=0):
            return cols[:, COLS[name] + k:COLS[name] + k + 1]

        @block.sync
        def _(sp):
            for ap, src in [(x[:, 0, :], io["x_prompt"][0]),
                            (x[:, 1:3, :], io["x_sample"][0].rearrange("(a p) d -> p a d", p=P)),
                            (cols[:], io["cols"]), (ident[:], io["consts"][:, 0:128]),
                            (headones[:], io["consts"][:, 128:256]), (stacked[:], io["consts"][:, 256:320]),
                            (scanmask, io["consts"][:, 320:704]), (iota[:], io["consts"][:, 704:832])]:
                sp.dma_start(ap, src).then_inc(s("inputs"), 16)

            def job_load(j, k, used):
                if used is not None:
                    sp.wait_ge(s("slot_used"), used)
                sp.dma_start(ring[:, k, :], io["stream"][j]).then_inc(s("landed%d" % k), 16)

            def load_plain(first, last):
                for j in sorted(set(range(first, last)) - set(SCRATCH)):
                    job_load(j, SLOT_OF[j], BEFORE[j] + 1 if BEFORE[j] >= 0 else None)
            load_plain(0, RING)
            m = SCRATCH[0] // RING
            n = JOB[("uv", 0)] // RING
            for first, last in ((1, m), (m + 1, n)):
                with sp.Fori(first, last) as i:
                    for k in range(RING):
                        job_load(i * RING + k, k, i * RING + (k - RING + 1))
                load_plain(last * RING, last * RING + RING if last == m else JOB[("uv", 0)])
            for l in range(2):
                first = JOB[("uv", l)]
                load_plain(first, first + UVRING)
                with sp.Fori(1, UVJOBS // UVRING) as i:
                    for k in range(UVRING):
                        job_load(i * UVRING + (first + k), k, i * UVRING + (first + k - UVRING + 1))
                load_plain(first + UVJOBS, JOB[("uv", 1)] if l == 0 else N_JOBS)

        @block.gpsimd
        def _(pool):
            bank_full(pool, "norm0", 5)
            for ap, src in [(masks, io["masks"]), (rows, io["rows"].to_broadcast([P, N_ROWS])),
                            (rope[:, 0], io["rope"][0].rearrange("(a p) f -> p a f", p=P)),
                            (rope[:, 1], io["rope"][1].rearrange("(a p) f -> p a f", p=P)),
                            (ckv[:, 1, :], io["cache_mla_ckv"][0, 0]), (kpe[:, 1, :], io["cache_mla_kpe"][0, 0]),
                            (s0[:, 0], io["state_rwkv_fwd"][0, 0].rearrange("h v k -> v h k")),
                            (s0[:, 1], io["state_rwkv_bwd"][0, 0].rearrange("h v k -> v h k"))]:
                pool.dma_start(ap, src).then_inc(s("mixer_params"), 16)
            pool.wait_ge(s("latents"), 1)
            pool.dma_start(io["o_ckv"][0, 0], ckv[:, 0, :]).then_inc(s("stored"), 16)
            pool.dma_start(io["o_kpe"][0, 0], kpe[:, 0, :]).then_inc(s("stored"), 16)

            def block_masks(stage, i):
                for lev, d in [(lev, d) for lev in range(1, 6) for d in range(2)]:
                    ex, NT, NTm, Tm, TT, Pm, KT, RkT, RbT, ktok, btok, Vt, Xt, SA = scan_mem[d]
                    if lev == 1:
                        copied(pool, stage, sg(d, 1), i)
                    else:
                        bank_full(pool, stage, sg(d, 8 + 3 * (lev - 2)), i)
                    m = masks[:, lev + 6 * d, :].unsqueeze(1).to_broadcast([P, PAIRS, P])
                    nc.gpsimd.tensor_tensor(blocks(NTm), blocks(NT), m, ALU.mult).then_inc(s("ntm_ready%d" % d), 1)
            with pool.Fori(0, 2) as i:
                block_masks("scanp", i)
            pool.wait_ge(s("state_copied"), 2)
            for d, name in enumerate(("o_fwd", "o_bwd")):
                pool.dma_start(io[name][0, 0].rearrange("h v k -> v h k"), s0[:, d]).then_inc(s("stored"), 16)
            with pool.Fori(0, 4) as i:
                block_masks("scans", i)
            pool.wait_ge(s("scan_done"), 1)
            for h in range(2):
                for m, name in enumerate(("lnx_g", "lnx_b")):
                    pool.dma_start(lnx[64 * h:64 * h + 64, m],
                                   io[name][h:h + 1].to_broadcast([64, PAIRS, CH])).then_inc(s("lnx_loaded"), 16)
            pool.wait_ge(s("y_done"), 1)
            pool.dma_start(io["o_prompt"][0], x[:, 0, :]).then_inc(s("stored"), 16)
            pool.dma_start(io["o_sample"][0].rearrange("(a p) d -> p a d", p=P), x[:, 1:3, :]).then_inc(s("stored"), 16)
            pool.wait_ge(s("stored"), 16 * 6)

        @block.tensor
        def _(pe):
            mm = nc.tensor.matmul

            def hand_back(ins, jobs=1):
                ins.then_inc(s("slot_used"), jobs)

            def adaln_jobs(l, stage, i):
                def row(n):
                    job = JOB[("mod", l)] + 4 * i + n
                    w = slot(job).rearrange("p (k n) -> p k n", k=KD)
                    landed(pe, job)
                    b = bank_free(pe, stage, n, i)
                    for k in range(KD):
                        ins = mm(b[0:2, :], condT[:, k, :], w[:, k, :], start=k == 0, stop=k == KD - 1)
                        if k == 0 and job > 0:
                            hand_back(ins)
                    full(ins, n)

                def columns(n):
                    copied(pe, stage, n, i)
                    b = bank_free(pe, stage, 4 + n, i)
                    for m in range(4):
                        ins = nc.tensor.transpose(b[:, 2 * m:2 * m + 2], modrow[0:2, n % 2, m * P:(m + 1) * P],
                                                  ident[0:2, 0:2])
                    full(ins, 4 + n)
                for n in range(4):
                    row(n)
                    if n > 0:
                        columns(n - 1)
                columns(3)

            def norm_transposes(stage):
                for t in range(TILES):
                    pe.wait_ge(s("normed"), NORM_NO[stage] * TILES + t + 1)
                    for h in range(2):
                        b = bank_free(pe, stage, 2 * t + h)
                        for k in range(4):
                            ins = nc.tensor.transpose(b[:, k * P:(k + 1) * P],
                                                      (xn, xn2)[t % 2][:, (4 * h + k) * P:(4 * h + k + 1) * P], ident[:])
                            if stage != "norm1" and t == 0 and h == 0 and k == 0:
                                hand_back(ins)
                        full(ins, 2 * t + h)

            def feature_product(stage, g, w, cols_, back=False):
                b = bank_free(pe, stage, g)
                for k in range(KD):
                    ins = mm(b[:, 0:T], w[:, k, cols_], hT[:, k, :], start=k == 0, stop=k == KD - 1)
                    if back and k == 0:
                        hand_back(ins)
                full(ins, g)

            def token_product(stage, g, w, n, t, back=False):
                b = bank_free(pe, stage, g)
                for k in range(KD):
                    ins = mm(b[:, 0:n], hT[:, k, t * P:(t + 1) * P], w[:, k, 0:n], start=k == 0, stop=k == KD - 1)
                    if back and k == 0:
                        hand_back(ins)
                full(ins, g)

            def out_product(l):
                for j in range(2):
                    job = JOB[("out", l)] + j
                    landed(pe, job)
                    w = slot(job).rearrange("p (k n) -> p k n", k=KD)
                    for t in range(TILES):
                        token_product("out%d" % l, 3 * j + t, w, 512, t, back=j == 1 and t == 0)

            def gate_rows(stage, l):
                pe.wait_ge(s("gate_cols"), GATE_NO[stage] + 1)
                for c in range(2):
                    for h in range(2):
                        g = GROUPS[stage][2 * c + h]
                        b = bank_free(pe, stage, g)
                        for k in range(4):
                            ins = mm(b[:, k * P:(k + 1) * P], gate_bc[:, 8 * c + 4 * h + k, :], ident[:],
                                     start=True, stop=True)
                            if (c, h, k) == (0, 0, 0) and (stage[-1] == "b" or stage == "gate1"):
                                hand_back(ins)
                        full(ins, g)

            pe.wait_ge(s("inputs"), 16 * 8)
            pe.wait_ge(s("cond_ready"), 1)
            for i in range(3):
                adaln_jobs(0, "mod0", i)
            norm_transposes("norm0")
            copied(pe, "norm0", 4)
            copied(pe, "norm0", 5)
            for j in range(4):
                job = JOB[("in", 0)] + j
                landed(pe, job)
                w = slot(job).rearrange("p (k n) -> p k n", k=KD)
                for m in range(4 if j < 3 else 2):
                    feature_product("in0", 4 * j + m, w, slice(m * P, (m + 1) * P), back=j > 0 and m == 0)
            job = JOB[("in", 0)] + 4
            landed(pe, job)
            for t in range(TILES):
                token_product("in0", 14 + t, slot(job).rearrange("p (k n) -> p k n", k=KD), 448, t, back=t == 0)

            small = slot(JOB[("small", 0)])
            q_up = small[:, 0:1536].rearrange("p (k n) -> p k n", k=2)
            kv_up = small[:, 1536:2560]
            w2a2 = small[:, 2560:3584].rearrange("p (d n) -> p d n", d=2)
            g2 = small[:, 3584:4096]
            pe.wait_ge(s("latents"), 1)
            for k in range(2):
                b = bank_free(pe, "qkvT", k)
                for t in range(TILES):
                    ins = nc.tensor.transpose(b[:, t * P:(t + 1) * P], qc[:, t, k * P:(k + 1) * P], ident[:])
                    if k == 0 and t == 0:
                        hand_back(ins)
                full(ins, k)
            b = bank_free(pe, "qkvT", 2)
            for t in range(KEYTILES):
                ins = nc.tensor.transpose(b[:, t * P:(t + 1) * P], ckv[:, t, :], ident[:])
            full(ins, 2)
            landed(pe, JOB[("small", 0)])
            for g in range(3):
                copied(pe, "qkvT", g)
            for t in range(TILES):
                for h in range(2):
                    b = bank_free(pe, "up", 2 * t + h)
                    for k in range(2):
                        ins = mm(b[:, 0:384], qcT[:, k, t * P:(t + 1) * P], q_up[:, k, 384 * h:384 * h + 384],
                                 start=k == 0, stop=k == 1)
                    full(ins, 2 * t + h)
            for t in range(KEYTILES):
                for h in range(2):
                    b = bank_free(pe, "up", 6 + 2 * t + h)
                    full(mm(b, ckvT[:, t * P:(t + 1) * P], kv_up[:, 512 * h:512 * h + 512], start=True, stop=True),
                         6 + 2 * t + h)
            pe.wait_ge(s("heads_ready"), 1)
            for h in range(MLA_HEADS):
                for part, (src, n) in enumerate(((q, TILES), (q, TILES), (kx, KEYTILES), (kx, KEYTILES))):
                    g = 4 * h + part
                    b = bank_free(pe, "headT", g)
                    for t in range(n):
                        if part % 2 == 0:
                            ins = nc.tensor.transpose(b[:, t * P:(t + 1) * P], src[:, t, h, 0:P], ident[:])
                        else:
                            ins = nc.tensor.transpose(b[0:64, t * P:(t + 1) * P], src[:, t, h, P:QK], ident[:])
                    full(ins, g)
            for h in range(MLA_HEADS):
                if h == 0:
                    for g in range(8, 16):
                        copied(pe, "headT", g)
                for t in range(TILES):
                    keys = slice(0, P) if t == 0 else slice(P, 4 * P)
                    n = keys.stop - keys.start
                    b = bank_free(pe, "att", t, h)
                    mm(b[:, 0:n], qTn[:, h, t * P:(t + 1) * P], kTn[:, h, keys], start=True, stop=False)
                    full(mm(b[:, 0:n], qTr[0:64, h, t * P:(t + 1) * P], kTr[0:64, h, keys], start=False, stop=True), t)
                pe.wait_ge(s("probs"), h + 1)
                b = bank_free(pe, "att", 3, h)
                for n in range(4):
                    ins = nc.tensor.transpose(b[:, n * P:(n + 1) * P], prob[:, n, :], ident[:])
                full(ins, 3)
                b = bank_free(pe, "att", 4, h)
                for n in range(3):
                    ins = nc.tensor.transpose(b[:, n * P:(n + 1) * P], prob[:, 4 + n, :], ident[:])
                full(ins, 4)
                copied(pe, "att", 3, h)
                copied(pe, "att", 4, h)
                b = bank_free(pe, "att", 5, h)
                mm(b[:, 0:P], vx[:, 0, h, :], probT[:, 0, :], start=True, stop=True)
                for t in range(1, 3):
                    for n in range(3):
                        ins = mm(b[:, t * P:(t + 1) * P], vx[:, 1 + n, h, :], probT[:, 3 * t - 2 + n, :],
                                 start=n == 0, stop=n == 2)
                full(ins, 5)

            pe.wait_ge(s("kk_squares"), 1)
            for m in range(PAIRS):
                b = bank_free(pe, "knorm", m)
                full(mm(b[:, 0:T], headones[:], ld[:, m, :], start=True, stop=True), m)
            pe.wait_ge(s("lora_in"), 3)
            for d in range(2):
                for part in range(2):
                    for m in range(PAIRS):
                        g = 8 * d + 4 * part + m
                        b = bank_free(pe, "lora", g)
                        full(mm(b[:, 0:T], w2a2[:, d, m * P:(m + 1) * P], lora_rhs[:, part, :],
                                start=True, stop=True), g)
            for m in range(PAIRS):
                b = bank_free(pe, "lora", 16 + m)
                full(mm(b[:, 0:T], g2[:, m * P:(m + 1) * P], gd, start=True, stop=True), 16 + m)
            pe.wait_ge(s("mixer_params"), 16 * 8)
            for d in range(2):
                for h in range(2):
                    b = bank_free(pe, "state_in", 2 * d + h)
                    for n in range(2):
                        m = 2 * h + n
                        ins = nc.tensor.transpose(b[:, n * 64:(n + 1) * 64],
                                                  s0[:, d, 2 * m:2 * m + 2, :].rearrange("v h k -> v (h k)"),
                                                  ident[0:64, 0:64])
                        if (d, h, n) == (0, 0, 0):
                            hand_back(ins)
                    full(ins, 2 * d + h)
            b = bank_free(pe, "coef", 0)
            for n in range(PAIRS * NCH):
                pe.wait_ge(s("bonus_exp"), n + 1)
                ins = mm(b[:, n:n + 1], bexp[:, n % 2, :], ones[:, 0:1], start=True, stop=True)
                if n < PAIRS * NCH - 1:
                    ins.then_inc(s("bonus_mm"), 1)
            full(ins, 0)

            def scan_item(stage, i, d, base):
                ex, NT, NTm, Tm, TT, Pm, KT, RkT, RbT, ktok, btok, Vt, Xt, SA = scan_mem[d]
                r_, a_, b_, k_, v_ = (ex[:, n] for n in range(5))
                S = ST[:, 0 if stage == "scanp" else 1, d]

                def pairs(g, lhsT, rhs, n=P):
                    b = bank_free(pe, stage, sg(d, g), i)
                    for m in range(PAIRS):
                        ins = mm(b[:, m * n:(m + 1) * n], lhsT(m), rhs(m), start=True, stop=True)
                    full(ins, sg(d, g))

                def sl(ap, n=P):
                    return lambda m: ap[:, m * n:(m + 1) * n]

                def pr(ap):
                    return lambda m: ap[:, m, :]
                pe.wait_ge(s("expanded%d" % d), i * 5 + (5 * base + 5))
                pairs(0, pr(a_), pr(b_))
                pairs(1, pr(b_), pr(a_))
                pairs(2, pr(k_), pr(a_))
                pairs(3, pr(k_), pr(r_))
                pairs(4, pr(b_), pr(r_))
                b = bank_free(pe, stage, sg(d, 5), i)
                for m in range(PAIRS):
                    ins = nc.tensor.transpose(b[:, m * P:(m + 1) * P], k_[:, m, :], ident[:])
                full(ins, sg(d, 5))
                b = bank_free(pe, stage, sg(d, 6), i)
                for m in range(PAIRS):
                    ins = nc.tensor.transpose(b[:, m * P:(m + 1) * P], b_[:, m, :], ident[:])
                full(ins, sg(d, 6))
                pairs(7, pr(v_), lambda m: stacked[:], CH)
                yield
                g = 8
                for lev in range(1, 6):
                    pe.wait_ge(s("ntm_ready%d" % d), i * 5 + (5 * base + lev))
                    pe.wait_ge(s("t_ready%d" % d), i * 6 + (6 * base + lev))
                    pairs(g, sl(NTm), sl(Tm))
                    yield
                    copied(pe, stage, sg(d, g), i)
                    if lev < 5:
                        pairs(g + 1, sl(TT), sl(Pm))
                        pairs(g + 2, sl(Pm), sl(TT))
                    else:
                        pairs(g + 1, sl(Pm), sl(TT))
                    g += 3
                    yield
                pe.wait_ge(s("state_ready%d" % d), i + (base + 1))
                if d == 1:
                    pe.wait_ge(s("state_scaled"), i + (base + 1))
                copied(pe, stage, sg(d, 7), i)
                copied(pe, stage, sg(d, 2), i)
                b = bank_free(pe, stage, sg(d, 22), i)
                for m in range(PAIRS):
                    o = b[:, m * CH:(m + 1) * CH]
                    mm(o, a_[:, m, :], S[:, m, :], start=True, stop=False)
                    ins = mm(o, KT[:, m * P:(m + 1) * P], Vt[:, m * CH:(m + 1) * CH], start=False, stop=True)
                full(ins, sg(d, 22))
                yield
                pe.wait_ge(s("t_ready%d" % d), i * 6 + (6 * base + 6))
                copied(pe, stage, sg(d, 22), i)
                pairs(23, sl(TT), sl(Xt, CH), CH)
                yield
                copied(pe, stage, sg(d, 23), i)
                for g in range(3, 7):
                    copied(pe, stage, sg(d, g), i)
                b = bank_free(pe, stage, sg(d, 24), i)
                for m in range(PAIRS):
                    o = b[:, m * CH:(m + 1) * CH]
                    mm(o, r_[:, m, :], S[:, m, :], start=True, stop=False)
                    mm(o, RkT[:, m * P:(m + 1) * P], Vt[:, m * CH:(m + 1) * CH], start=False, stop=False)
                    ins = mm(o, RbT[:, m * P:(m + 1) * P], SA[:, m * CH:(m + 1) * CH], start=False, stop=True)
                full(ins, sg(d, 24))
                b = bank_free(pe, stage, sg(d, 25), i)
                for m in range(PAIRS):
                    o = b[:, m * CH:(m + 1) * CH]
                    mm(o, ktok[:, m * P:(m + 1) * P], Vt[:, m * CH:(m + 1) * CH], start=True, stop=False)
                    ins = mm(o, btok[:, m * P:(m + 1) * P], SA[:, m * CH:(m + 1) * CH], start=False, stop=True)
                full(ins, sg(d, 25))

            for d in range(2):
                pe.wait_ge(s("state_ready%d" % d), 1)
            with pe.Fori(0, 2) as i:
                both(scan_item("scanp", i, d, 0) for d in range(2))
            for d in range(2):
                pe.wait_ge(s("state_ready%d" % d), 3)
                b = bank_free(pe, "state_out", d)
                for m in range(PAIRS):
                    ins = nc.tensor.transpose(b[0:64, m * P:(m + 1) * P], ST[:, 0, d, m, :], ident[:])
                full(ins, d)
            with pe.Fori(0, 4) as i:
                both(scan_item("scans", i, d, 2) for d in range(2))
            for part, name in enumerate(("vexp_ready", "yexp_ready")):
                for c in range(NCH):
                    pe.wait_ge(s(name), c + 1)
                    b = bank_free(pe, "yT", NCH * part + c)
                    for m in range(PAIRS):
                        ins = mm(b[:, m * CH:(m + 1) * CH], zexp[:, part, m, :], stacked[:], start=True, stop=True)
                        if (part, c, m) == (0, 0, 0):
                            hand_back(ins, len(SCRATCH))
                    full(ins, NCH * part + c)
            gate_rows("gate0", 0)
            for g in range(NCH, 2 * NCH):
                copied(pe, "yT", g)
            copied(pe, "att", 5, MLA_HEADS - 1)
            out_product(0)

            def peer(l):
                norm_transposes("norm%db" % l)
                copied(pe, "norm%db" % l, 4)
                copied(pe, "norm%db" % l, 5)
                pe.wait_ge(s("subkeys_in"), l + 1)
                for j in range(4):
                    job = JOB[("wq", l)] + j
                    landed(pe, job)
                    w = slot(job).rearrange("p (k n) -> p k n", k=KD)
                    for m in range(4):
                        feature_product("wk%d" % l, WQ[4 * j + m], w, slice(m * P, (m + 1) * P), back=m == 0)
                        if m == 0 and j > 0:
                            key_products(l, j - 1)
                key_products(l, 3)
                for t in range(TILES):
                    if l == 0:
                        adaln_jobs(1, "sel0", t)
                    pe.wait_ge(s("picked%d" % l), t + 1)
                    b = bank_free(pe, "sel%d" % l, SELG[l], t)
                    for n in range(3):
                        ins = nc.tensor.transpose(b[:, n * P:(n + 1) * P], pick[:, n, :], ident[:])
                        if n == 0 and t == (TILES - 1, 0)[l]:
                            hand_back(ins)
                    full(ins, SELG[l])
                for g in range(6):
                    bank_free(pe, "hot%d" % l, g)
                for g in (6, 7):
                    pe.wait_ge(s("bank_free%d" % g), FIRST["hot%d" % l][g])
                hot(l)

            def key_products(l, g):
                copied(pe, "wk%d" % l, WQ[4 * g + 2])
                copied(pe, "wk%d" % l, WQ[4 * g + 3])
                for t in range(TILES):
                    b = bank_free(pe, "wk%d" % l, KEYG[t][g])
                    for k in range(4):
                        side = 4 * g + k
                        ins = mm(b[:, k * P:(k + 1) * P], qT[:, side, t * P:(t + 1) * P], subkeys[:, side, :],
                                 start=True, stop=True)
                    full(ins, KEYG[t][g])

            def hot(l):
                j0 = JOB[("uv", l)]
                c0 = P * l
                g0 = SLICES * NG * l

                def group(g, par):
                    pe.wait_ge(s("onehots"), g + 1)
                    at_least(pe, "w_copied", g)
                    for t in range(BUILD):
                        ins = mm(psum[:, 7, 3 * SLICE * t:3 * SLICE * (t + 1)], ohA[:, par, :, t],
                                 ohB[:, par].rearrange("p m n t -> p (m n) t")[:, :, t], start=True, stop=True)
                    ins.then_inc(s("w_ready"), 1)

                def products(out, a, b, start, stop, used=False):
                    for n, (ka, kb) in enumerate(((0, 0), (0, 1), (1, 0))):
                        ins = mm(out, a[ka], b[kb], start=start and n == 0, stop=stop and n == 2,
                                 skip_group_check=True)
                        if used and n == 0:
                            ins.then_inc(s("slot_used"), 1)
                    return ins

                def v_tile(par, t, start=False, stop=False, used=False):
                    for h in range(2):
                        ins = products(psum[:, 2 * t + h, :], [gs[:, par, a, t * P:(t + 1) * P] for a in range(2)],
                                       [vs[:, par, b, 512 * h:512 * h + 512] for b in range(2)],
                                       start, stop, used and h == 0)
                        if stop:
                            full(ins, 2 * t + h)
                    return ins

                def v_waits(n):
                    pe.wait_ge(s("g_lo"), n + 1)
                    pe.wait_ge(s("v_lo"), n + 1)

                def step(lin, sl, j, u, par, where):
                    n = lin(STEPS, c0 + u)
                    g = lin(STEPS * PER_STEP, g0 + NG + PER_STEP * u)
                    build = sl is not None
                    pe.wait_ge(s("u_lo"), n + 1)
                    at_least(pe, "gelu_done", n)
                    for k in range(KD):
                        ins = products(psum[:, 6, 0:T], [us[:, u % 2, a, k * P:(k + 1) * P] for a in range(2)],
                                       [xs[:, b, k, :] for b in range(2)], k == 0, k == KD - 1)
                        if k == KD // 2 - 1 and build:
                            group(g, u % 2)
                    ins.then_inc(s("h_ready"), 1)
                    if where != "first":
                        v_waits(n - 1)
                    for t in range(TILES):
                        used = t == 1 and u % 2 == 1 and where != "end"
                        if used:
                            pe.wait_ge(s("v_lo"), n + 1)
                        if where != "first":
                            ins = v_tile((u + 1) % 2, t, start=isinstance(n, int) and n == c0 + 1, used=used)
                            if t == TILES - 1:
                                ins.then_inc(s("v_done"), 1)
                        if build and t != 1:
                            group(g + (1 if t == 0 else 2), (u + 1 + t // 2) % 2)

                def first_group(g, par):
                    pe.wait_ge(s("onehots"), g + 1)
                    at_least(pe, "w_copied", g - 1)
                    for t in range(BUILD):
                        for m in range(3):
                            ins = mm(psum[:, 6 + par, SLICE * t:SLICE * (t + 1)], ohA[:, par, :, t],
                                     ohB[:, par, m, :, t], start=m == 0, stop=m == 2)
                    ins.then_inc(s("w_ready"), 1)
                first_group(g0, 0)
                first_group(g0 + 1, 1)
                with pe.Fori(1, NG // 2) as i:
                    for par in range(2):
                        first_group(i * 2 + (g0 + par), par)
                pe.wait_ge(s("w_copied"), g0 + NG)
                pe.wait_ge(s("x_parts"), l + 1)
                expert_steps(pe, step)
                v_waits(c0 + P - 1)
                for t in range(TILES):
                    v_tile(1, t, stop=True)

            peer(0)
            gate_rows("gate0b", 0)

            norm_transposes("norm1")
            copied(pe, "norm1", 4)
            copied(pe, "norm1", 5)
            for j in range(6):
                job = JOB[("in", 1)] + j
                landed(pe, job)
                w = slot(job).rearrange("p (k n) -> p k n", k=KD)
                for m in range(4):
                    feature_product("in1", 4 * j + m, w, slice(m * P, (m + 1) * P), back=j > 0 and m == 0)
            job_f, job_d = JOB[("filter", 1)], JOB[("dft", 1)]
            fw = slot(job_f)
            w3, zpos, w1, w2 = fw[0:64, 0:2048], fw[0:33, 2048:2432], fw[0:33, 2432:2496], fw[0:64, 2496:2560]
            landed(pe, job_f)
            b = bank_free(pe, "hid", 0)
            full(mm(b[0:64, 0:T], w1, zpos, start=True, stop=True), 0)
            pe.wait_ge(s("hid_ready"), 1)
            b = bank_free(pe, "hid", 1)
            full(mm(b[0:64, 0:T], w2, hid[0:64, 0, :], start=True, stop=True), 1)
            pe.wait_ge(s("hid_ready"), 2)
            for t in range(TILES):
                for n in range(4):
                    b = bank_free(pe, "filt", 4 * t + n)
                    full(mm(b, hid[0:64, 1, t * P:(t + 1) * P], w3[:, 512 * n:512 * n + 512], start=True, stop=True),
                         4 * t + n)
            na = 0
            pe.wait_ge(s("abs_ready"), 12)
            for seq, tiles in ((0, (1, 2)), (1, (0,))):
                for h in range(2):
                    b = bank_free(pe, "norm_f", 2 * seq + h)
                    n = 2 * len(tiles)
                    for m in range(n):
                        ins = mm(b, ones[:], absf[:, na, :], start=m == 0, stop=m == n - 1)
                        na += 1
                    full(ins, 2 * seq + h)
            dft = slot(job_d)
            landed(pe, job_d)
            Fz = [dft[:, 0:1024].rearrange("p (a f) -> p a f", a=2), dft[:, 3072:3328].rearrange("p (a f) -> p a f", a=1)]
            Fb = [dft[:, 1024:2048].rearrange("p (a f) -> p a f", a=2), dft[:, 3328:3584].rearrange("p (a f) -> p a f", a=1)]
            Gi = [dft[:, 2048:3072].rearrange("p (a f) -> p a f", a=4), dft[:, 3584:3840].rearrange("p (a f) -> p a f", a=2)]
            SEQ = ((0, (1, 2), 0, 4), (1, (0,), 4, 2))

            def transform(stage, parts):
                for sq_, tiles, f0, nf in SEQ:
                    for f in range(nf):
                        for h in range(2):
                            g = 2 * (f0 + f) + h
                            b = bank_free(pe, stage, g)
                            todo = [(mat[sq_][:, a, f * P:(f + 1) * P], src(t, h)) for mat, src in parts
                                    for a, t in enumerate(tiles)]
                            for n, (lhsT, rhs) in enumerate(todo):
                                ins = mm(b, lhsT, rhs, start=n == 0, stop=n == len(todo) - 1)
                                if stage == "filtF" and g == 0 and n == 0:
                                    hand_back(ins, 2)
                            full(ins, g)
            transform("filtF", [(Fz, lambda t, h: filt[:, t, 512 * h:512 * h + 512]),
                                (Fb, lambda t, h: filt[:, t, D + 512 * h:D + 512 * h + 512])])
            pe.wait_ge(s("zin_ready"), KD)
            copied(pe, "filtF", 11)
            for t in range(TILES):
                for h in range(2):
                    b = bank_free(pe, "zT", 2 * t + h)
                    for k in range(4):
                        ins = nc.tensor.transpose(b[:, k * P:(k + 1) * P], zinT[:, 4 * h + k, t * P:(t + 1) * P], ident[:])
                    full(ins, 2 * t + h)
            for g in range(6):
                copied(pe, "zT", g)
            transform("zF", [(Fz, lambda t, h: z[:, t, 512 * h:512 * h + 512])])
            pe.wait_ge(s("spectra_ready"), 1)
            for k in range(KD):
                b = bank_free(pe, "conv", k)
                for sq_, tiles, f0, nf in SEQ:
                    n = len(tiles) * P
                    o = tiles[0] * P
                    for f in range(nf):
                        ins = mm(b[:, o:o + n], zF[:, f0 + f, k * P:(k + 1) * P], Gi[sq_][:, f, :],
                                 start=f == 0, stop=f == nf - 1)
                full(ins, k)
            gate_rows("gate1", 1)
            pe.wait_ge(s("conv_out"), KD)
            out_product(1)
            peer(1)
            gate_rows("gate1b", 1)

        @block.vector
        def _(dve):
            V = nc.vector
            L, enter = chain(dve, "dve_chain")
            normed = [0]
            x_new = [0]

            def rms(ss, n, count, eps=EPS):
                a = stat[:, ss:ss + n]
                V.tensor_scalar(a, a, 1.0 / count, eps, ALU.mult, ALU.add).then_inc(s("to_root"), 1)
                roots[0] += 1
                dve.wait_ge(s("rooted"), roots[0])
                L(V.reciprocal(a, a))
            roots = [0]

            def norm(stage, l, part):
                no = NORM_NO[stage]
                o = COLS["g"] + 8 * (2 * l + part)
                L(V.tensor_scalar(gsc[:], modc[:, l, 24 * part + 8:24 * part + 16, :], 1.0, None, ALU.add))
                tell(dve, V.tensor_tensor(gsc[:], gsc[:], bc(cols[:, o:o + 8], 2), ALU.mult), "gsc_ready", no + 1)
                dve.wait_ge(s("x_squares"), no + 1)
                rms(0, 3, D)
                for t in range(TILES):
                    if t == 2:
                        bank_full(dve, stage, 1)
                    tell(dve, V.tensor_scalar((xn, xn2)[t % 2], x[:, t, :], stat[:, t:t + 1], None, ALU.mult),
                              "normed", no * TILES + t + 1)

            def gate_columns(stage, l, part):
                for c in range(2):
                    ins = V.tensor_copy(gate_bc[:, 8 * c:8 * c + 8, :], bc(modc[:, l, 8 * part:8 * part + 8, c], P))
                    if c == 0:
                        L(ins)
                    else:
                        tell(dve, ins, "gate_cols", GATE_NO[stage] + 1)

            def add_out(stage, gate, order):
                for n in (1, 3):
                    copied(dve, gate, GROUPS[gate][n])
                for g, t, h in order:
                    b = bank_full(dve, stage, g)
                    c = 0 if t == 0 else 1
                    tmp = (xn, xn2)[g % 2][:, 0:512]
                    ins = V.tensor_tensor(tmp, b, gate_row[:, c, 512 * h:512 * h + 512], ALU.mult)
                    free(ins, g)
                    copied(dve, stage, g)
                    xs = x[:, t, 512 * h:512 * h + 512]
                    ins = V.tensor_tensor(xs, xs, tmp, ALU.add)
                    if g == 5:
                        x_new[0] += 1
                        tell(dve, ins, "x_new", x_new[0])
                    else:
                        L(ins)

            dve.wait_ge(s("inputs"), 16 * 8)
            L(V.memset(ones[:], 1.0))
            dve.wait_ge(s("cond_sig"), 1)
            cond = cols[:, COLS["cond"]:COLS["cond"] + 16].rearrange("p (k c) -> p k c", k=KD)
            tell(dve, V.tensor_tensor(condT[:], condT[:], cond, ALU.mult), "cond_ready", 1)
            L(V.tensor_copy(rep16.rearrange("p (n t) -> p n t", t=BUILD), bc(iota[:], BUILD)))
            for n in range(4, 8):
                copied(dve, "mod0", n, 2)
            norm("norm0", 0, 0)

            bank_full(dve, "norm0", 5)
            tell(dve, V.memset(pad, 0.0), "pad_zero", 1)
            mu = cols[:, COLS["mu"]:COLS["mu"] + 14]
            L(V.tensor_scalar(stat[:, 32:46], mu, 0.5, None, ALU.mult))
            L(V.tensor_scalar(stat[:, 46:60], mu, -1.0, 1.0, ALU.mult, ALU.add))
            for g in range(14):
                dst = rkv[:, g, :] if g < 12 else (wdad, gd)[g - 12]
                pd = pad[:, g % 2, :]
                dve.wait_ge(s("bank_free%d" % (g % 8)), use_of("in0", g) + 1)
                L(V.tensor_tensor(padt[:, 1:386], pd[:, 0:385], pd[:, 2:387], ALU.add))
                L(V.tensor_scalar(padt[:, 1:386], padt[:, 1:386], stat[:, 32 + g:33 + g], None, ALU.mult))
                om = stat[:, 46 + g:47 + g]
                L(V.scalar_tensor_tensor(dst[:, 0:P], pd[:, 1:129], om, padt[:, 1:129], ALU.mult, ALU.add))
                tell(dve, V.scalar_tensor_tensor(dst[:, P:T], pd[:, 130:386], om, padt[:, 130:386], ALU.mult, ALU.add),
                          "shifted", g + 1)

            dve.wait_ge(s("mixer_params"), 16 * 8)
            dve.wait_ge(s("latent_squares"), 1)
            L(V.tensor_scalar(stat[:, 3:6], stat[:, 3:6], 256.0 / 128.0, None, ALU.mult))
            rms(0, 6, 256)
            for t, kt in enumerate((0, 2, 3)):
                L(V.tensor_copy(kpe[:, kt, :], mla[:, t, 384:448]))
                L(V.scalar_tensor_tensor(ckv[:, kt, :], mla[:, t, 256:384], stat[:, 3 + t:4 + t], rows[:, 256:384],
                                         ALU.mult, ALU.mult))
                ins = V.scalar_tensor_tensor(qc[:, t, :], mla[:, t, 0:256], stat[:, t:t + 1], rows[:, 0:256],
                                             ALU.mult, ALU.mult)
                if t < 2:
                    L(ins)
            tell(dve, ins, "latents", 1)
            for t in range(KEYTILES):
                L(V.tensor_copy(kx[:, t, :, P:QK], head_bc(kpe[:, t, :], 64, MLA_HEADS)))
                for h in range(2):
                    g = 6 + 2 * t + h
                    b = bank_full(dve, "up", g).rearrange("p (h n) -> p h n", h=2)
                    L(V.tensor_copy(kx[:, t, 2 * h:2 * h + 2, 0:P], b[:, :, 0:P]))
                    free(V.tensor_copy(vx[:, t, 2 * h:2 * h + 2, :], b[:, :, P:2 * P]), g)
                    copied(dve, "up", g)
            for g in range(6):
                copied(dve, "up", g)
            for buf, n, o, row in ((q, 12, 6, "qn"), (kx, 16, 6, "kn")):
                a = buf.rearrange("p t h c -> p (t h) c")
                sv = sq[:, 0:n * QK].rearrange("p (r c) -> p r c", r=n)
                L(V.tensor_tensor(sv, a, a, ALU.mult))
                L(V.tensor_reduce(stat[:, o:o + n], sv, AX.X, ALU.add))
                rms(o, n, QK)
                L(V.tensor_tensor(a, a, bc(stat[:, o:o + n], QK), ALU.mult))
                r0 = ROWS[row][0]
                L(V.tensor_tensor(a, a, head_bc(rows[:, r0:r0 + QK], QK, n), ALU.mult))
            for n_, (buf, t0) in enumerate(((q, 1), (kx, 2))):
                x1, x2 = (buf[:, t0:t0 + 2, :, P + e:QK:2] for e in range(2))
                cs, sn = (rope[:, e].unsqueeze(2).to_broadcast([P, 2, MLA_HEADS, 32]) for e in range(2))
                for n, (a, w) in enumerate(((x1, cs), (x2, sn), (x1, sn), (x2, cs))):
                    L(V.tensor_tensor(rtmp[:, n], a, w, ALU.mult))
                L(V.tensor_tensor(x1, rtmp[:, 0], rtmp[:, 1], ALU.subtract))
                ins = V.tensor_tensor(x2, rtmp[:, 2], rtmp[:, 3], ALU.add)
                if n_ == 0:
                    L(ins)
            tell(dve, ins, "heads_ready", 1)
            for h in range(MLA_HEADS):
                for part in (2, 3):
                    g = 4 * h + part
                    b = bank_full(dve, "headT", g)
                    if part == 2:
                        free(V.tensor_copy(kTn[:, h, :], b), g)
                    else:
                        free(V.tensor_copy(kTr[0:64, h, :], b[0:64, :]), g)
            scale = float(QK) ** -0.5
            for h in range(MLA_HEADS):
                for t in range(TILES):
                    n = P if t == 0 else 3 * P
                    b = bank_full(dve, "att", t, h)
                    m = stat[:, 3 * h + t:3 * h + t + 1]
                    L(V.tensor_reduce(m, b[:, 0:n], AX.X, ALU.max, negate=True))
                    tell(dve, V.tensor_scalar(m, m, scale, None, ALU.mult), "row_max", 3 * h + t + 1)
                dve.wait_ge(s("exps"), 3 * h + 3)
                r = stat[:, 12 + 3 * h:15 + 3 * h]
                L(V.reciprocal(r, r))
                for t, (o, n) in enumerate(((0, 1), (1, 3), (4, 3))):
                    ins = V.tensor_scalar(prob[:, o:o + n, :], prob[:, o:o + n, :], r[:, t:t + 1], None, ALU.mult)
                    if t < 2:
                        L(ins)
                tell(dve, ins, "probs", h + 1)
                b = bank_full(dve, "att", 4, h)
                free(V.tensor_copy(probT[:, 4:7, :], b[:, 0:384].rearrange("p (n c) -> p n c", n=3)), 4)
                copied(dve, "att", 4, h)

            copied(dve, "att", 5, MLA_HEADS - 1)
            tell(dve, V.memset(lora_rhs, 0.0), "lora_zero", 1)
            for m in range(PAIRS):
                L(V.tensor_scalar(kk[:, m, :], rkv[:, 4 + m, :], col("k_k", m), None, ALU.mult))
            tell(dve, V.tensor_tensor(ld, kk, kk, ALU.mult), "kk_squares", 1)
            for m in range(PAIRS):
                copied(dve, "knorm", m)
            L(V.tensor_scalar(cum, cum, 1e-12, None, ALU.max))
            L(V.reciprocal(cum, cum))
            tell(dve, V.tensor_tensor(kk, kk, cum, ALU.mult), "kk_ready", 1)
            decay = -float(np.exp(np.float64(-0.5)))
            for d in range(2):
                for m in range(PAIRS):
                    copied(dve, "lora", 8 * d + m)
                    copied(dve, "lora", 8 * d + 4 + m)
                L(V.tensor_scalar(ld, ld, decay, None, ALU.mult))
                for m in range(PAIRS):
                    L(V.tensor_tensor_scan(cum[:, m, :], scanmask, ld[:, m, :], 0.0, ALU.mult, ALU.add))
                tell(dve, V.tensor_tensor(cumx, cum, ld, ALU.subtract), "cums", d + 1)
                dve.wait_ge(s("decays"), d + 1)
                tr, ta, tb, tk = (tilde[:, 4 * d + n] for n in range(4))
                L(V.tensor_tensor(tr, tr, rkv[:, 0:4, :], ALU.mult))
                L(V.scalar_tensor_tensor(ta, ta, -1.0, kk, ALU.mult, ALU.mult))
                L(V.tensor_copy(tk, tb))
                L(V.tensor_tensor(tb, tb, kk, ALU.mult))
                L(V.tensor_tensor(tb, tb, lr, ALU.mult))
                for m in range(PAIRS):
                    L(V.tensor_scalar(lr[:, m, :], lr[:, m, :], -1.0, col("k_a", m), ALU.add, ALU.mult))
                kd = cum
                L(V.scalar_tensor_tensor(kd, lr, 1.0, rkv[:, 4:8, :], ALU.add, ALU.mult))
                L(V.tensor_tensor(tk, tk, kd, ALU.mult))
                if d == 0:
                    tell(dve, V.tensor_copy(gateT, kd), "dir_done", 1)
                else:
                    L(V.tensor_tensor(gateT, gateT, kd, ALU.add))
            L(V.tensor_tensor(bonus_w, gateT, rkv[:, 0:4, :], ALU.mult))
            L(V.memset(bexp, 0.0))
            for m in range(PAIRS):
                ins = V.tensor_scalar(bonus_w[:, m, :], bonus_w[:, m, :], col("r_k", m), None, ALU.mult)
                if m < PAIRS - 1:
                    L(ins)
            tell(dve, ins, "gate_free", 1)
            L(V.memset(ST[:, 0], 0.0))
            for g in range(4):
                d, h = g // 2, g % 2
                b = bank_full(dve, "state_in", g)
                free(V.tensor_copy(ST[:, 1, d, 2 * h:2 * h + 2, :], b[:, 0:2 * CH].rearrange("p (m c) -> p m c", m=2)), g)
                copied(dve, "state_in", g)
            L(V.memset(y, 0.0))
            for d in range(2):
                tell(dve, V.memset(scan_mem[d][0], 0.0), "state_ready%d" % d, 1)
            for n in range(PAIRS * NCH):
                m, c = n // NCH, n % NCH
                if n >= 2:
                    dve.wait_ge(s("bonus_mm"), n - 1)
                L(V.tensor_copy(bexp[0:64, n % 2, 0:CH], bonus_w[0:64, m, c * CH:(c + 1) * CH]))
                tell(dve, V.tensor_copy(bexp[64:P, n % 2, CH:P], bonus_w[64:P, m, c * CH:(c + 1) * CH]), "bonus_exp", n + 1)
            b = bank_full(dve, "coef", 0)
            free(V.tensor_copy(coef[:].rearrange("p m c -> p (m c)"), b[:, 0:PAIRS * NCH]), 0)
            copied(dve, "coef", 0)

            def scan_item(stage, i, d, base, chunk, seq):
                ex, NT, NTm, Tm, TT, Pm, KT, RkT, RbT, ktok, btok, Vt, Xt, SA = scan_mem[d]
                S = ST[:, seq, d]
                c = chunk

                def expand(n):
                    src = tilde[:, 4 * d + n]
                    L(V.tensor_copy(ex[0:64, n, :, 0:CH], src[0:64, :, bass.ts(c, CH)]))
                    V.tensor_copy(ex[64:P, n, :, CH:P], src[64:P, :, bass.ts(c, CH)]).then_inc(s("expanded%d" % d), 1)
                el = elast[:, d, :, bass.ts(c, 1)].to_broadcast([P, PAIRS, CH])
                for n in range(3):
                    expand(n)
                yield
                dve.wait_ge(s("state_ready%d" % d), i + (base + 1))
                if d == 1:
                    V.tensor_tensor(S, S, el, ALU.mult).then_inc(s("state_scaled"), 1)
                    dve.wait_ge(s("state_scaled"), i + (base + 1))
                m0 = head_bc(masks[:, (6, 0)[d], :], P, PAIRS)
                m0T = head_bc(masks[:, (0, 6)[d], :], P, PAIRS)
                eye = head_bc(ident[:], P, PAIRS)
                b = bank_full(dve, stage, sg(d, 0), i)
                free(V.tensor_tensor(blocks(Tm), blocks(b), m0, ALU.mult), sg(d, 0))
                copied(dve, stage, sg(d, 1), i)
                L(V.tensor_tensor(blocks(TT), blocks(NT), m0T, ALU.mult))
                copied(dve, stage, sg(d, 0), i)
                L(V.tensor_tensor(blocks(Tm), blocks(Tm), eye, ALU.add))
                V.tensor_tensor(blocks(TT), blocks(TT), eye, ALU.add).then_inc(s("t_ready%d" % d), 1)
                for n, (dst, m) in enumerate(((KT, 12 + 2 * d), (RkT, 13 + 2 * d), (RbT, 13 + 2 * d))):
                    b = bank_full(dve, stage, sg(d, 2 + n), i)
                    free(V.tensor_tensor(blocks(dst), blocks(b), head_bc(masks[:, m, :], P, PAIRS), ALU.mult), sg(d, 2 + n))
                dve.wait_ge(s("t_ready%d" % d), i * 6 + (6 * base + 1))
                g = 9
                for lev in range(1, 6):
                    yield
                    if lev < 5:
                        b = bank_full(dve, stage, sg(d, g), i)
                        free(V.tensor_tensor(Tm, Tm, b, ALU.add), sg(d, g))
                        copied(dve, stage, sg(d, g), i)
                        g += 1
                    b = bank_full(dve, stage, sg(d, g), i)
                    free(V.tensor_tensor(TT, TT, b, ALU.add), sg(d, g))
                    copied(dve, stage, sg(d, g), i)
                    g += 2
                    V.tensor_copy(stat[:, 62:63], ones[:, 0:1]).then_inc(s("t_ready%d" % d), 1)
                    dve.wait_ge(s("t_ready%d" % d), i * 6 + (6 * base + lev + 1))
                yield
                b = bank_full(dve, stage, sg(d, 24), i)
                yv = y[:, bass.ts(c, 1)].rearrange("p o m v -> p (o m v)")
                free(V.tensor_tensor(yv, yv, b[:, 0:256], ALU.add), sg(d, 24))
                b = bank_full(dve, stage, sg(d, 25), i)
                Sf = S.rearrange("p m v -> p (m v)")
                copied(dve, stage, sg(d, 24), i)
                ins = V.tensor_tensor(Sf, Sf, b[:, 0:256], ALU.add)
                free(ins, sg(d, 25))
                copied(dve, stage, sg(d, 25), i)
                if d == 0:
                    ins = V.tensor_tensor(S, S, el, ALU.mult)
                else:
                    ins = V.tensor_copy(stat[:, 61:62], ones[:, 0:1])
                ins.then_inc(s("state_ready%d" % d), 1)

            c0, per = enter(0), 2 * (3 + 2)
            with dve.Fori(0, 2) as i:
                back = dve.snap(1 - i)
                enter(i * per + c0)
                both(scan_item("scanp", i, d, 0, (i, back)[d], 0) for d in range(2))
            with dve.Fori(0, 4) as i:
                back = dve.snap(5 - i)
                enter(i * per + (c0 + 2 * per))
                both(scan_item("scans", i, d, 2, (i + 2, back)[d], 1) for d in range(2))
            enter(c0 + 6 * per)

            bank_full(dve, "scans", sg(1, 25), 3)
            tell(dve, V.memset(zexp, 0.0), "scan_done", 1)
            yr = y.rearrange("p c m v -> p (c m) v")
            ycr, ysr = (a.rearrange("p c m v -> p (c m) v") for a in (yc, ysq))
            n = NCH * PAIRS
            mean, var = stat[:, 0:n], stat[:, n:2 * n]
            L(V.tensor_reduce(mean, yr, AX.X, ALU.add))
            L(V.tensor_scalar(mean, mean, 1.0 / CH, None, ALU.mult))
            L(V.tensor_tensor(ycr, yr, bc(mean, CH), ALU.subtract))
            L(V.tensor_tensor(ysr, ycr, ycr, ALU.mult))
            L(V.tensor_reduce(var, ysr, AX.X, ALU.add))
            rms(n, n, CH, LNX_EPS)
            L(V.tensor_tensor(ycr, ycr, bc(var, CH), ALU.mult))
            dve.wait_ge(s("lnx_loaded"), 16 * 4)
            for m, op in ((0, ALU.mult), (1, ALU.add)):
                L(V.tensor_tensor(yc, yc, lnx[:, m].unsqueeze(1).to_broadcast([P, NCH, PAIRS, CH]), op))

            def expand_z(part, src, c, name):
                if c > 0:
                    bank_full(dve, "yT", NCH * part + c - 1)
                L(V.tensor_copy(zexp[0:64, part, :, 0:CH], src(0)))
                tell(dve, V.tensor_copy(zexp[64:P, part, :, CH:P], src(1)), name, c + 1)
            for c in range(NCH):
                expand_z(0, lambda h, c=c: rkv[64 * h:64 * h + 64, 8:12, c * CH:(c + 1) * CH], c, "vexp_ready")
            for c in range(NCH):
                b = bank_full(dve, "yT", c)
                cf = coef[:, :, c:c + 1].to_broadcast([P, PAIRS, CH])
                free(V.tensor_tensor(vtok[:, c], b[:, 0:256].rearrange("p (m v) -> p m v", m=PAIRS), cf, ALU.mult), c)
                copied(dve, "yT", c)
                L(V.tensor_tensor(yc[:, c], yc[:, c], vtok[:, c], ALU.add))
            copied(dve, "lora", 19)
            for c in range(NCH):
                expand_z(1, lambda h, c=c: yc[64 * h:64 * h + 64, c], c, "yexp_ready")
                g = NCH + c
                b = bank_full(dve, "yT", g)
                free(V.tensor_tensor(hT[:, 0:4, c * CH:(c + 1) * CH], b[:, 0:256].rearrange("p (m v) -> p m v", m=PAIRS),
                                     gateT[:, :, c * CH:(c + 1) * CH], ALU.mult), g)
            gate_columns("gate0", 0, 2)
            add_out("out0", "gate0", [(3 * j + t, t, j) for j in range(2) for t in range(TILES)])

            def peer(l):
                norm("norm%db" % l, l, 1)
                for g, t in [(g, t) for g in range(4) for t in range(TILES)]:
                    copied(dve, "wk%d" % l, KEYG[t][g])
                    for a in range(4 * g, 4 * g + 4):
                        v, o, oi = sc[:, a, t, :], top[:, t, a, :], topi[:, t, a, :].bitcast(U32)
                        L(V.max(o[:, 0:8], v))
                        L(V.max_index(oi[:, 0:8], o[:, 0:8], v))
                        L(V.match_replace(v, o[:, 0:8], v, -3.0e38))
                        L(V.max(o[:, 8:16], v))
                        L(V.max_index(oi[:, 8:16], o[:, 8:16], v))
                for t in range(TILES):
                    L(V.tensor_copy(topif[:, t], topi[:, t].bitcast(U32)))
                    tv = top[:, t].rearrange("p (h e) k -> p h e k", e=2)
                    ti = topif[:, t].rearrange("p (h e) k -> p h e k", e=2)
                    c4 = cand.rearrange("p h (i j) -> p h i j", i=TOPK)
                    sh = [P, HEADS, TOPK, TOPK]
                    L(V.tensor_tensor(c4, tv[:, :, 0, :].unsqueeze(3).to_broadcast(sh),
                                      tv[:, :, 1, :].unsqueeze(2).to_broadcast(sh), ALU.add))
                    for h in range(HEADS):
                        v, o, oi = cand[:, h, :], tops[:, h, :], posu[:, h, :].bitcast(U32)
                        L(V.max(o[:, 0:8], v))
                        L(V.max_index(oi[:, 0:8], o[:, 0:8], v))
                        L(V.match_replace(v, o[:, 0:8], v, -3.0e38))
                        L(V.max(o[:, 8:16], v))
                        L(V.max_index(oi[:, 8:16], o[:, 8:16], v))
                    L(V.tensor_scalar(hi.bitcast(U32), posu.bitcast(U32), 4, None, ALU.logical_shift_right))
                    L(V.tensor_scalar(lo.bitcast(U32), posu.bitcast(U32), 15, None, ALU.bitwise_and))
                    if t > 0:
                        bank_full(dve, "sel%d" % l, SELG[l], t - 1)
                    for e, pos in enumerate((hi, lo)):
                        L(V.tensor_copy(pos, pos.bitcast(U32)))
                        ranks = iota[:, 0:TOPK].unsqueeze(1).unsqueeze(1).to_broadcast(sh)
                        L(V.tensor_tensor(oh, pos.unsqueeze(3).to_broadcast(sh), ranks, ALU.is_equal))
                        L(V.tensor_tensor(oh, oh, ti[:, :, e, :].unsqueeze(2).to_broadcast(sh), ALU.mult))
                        L(V.tensor_reduce(pick[:, e, :], oh.rearrange("p h k m -> p (h k) m"), AX.X, ALU.add))
                    gt = pick[:, 2, :].rearrange("p (h k) -> p h k", h=HEADS)
                    tell(dve, V.tensor_tensor(gt, tops, tops[:, :, 0:1].to_broadcast([P, HEADS, TOPK]), ALU.subtract),
                              "shifted_tops", 3 * l + t + 1)
                    dve.wait_ge(s("tops_exp"), 3 * l + t + 1)
                    L(V.tensor_reduce(stat[:, 0:8], gt, AX.X, ALU.add))
                    L(V.reciprocal(stat[:, 0:8], stat[:, 0:8]))
                    tell(dve, V.tensor_tensor(gt, gt, bc(stat[:, 0:8], TOPK), ALU.mult), "picked%d" % l, t + 1)
                for t in range(TILES):
                    copied(dve, "sel%d" % l, SELG[l], t)
                L(V.tensor_copy(sel16[:, 0:2, :], sel[:, 0:2, :]))
                rest = sel[:, 2, :]
                for n in range(2, 5):
                    L(V.tensor_copy(sel16[:, n, :], rest))
                    if n < 4:
                        L(V.tensor_tensor(sel[:, 0, :], rest, sel16[:, n, :], ALU.subtract))
                        rest = sel[:, 0, :]
                j0 = JOB[("uv", l)]
                c0 = P * l
                g0 = SLICES * NG * l
                dve.wait_ge(s("x_hi"), l + 1)
                tell(dve, V.tensor_tensor(xs[:, 1], hT[:], xs[:, 0].bitcast(F32), ALU.subtract), "x_parts", l + 1)

                def onehots(g, tok, first, par):
                    at_least(dve, "w_ready", g - 1)
                    sh = [P, P, BUILD]
                    V.tensor_tensor(ohA[:, par], rep16.rearrange("p (n t) -> p n t", t=BUILD),
                                    sel16[:, 0, bass.ds(tok, BUILD)].unsqueeze(1).to_broadcast(sh), ALU.is_equal)
                    sh = [P, SLICE, BUILD]
                    at_least(dve, "onehots", g)
                    tell(dve, V.tensor_tensor(ohE[:], rep16[:, bass.ds(first, SLICE * BUILD)].rearrange(
                        "p (n t) -> p n t", t=BUILD), sel16[:, 1, bass.ds(tok, BUILD)].unsqueeze(1).to_broadcast(sh),
                        ALU.is_equal), "onehot_i2", g + 1)
                    sh = [P, 3, SLICE, BUILD]
                    V.tensor_tensor(ohB[:, par], ohE[:].unsqueeze(1).to_broadcast(sh),
                                    sel16[:, 2:5, bass.ds(tok, BUILD)].unsqueeze(2).to_broadcast(sh),
                                    ALU.mult).then_inc(s("onehots"), 1)

                def dense(g, tok, par):
                    dve.wait_ge(s("w_ready"), g + 1)
                    V.tensor_reduce(wd[:, par, bass.ds(tok, BUILD), :], psum[:, 7, 0:3 * SLICE * BUILD].rearrange(
                        "p (t m n) -> p t n m", t=BUILD, m=3), AX.X, ALU.add).then_inc(s("w_copied"), 1)

                def step(lin, sl, j, u, par, where):
                    n = lin(STEPS, c0 + u)
                    g = lin(STEPS * PER_STEP, g0 + NG + PER_STEP * u)
                    tok = j * (STEPS * PER_STEP * BUILD) + PER_STEP * BUILD * u
                    build = sl is not None
                    if build:
                        first = sl(SLICE * BUILD, SLICE * BUILD)
                        for k in range(2):
                            onehots(g + k, tok + BUILD * k, first, (u + k) % 2)
                    v = table(j0, u)[1]
                    dve.wait_ge(s("v_hi"), n + 1)
                    V.tensor_tensor(vs[:, u % 2, 1, :], v, vs[:, u % 2, 0, :].bitcast(F32),
                                    ALU.subtract).then_inc(s("v_lo"), 1)
                    if build:
                        at_least(dve, "g_made", n)
                        dense(g, tok, 1 - par)
                    if where != "end":
                        u_part(u + 1, n + 1)
                    dve.wait_ge(s("gelu_done"), n + 1)
                    dve.wait_ge(s("w_copied"), sl(NG, g0 + NG) if build else g0 + SLICES * NG)
                    at_least(dve, "g_lo", n - 1)
                    V.tensor_tensor(gw[:, u % 2, :], gel[:, u % 2, :],
                                    wd[:, par, :, bass.ds(j * STEPS + u, 1)].rearrange("p t o -> p (t o)"),
                                    ALU.mult).then_inc(s("g_made"), 1)
                    if build:
                        onehots(g + 2, tok + 2 * BUILD, first, u % 2)
                    dve.wait_ge(s("g_hi"), n + 1)
                    V.tensor_tensor(gs[:, u % 2, 1, :], gw[:, u % 2, :], gs[:, u % 2, 0, :].bitcast(F32),
                                    ALU.subtract).then_inc(s("g_lo"), 1)
                    if build:
                        for k in (1, 2):
                            dense(g + k, tok + BUILD * k, 1 - par)

                def u_part(u, n):
                    dve.wait_ge(s("u_hi"), n + 1)
                    V.tensor_tensor(us[:, u % 2, 1, :], table(j0, u)[0], us[:, u % 2, 0, :].bitcast(F32),
                                    ALU.subtract).then_inc(s("u_lo"), 1)

                onehots(g0, 0, 0, 0)
                onehots(g0 + 1, BUILD, 0, 1)
                with dve.Fori(1, NG // 2) as i:
                    for k in range(2):
                        onehots(i * 2 + (g0 + k), i * (2 * BUILD) + k * BUILD, 0, k)
                u_part(0, c0)
                expert_steps(dve, step)
                dve.wait_ge(s("g_lo"), P * (l + 1))
                gate_columns("gate%db" % l, l, 5)
                add_out("hot%d" % l, "gate%db" % l, [(2 * t + h, t, h) for t in range(TILES) for h in range(2)])

            bank_full(dve, "out0", 5)
            peer(0)

            norm("norm1", 1, 0)
            bank_full(dve, "norm1", 5)
            tell(dve, V.memset(pad1, 0.0), "pad_zero", 2)
            for g in range(24):
                pd = pad1[:, g % 2, :]
                dve.wait_ge(s("bank_free%d" % (g % 8)), use_of("in1", g) + 1)
                k = g % 8
                dst = (x0T[:, k, :], zinT[:, k, :], vtmp)[g // 8]
                L(V.tensor_scalar(padt1[:, 1:386], pd[:, 0:385], col("conv_w", g), col("conv_b", g), ALU.mult, ALU.add))
                L(V.scalar_tensor_tensor(padt1[:, 1:386], pd[:, 1:386], col("conv_w", 24 + g), padt1[:, 1:386],
                                         ALU.mult, ALU.add))
                for (a, b_), o in (((1, 129), 0), ((130, 386), P)):
                    ins = V.scalar_tensor_tensor(dst[:, o:o + b_ - a], pd[:, a + 1:b_ + 1], col("conv_w", 48 + g),
                                                 padt1[:, a:b_], ALU.mult, ALU.add)
                    if o == 0:
                        L(ins)
                tell(dve, ins, "shifted", 14 + g + 1)
                if g >= 16:
                    tell(dve, V.tensor_tensor(zinT[:, k, :], zinT[:, k, :], vtmp, ALU.mult), "zin_ready", k + 1)
            V.tensor_copy(stat[:, 62:63], ones[:, 0:1]).then_inc(s("slot_used"), 1)
            dve.wait_ge(s("slot_used"), JOB[("in", 1)] + 6)

            magic, two_pi = 12582912.0, 2 * np.pi
            c1 = float(np.float32(6.28125))
            c2 = float(np.float32(round((two_pi - c1) * 2 ** 20) / 2 ** 20))
            c3 = float(np.float32(two_pi - c1 - c2))
            for n in range(2):
                b = bank_full(dve, "hid", n)
                a, k_ = htmp[0:64, 0, :], htmp[0:64, 1, :]
                free(V.tensor_scalar(a, b[0:64, 0:T], col("f_b1" if n == 0 else "f_b2")[0:64], col("freq")[0:64],
                                     ALU.add, ALU.mult), n)
                copied(dve, "hid", n)
                L(V.tensor_scalar(k_, a, float(1 / two_pi), magic, ALU.mult, ALU.add))
                L(V.tensor_scalar(k_, k_, -magic, None, ALU.add))
                for c in (c1, c2, c3):
                    L(V.scalar_tensor_tensor(a, k_, -c, a, ALU.mult, ALU.add))
                tell(dve, V.tensor_scalar(a, a, 3.1415925, -3.1415925, ALU.min, ALU.max), "sin_in", n + 1)
            job_w = JOB[("window", 1)]
            landed(dve, job_w)
            win = slot(job_w)[:, 0:3072].rearrange("p (t c) -> p t c", t=3)
            for t in range(TILES):
                for n in range(4):
                    g = 4 * t + n
                    b = bank_full(dve, "filt", g)
                    h = n % 2
                    free(V.tensor_tensor(filt[:, t, 512 * n:512 * n + 512], b, win[:, t, 512 * h:512 * h + 512],
                                         ALU.mult), g)
                    copied(dve, "filt", g)
            L(V.memset(filt[0:1, 0, D:2 * D], 0.0))
            tell(dve, V.memset(filt[0:1, 1, D:2 * D], 0.0), "filters", 1)
            for g in range(4):
                b = bank_full(dve, "norm_f", g)
                free(V.reciprocal(rnorm[:, g // 2, 512 * (g % 2):512 * (g % 2) + 512], b), g)
                copied(dve, "norm_f", g)
            for g in range(12):
                f, h = g // 2, g % 2
                b = bank_full(dve, "filtF", g)
                seq = 0 if f < 4 else 1
                free(V.tensor_tensor(filtF[:, f, 512 * h:512 * h + 512], b, rnorm[:, seq, 512 * h:512 * h + 512],
                                     ALU.mult), g)
                copied(dve, "filtF", g)
            for g in range(12):
                copied(dve, "zF", g)
            for n, (re, im, special) in enumerate(((0, 2, True), (1, 3, False), (4, 5, True))):
                zr, zi, hr, hi_ = zF[:, re], zF[:, im], filtF[:, re], filtF[:, im]
                p0, p1 = prod[:, 0], prod[:, 1]
                L(V.tensor_tensor(p0, zr, hr, ALU.mult))
                L(V.tensor_tensor(p1, zi, hi_, ALU.mult))
                L(V.tensor_tensor(zr, zr, hi_, ALU.mult))
                L(V.tensor_tensor(zi, zi, hr, ALU.mult))
                L(V.tensor_tensor(zi, zi, zr, ALU.add))
                L(V.tensor_tensor(zr, p0, p1, ALU.subtract))
                if special:
                    L(V.tensor_copy(zr[0:1, :], p0[0:1, :]))
                    ins = V.tensor_copy(zi[0:1, :], p1[0:1, :])
                    if n < 2:
                        L(ins)
            tell(dve, ins, "spectra_ready", 1)
            for k in range(KD):
                b = bank_full(dve, "conv", k)
                free(V.scalar_tensor_tensor(zinT[:, k, :], zinT[:, k, :], col("bias", k), b[:, 0:T], ALU.mult, ALU.add), k)
                copied(dve, "conv", k)
                tell(dve, V.tensor_tensor(hT[:, k, :], zinT[:, k, :], x0T[:, k, :], ALU.mult), "conv_out", k + 1)
            gate_columns("gate1", 1, 2)
            add_out("out1", "gate1", [(3 * j + t, t, j) for j in range(2) for t in range(TILES)])
            bank_full(dve, "out1", 5)
            peer(1)
            V.tensor_copy(stat[:, 62:63], ones[:, 0:1]).then_inc(s("y_done"), 1)

        @block.scalar
        def _(act):
            A = nc.scalar.activation
            L, enter = chain(act, "act_chain")
            roots = [0]

            def root(ss, n):
                roots[0] += 1
                act.wait_ge(s("to_root"), roots[0])
                A(stat[:, ss:ss + n], stat[:, ss:ss + n], ACT.Sqrt).then_inc(s("rooted"), 1)

            def norm(stage, l, part):
                no = NORM_NO[stage]
                if no > 0:
                    act.wait_ge(s("x_new"), no)
                for t in range(TILES):
                    ins = A(junk, x[:, t, :], ACT.Square, accum_out=stat[:, t:t + 1])
                    if t < 2:
                        L(ins)
                tell(act, ins, "x_squares", no + 1)
                root(0, 3)
                act.wait_ge(s("gsc_ready"), no + 1)
                for t in range(TILES):
                    c = 0 if t == 0 else 1
                    for h in range(2):
                        b = bank_full(act, stage, 2 * t + h)
                        for j in range(4):
                            k = 4 * h + j
                            ins = A(hT[:, k, t * P:(t + 1) * P], b[:, j * P:(j + 1) * P], ACT.Identity,
                                    bias=modc[:, l, 24 * part + k, c:c + 1], scale=gsc[:, k, c:c + 1])
                        free(ins, 2 * t + h)

            def adaln_jobs(l, stage, i):
                def row(n):
                    if n > 1:
                        bank_full(act, stage, 2 + n, i)
                    b = bank_full(act, stage, n, i)
                    free(A(modrow[0:2, n % 2, :], b[0:2, :], ACT.Copy), n)

                def columns(n):
                    b = bank_full(act, stage, 4 + n, i)
                    for m in range(4):
                        j = 16 * i + 4 * n + m
                        ins = A(modc[:, l, j, :], b[:, 2 * m:2 * m + 2], ACT.Identity, bias=col("b_mod", 48 * l + j))
                    free(ins, 4 + n)
                for n in range(4):
                    row(n)
                    if n > 0:
                        columns(n - 1)
                columns(3)

            def gate_rows(stage):
                for c in range(2):
                    for h in range(2):
                        g = GROUPS[stage][2 * c + h]
                        b = bank_full(act, stage, g)
                        free(A(gate_row[:, c, 512 * h:512 * h + 512], b, ACT.Copy), g)

            act.wait_ge(s("inputs"), 16 * 8)
            cond = cols[:, COLS["cond"]:COLS["cond"] + 16].rearrange("p (k c) -> p k c", k=KD)
            A(condT[:], cond, ACT.Sigmoid).then_inc(s("cond_sig"), 1)
            for i in range(3):
                if i > 0:
                    bank_full(act, "mod0", 7, i - 1)
                adaln_jobs(0, "mod0", i)
            norm("norm0", 0, 0)
            act.wait_ge(s("pad_zero"), 1)
            for g in range(14):
                if g >= 2:
                    act.wait_ge(s("shifted"), g - 1)
                b = bank_full(act, "in0", g)
                L(A(pad[:, g % 2, 1:129], b[:, 0:P], ACT.Copy))
                free(A(pad[:, g % 2, 130:386], b[:, P:T], ACT.Copy), g)
            for t in range(TILES):
                b = bank_full(act, "in0", 14 + t)
                free(A(mla[:, t, :], b[:, 0:448], ACT.Copy), 14 + t)
            for t in range(TILES):
                copied(act, "in0", 14 + t)
            act.wait_ge(s("shifted"), 14)
            for t in range(TILES):
                L(A(padt[:, 0:256], mla[:, t, 0:256], ACT.Square, accum_out=stat[:, t:t + 1]))
                ins = A(padt[:, 0:128], mla[:, t, 256:384], ACT.Square, accum_out=stat[:, 3 + t:4 + t])
                if t < 2:
                    L(ins)
            tell(act, ins, "latent_squares", 1)
            root(0, 6)
            for g in range(3):
                b = bank_full(act, "qkvT", g)
                if g < 2:
                    free(A(qcT[:, g, :], b[:, 0:T], ACT.Copy), g)
                else:
                    free(A(ckvT, b, ACT.Copy), g)
            for t in range(TILES):
                for h in range(2):
                    b = bank_full(act, "up", 2 * t + h)
                    free(A(q[:, t, 2 * h:2 * h + 2, :], b[:, 0:384].rearrange("p (h c) -> p h c", h=2), ACT.Copy), 2 * t + h)
            root(6, 12)
            root(6, 16)
            for h in range(MLA_HEADS):
                b = bank_full(act, "headT", 4 * h)
                free(A(qTn[:, h, :], b[:, 0:T], ACT.Copy), 4 * h)
                b = bank_full(act, "headT", 4 * h + 1)
                free(A(qTr[0:64, h, :], b[0:64, 0:T], ACT.Copy), 4 * h + 1)
            scale = float(QK) ** -0.5
            for h in range(MLA_HEADS):
                if h > 0:
                    bank_full(act, "att", 4, h - 1)
                for t, (o, n) in enumerate(((0, 1), (1, 3), (4, 3))):
                    act.wait_ge(s("row_max"), 3 * h + t + 1)
                    b = bank_full(act, "att", t, h)
                    ins = A(prob[:, o:o + n, :], b[:, 0:n * P].rearrange("p (n c) -> p n c", n=n), ACT.Exp,
                            bias=stat[:, 3 * h + t:3 * h + t + 1], scale=scale,
                            accum_out=stat[:, 12 + 3 * h + t:13 + 3 * h + t])
                    free(ins, t)
                    copied(act, "att", t, h)
                    A(stat[:, 60:61], ones[:, 0:1], ACT.Copy).then_inc(s("exps"), 1)
                    act.wait_ge(s("exps"), 3 * h + t + 1)
                b = bank_full(act, "att", 3, h)
                free(A(probT[:, 0:4, :], blocks(b), ACT.Copy), 3)
                b = bank_full(act, "att", 5, h)
                free(A(hT[:, 4 + h, :], b[:, 0:T], ACT.Copy), 5)
            act.wait_ge(s("lora_zero"), 1)
            A(lora_rhs[0:64, 0, :], wdad[0:64, :], ACT.Tanh).then_inc(s("lora_in"), 1)
            A(lora_rhs[64:P, 1, :], wdad[64:P, :], ACT.Copy).then_inc(s("lora_in"), 1)
            A(gd, gd, ACT.Sigmoid).then_inc(s("lora_in"), 1)
            for m in range(PAIRS):
                b = bank_full(act, "knorm", m)
                free(A(cum[:, m, :], b[:, 0:T], ACT.Sqrt), m)
            for d in range(2):
                if d == 0:
                    act.wait_ge(s("kk_ready"), 1)
                else:
                    act.wait_ge(s("dir_done"), 1)
                for part, (dst, name) in enumerate(((ld, "w0"), (lr, "a0"))):
                    for m in range(PAIRS):
                        g = 8 * d + 4 * part + m
                        b = bank_full(act, "lora", g)
                        free(A(dst[:, m, :], b[:, 0:T], ACT.Sigmoid, bias=col(name, 4 * d + m)), g)
                act.wait_ge(s("cums"), d + 1)
                if d == 0:
                    act.wait_ge(s("stored"), 16 * 2)
                L(A(elast[:, d], cum[:, :, CH - 1:T:CH], ACT.Exp))
                tr, ta, tb = (tilde[:, 4 * d + n] for n in range(3))
                for n, (dst, src, sign) in enumerate((((tr, cum, 1.0), (ta, cumx, 1.0), (tb, cum, -1.0)),
                                                      ((tr, cumx, -1.0), (ta, cum, -1.0), (tb, cumx, 1.0)))[d]):
                    ins = A(dst, src, ACT.Exp, scale=sign)
                    if n < 2:
                        L(ins)
                tell(act, ins, "decays", d + 1)
            act.wait_ge(s("gate_free"), 1)
            for m in range(PAIRS):
                b = bank_full(act, "lora", 16 + m)
                free(A(gateT[:, m, :], b[:, 0:T], ACT.Copy), 16 + m)

            def scan_item(stage, i, d, base, chunk):
                ex, NT, NTm, Tm, TT, Pm, KT, RkT, RbT, ktok, btok, Vt, Xt, SA = scan_mem[d]
                for n, src in ((3, tilde[:, 4 * d + 3]), (4, rkv[:, 8:12, :])):
                    L(A(ex[0:64, n, :, 0:CH], src[0:64, :, bass.ts(chunk, CH)], ACT.Copy))
                    A(ex[64:P, n, :, CH:P], src[64:P, :, bass.ts(chunk, CH)], ACT.Copy).then_inc(s("expanded%d" % d), 1)
                yield
                for g, dst in ((1, NT), (5, ktok), (6, btok), (7, Vt)):
                    b = bank_full(act, stage, sg(d, g), i)
                    free(A(dst, b[:, 0:dst.shape[1]], ACT.Copy), sg(d, g))
                g = 8
                for lev in range(1, 6):
                    yield
                    b = bank_full(act, stage, sg(d, g), i)
                    free(A(Pm, b, ACT.Copy), sg(d, g))
                    g += 3
                for g, dst in ((22, Xt), (23, SA)):
                    yield
                    b = bank_full(act, stage, sg(d, g), i)
                    free(A(dst, b[:, 0:256], ACT.Copy), sg(d, g))

            for d in range(2):
                act.wait_ge(s("state_ready%d" % d), 1)
            c0, per = enter(0), 4
            with act.Fori(0, 2) as i:
                back = act.snap(1 - i)
                enter(i * per + c0)
                both(scan_item("scanp", i, d, 0, (i, back)[d]) for d in range(2))
            for d in range(2):
                b = bank_full(act, "state_out", d)
                free(A(s0[:, d].rearrange("v h k -> v (h k)"), b[0:64, :], ACT.Copy), d)
                copied(act, "state_out", d)
                A(stat[:, 60:61], ones[:, 0:1], ACT.Copy).then_inc(s("state_copied"), 1)
                act.wait_ge(s("state_copied"), d + 1)
            with act.Fori(0, 4) as i:
                back = act.snap(5 - i)
                enter(i * per + (c0 + 2 * per))
                both(scan_item("scans", i, d, 2, (i + 2, back)[d]) for d in range(2))
            enter(c0 + 6 * per)
            root(24, 24)
            gate_rows("gate0")

            def peer(l):
                norm("norm%db" % l, l, 1)
                landed(act, JOB[("keys", l)])
                A(subkeys.rearrange("p a n -> p (a n)"), slot(JOB[("keys", l)])[:, 0:2048],
                  ACT.Copy).then_inc(s("subkeys_in"), 1)

                def scores(g):
                    for t in range(TILES):
                        b = bank_full(act, "wk%d" % l, KEYG[t][g])
                        free(A(sc[:, 4 * g:4 * g + 4, t, :], blocks(b), ACT.Copy), KEYG[t][g])
                for g in range(16):
                    b = bank_full(act, "wk%d" % l, WQ[g])
                    free(A(qT[:, g, :], b[:, 0:T], ACT.Copy), WQ[g])
                    if g > 0 and g % 4 == 0:
                        scores(g // 4 - 1)
                scores(3)
                for t in range(TILES):
                    if l == 0:
                        adaln_jobs(1, "sel0", t)
                    act.wait_ge(s("shifted_tops"), 3 * l + t + 1)
                    A(pick[:, 2, :], pick[:, 2, :], ACT.Exp).then_inc(s("tops_exp"), 1)
                    b = bank_full(act, "sel%d" % l, SELG[l], t)
                    free(A(sel[:, 0:3, t * P:(t + 1) * P], b[:, 0:384].rearrange("p (n c) -> p n c", n=3), ACT.Copy),
                         SELG[l])
                j0 = JOB[("uv", l)]
                c0 = P * l
                A(xs[:, 0], hT[:], ACT.Copy).then_inc(s("x_hi"), 1)

                def u_part(u):
                    A(us[:, u % 2, 0, :], table(j0, u)[0], ACT.Copy).then_inc(s("u_hi"), 1)

                def step(lin, sl, j, u, par, where):
                    n = lin(STEPS, c0 + u)
                    if where != "end":
                        if u % 2 == 1:
                            job = j0 + (u + 1) // 2
                            act.wait_ge(s("landed%d" % SLOT_OF[job]), lin(16, 16 * LANDING[job]))
                        at_least(act, "h_ready", n)
                        u_part(u + 1)
                    at_least(act, "v_done", lin(STEPS, (P - 1) * l + u - 1))
                    A(vs[:, u % 2, 0, :], table(j0, u)[1], ACT.Copy).then_inc(s("v_hi"), 1)
                    act.wait_ge(s("h_ready"), n + 1)
                    at_least(act, "g_made", n - 1)
                    A(gel[:, u % 2, :], psum[:, 6, 0:T], ACT.Gelu_apprx_tanh).then_inc(s("gelu_done"), 1)
                    act.wait_ge(s("g_made"), n + 1)
                    A(gs[:, u % 2, 0, :], gw[:, u % 2, :], ACT.Copy).then_inc(s("g_hi"), 1)
                landed(act, j0)
                u_part(0)

                def first_dense(g, tok, par):
                    act.wait_ge(s("w_ready"), g + 1)
                    A(wd[:, 0, bass.ds(tok, BUILD), :], psum[:, 6 + par, 0:SLICE * BUILD].rearrange(
                        "p (t n) -> p t n", t=BUILD), ACT.Copy).then_inc(s("w_copied"), 1)
                with act.Fori(0, NG // 2) as i:
                    for par in range(2):
                        first_dense(i * 2 + (SLICES * NG * l + par), i * (2 * BUILD) + par * BUILD, par)
                expert_steps(act, step)
                gate_rows("gate%db" % l)
            peer(0)

            norm("norm1", 1, 0)
            act.wait_ge(s("pad_zero"), 2)
            for g in range(24):
                if g >= 2:
                    act.wait_ge(s("shifted"), 14 + g - 1)
                b = bank_full(act, "in1", g)
                L(A(pad1[:, g % 2, 1:129], b[:, 0:P], ACT.Identity, bias=col("b_in", g)))
                free(A(pad1[:, g % 2, 130:386], b[:, P:T], ACT.Identity, bias=col("b_in", g)), g)
            for n in range(2):
                act.wait_ge(s("sin_in"), n + 1)
                A(hid[0:64, n, :], htmp[0:64, 0, :], ACT.Sin).then_inc(s("hid_ready"), 1)
            act.wait_ge(s("filters"), 1)
            na = 0
            for tiles in ((1, 2), (0,)):
                for h in range(2):
                    for t in tiles:
                        for part in range(2):
                            o = part * D + 512 * h
                            A(absf[:, na, :], filt[:, t, o:o + 512], ACT.Abs).then_inc(s("abs_ready"), 1)
                            na += 1
            copied(act, "filtF", 11)
            for g in range(6):
                b = bank_full(act, "zT", g)
                free(A(z[:, g // 2, 512 * (g % 2):512 * (g % 2) + 512], b, ACT.Copy), g)
            for g in range(12):
                b = bank_full(act, "zF", g)
                free(A(zF[:, g // 2, 512 * (g % 2):512 * (g % 2) + 512], b, ACT.Copy), g)
            gate_rows("gate1")
            peer(1)

    return nc


def weight_jobs(w):
    n = -(-w.shape[1] // 512)
    out = np.zeros((n, P, KD, 512), np.float32)
    for j in range(n):
        part = w[:, 512 * j:512 * (j + 1)]
        out[j, :, :, :part.shape[1]] = part.reshape(KD, P, -1).transpose(1, 0, 2)
    return out.reshape(n, P, SLOT)


def uv_jobs(u, v):
    out = np.empty((UVJOBS, P, 2, 2 * D), np.float32)
    out[:, :, 0, :] = u.reshape(P, UVJOBS, 2, KD, P).transpose(1, 4, 2, 3, 0).reshape(UVJOBS, P, 2 * D)
    out[:, :, 1, :] = v.reshape(P, UVJOBS, 2 * D).transpose(1, 0, 2)
    return out.reshape(UVJOBS, P, SLOT)


def column(v):
    return v.reshape(-1, P).T


def dft_tables(L):
    t, f = np.arange(L)[:, None], np.arange(L)[None, :]
    ang = 2 * np.pi * ((t * f) % (2 * L)) / (2 * L)
    re, im = np.cos(ang), -np.sin(ang)
    ny = np.cos(np.pi * t[:, 0])
    im[:, 0] = ny
    fwd = np.concatenate([re, im], 1)
    imb = np.sin(ang)
    imb[:, 0] = ny
    bwd = np.concatenate([re, imb], 1)
    bwd[0] = 0
    w = np.full(L, 2.0)
    w[0] = 1.0
    inv_re = (w[:, None] * np.cos(ang.T)) / (2 * L)
    inv_im = (-2.0 * np.sin(ang.T)) / (2 * L)
    inv_im[0] = ny / (2 * L)
    inv = np.concatenate([inv_re, inv_im], 0)
    return [a.astype(np.float32) for a in (fwd, bwd, inv)]


def hyena_constants():
    zpos, window = np.zeros((33, T), np.float32), np.zeros((P, 3, D), np.float32)
    f = np.float32
    deltas = np.linspace(np.log(1e-2) / 0.3, np.log(1e-2) / 1.5, D).astype(f)
    bands = np.linspace(1e-4, 15, 16).astype(f)
    for L, o in ((P, 0), (2 * P, P)):
        t = np.arange(L, dtype=f)[:, None]
        unit = t / f(L - 1)
        ang = (f(2.0 * np.pi) * t * bands / f(L)).astype(f)
        zpos[:, o:o + L] = np.concatenate([unit, np.cos(ang), -np.sin(ang)], 1).T
        win = np.exp(-unit * np.abs(deltas))
        window[:, o // P:(o + L) // P, :] = win.reshape(-1, P, D).transpose(1, 0, 2)
    return zpos, window


def scan_masks():
    j, t = np.arange(P)[:, None] % CH, np.arange(P)[None, :] % CH
    out = []
    for d in range(2):
        for lev in range(6):
            b = 1 << lev
            m = (t // (2 * b) == j // (2 * b)) & ((t // b) % 2 == 1) & ((j // b) % 2 == 0)
            if d == 1:
                m = (t // (2 * b) == j // (2 * b)) & ((j // b) % 2 == 1) & ((t // b) % 2 == 0)
            out.append(m)
    out += [j < t, j <= t, j > t, j >= t]
    return np.stack(out, 1).astype(np.float32)


def fill(n):
    return np.zeros((P, n), np.float32)


def kernel(**inputs):
    import concourse.bacc as bacc
    from concourse.bass_utils import run_bass_kernel_spmd

    a = {k: np.ascontiguousarray(v) for k, v in inputs.items()}
    f = np.float32
    zpos, window = hyena_constants()
    jobs = []
    for l in range(2):
        if l == 0:
            jobs.append(weight_jobs(a["w_mod"][0]))
            w = a["ab_w_in"][0]
            jobs += [weight_jobs(w[:, :1792]), weight_jobs(w[:, 1792:])]
            small = fill(SLOT)
            small[:, 0:1536] = a["mla_q_up"][0].reshape(2, P, 768).transpose(1, 0, 2).reshape(P, 1536)
            small[:, 1536:2560] = a["mla_kv_up"][0]
            small[0:64, 2560:3584] = a["rw_w2"][0].transpose(1, 0, 2).reshape(64, 1024)
            small[64:P, 2560:3584] = a["rw_a2"][0].transpose(1, 0, 2).reshape(64, 1024)
            small[:, 3584:4096] = a["rw_g2"][0]
            jobs += [small[None], np.zeros((2, P, SLOT), np.float32), weight_jobs(a["ab_w_out"][0])]
        else:
            jobs.append(weight_jobs(a["hy_w_in"][0]))
            win, flt, dft = fill(SLOT), fill(SLOT), fill(SLOT)
            win[:, 0:3072] = window.reshape(P, 3072)
            flt[0:64, 0:2048] = a["hy_f_w3"][0]
            flt[0:33, 2048:2432] = zpos
            flt[0:33, 2432:2496] = a["hy_f_w1"][0]
            flt[0:64, 2496:2560] = a["hy_f_w2"][0]
            o = 0
            for L in (2 * P, P):
                for m in dft_tables(L):
                    n = m.size // P
                    dft[:, o:o + n] = m.reshape(-1, P, m.shape[1]).transpose(1, 0, 2).reshape(P, n)
                    o += n
            jobs += [win[None], flt[None], dft[None], weight_jobs(a["hy_w_out"][0])]
        keys = fill(SLOT)
        keys[:, 0:2048] = a["peer_keys"][l].reshape(SIDES, P, P).transpose(2, 0, 1).reshape(P, 2048)
        jobs += [keys[None], weight_jobs(a["peer_w_q"][l])]
        if l == 0:
            jobs.append(weight_jobs(a["w_mod"][1]))
        jobs.append(uv_jobs(a["peer_u"][l], a["peer_v"][l]))
    stream = np.concatenate(jobs)
    assert len(stream) == N_JOBS

    cols = fill(N_COLS)

    def put(name, block):
        cols[:block.shape[0], COLS[name]:COLS[name] + block.shape[1]] = block
    put("mu", column(a["rw_mu"][0]))
    put("k_k", column(a["rw_k_k"][0]))
    put("k_a", column(a["rw_k_a"][0]))
    put("r_k", column(a["rw_r_k"][0]))
    put("w0", column(a["rw_w0"][0]))
    put("a0", column(a["rw_a0"][0]))
    put("g", column(a["norm_g"]))
    put("b_mod", column(a["b_mod"]))
    put("b_in", column(a["hy_b_in"][0]))
    put("conv_w", column(a["hy_conv_w"][0]))
    put("conv_b", column(a["hy_conv_b"][0]))
    put("bias", column(a["hy_bias"][0]))
    put("f_b1", a["hy_f_b1"][0][:, None])
    put("f_b2", a["hy_f_b2"][0][:, None])
    put("freq", a["hy_f_freq"][0][:, None])
    put("cond", np.stack([a["c_ctx"], a["c"][0]], 1).reshape(KD, P, 2).transpose(1, 0, 2).reshape(P, 16))

    consts = fill(832)
    i = np.arange(P)
    consts[:, 0:128] = np.eye(P)
    consts[:, 128:256] = i[:, None] // 64 == i[None, :] // 64
    consts[:, 256:320] = i[:, None] % 64 == np.arange(64)[None, :]
    consts[:, 320:704] = (np.arange(T) % CH != 0)[None, :]
    consts[:, 704:832] = i[None, :]

    pos = np.arange(2 * P)
    inv = (f(10000.0) ** (-np.arange(16, dtype=f) / f(16))).astype(f)
    ang = np.concatenate([(pos // 64)[:, None].astype(f) * inv, (pos % 64)[:, None].astype(f) * inv], 1)
    rope = np.stack([np.cos(ang), np.sin(ang)]).astype(f)

    arrays = {
        "x_prompt": a["x_prompt"], "x_sample": a["x_sample"], "cols": cols, "consts": consts,
        "masks": scan_masks(), "rope": rope, "stream": stream,
        "rows": np.concatenate([a["mla_q_norm"][0], a["mla_kv_norm"][0], a["mla_qn"][0], a["mla_kn"][0]])[None],
        "cache_mla_ckv": a["cache_mla_ckv"], "cache_mla_kpe": a["cache_mla_kpe"],
        "state_rwkv_fwd": a["state_rwkv_fwd"], "state_rwkv_bwd": a["state_rwkv_bwd"],
        "lnx_g": a["rw_lnx_g"][0].reshape(PAIRS, 2, CH).transpose(1, 0, 2).copy(),
        "lnx_b": a["rw_lnx_b"][0].reshape(PAIRS, 2, CH).transpose(1, 0, 2).copy(),
    }
    outs = {"o_prompt": (1, P, D), "o_sample": (1, 2 * P, D), "o_fwd": (1, 1, HEADS, 64, 64),
            "o_bwd": (1, 1, HEADS, 64, 64), "o_ckv": (1, 1, P, 128), "o_kpe": (1, 1, P, 64)}
    nc = bacc.Bacc("TRN2", target_bir_lowering=False, num_devices=1)
    io = {}
    for k, v in arrays.items():
        io[k] = nc.dram_tensor("in_" + k, v.shape, F32, kind="ExternalInput").ap()
    for k, shape in outs.items():
        io[k] = nc.dram_tensor(k, shape, F32, kind="ExternalOutput").ap()
    build(nc, io)
    r = run_bass_kernel_spmd(nc, [{"in_" + k: v for k, v in arrays.items()}], core_ids=[0]).results[0]
    return tuple(r[k] for k in outs)
```

```python
from contextlib import ExitStack
from itertools import zip_longest

import numpy as np

import concourse.bass as bass
from concourse import mybir

F32 = mybir.dt.float32
U32 = mybir.dt.uint32
BF16 = mybir.dt.bfloat16
F32R = mybir.dt.float32r
ALU = mybir.AluOpType
ACT = mybir.ActivationFunctionType
AX = mybir.AxisListType

P = 128
D = 1024
KD = D // P
TILES = 3
T = TILES * P
EPS = 1e-6
LNX_EPS = 64e-5
HEADS = 8
PAIRS = HEADS // 2
CH = 64
NCH = T // CH
MLA_HEADS = 4
QK = 192
KEYTILES = 4
SLOT = 4096
RING = 3
TOPK = 16
SIDES = 16
NEAR = 4
assert (NEAR + 1) ** 2 > TOPK
CANDS = NEAR * TOPK + (TOPK - NEAR) * NEAR
SLICE = 16
SLICES = P // SLICE
UVRING = 2
STEPS = 2 * UVRING
BLOCKS = SLICE // STEPS
BUILD = 8
PER_STEP = T // BUILD // SLICE
NG = T // BUILD
UVJOBS = 64

JOB_COUNTS = [[("mod", 4), ("in", 5), ("small", 1), ("mod0b", 8), ("scratch", 2), ("out", 2), ("keys", 1), ("wq", 4),
               ("mod1", 12),
               ("uv", UVJOBS)],
              [("in", 6), ("window", 1), ("filter", 1), ("dft", 1), ("out", 2), ("keys", 1),
               ("wq", 4), ("uv", UVJOBS)]]
JOB = {}
N_JOBS = 0
for _l, _jobs in enumerate(JOB_COUNTS):
    for _name, _n in _jobs:
        JOB[{"mod": "mod0", "mod1": "sel0"}.get(_name, _name), _l] = N_JOBS
        N_JOBS += _n

SLOT_OF, BEFORE, LANDING = [], [], []
SCRATCH = [JOB[("scratch", 0)], JOB[("scratch", 0)] + 1]
for _j in range(N_JOBS):
    _uv = [_j - JOB[("uv", _l)] for _l in range(2) if 0 <= _j - JOB[("uv", _l)] < UVJOBS]
    _slot = _uv[0] % UVRING if _uv else _j % RING
    _same = [_i for _i in range(_j) if SLOT_OF[_i] == _slot]
    SLOT_OF.append(_slot)
    BEFORE.append(_same[-1] if _same else -1)
    LANDING.append(len([_i for _i in _same if _i not in SCRATCH]) + 1)

SCAN_GROUPS = tuple(sorted(8 * (_g // 4) + 4 * _d + _g % 4 for _d in range(2) for _g in range(26)))
STAGES = [("mod0", 8, 1), ("norm0", 6, 1), ("in0", 17, 1), ("qkvT", 3, 1), ("up", 14, 1), ("headT", 16, 1),
          ("att", 6, MLA_HEADS), ("knorm", 4, 1), ("lora", 20, 1), ("mod0b", 8, 2), ("state_in", 4, 1),
          ("scanp", SCAN_GROUPS, 2), ("state_out", 2, 1), ("scans", SCAN_GROUPS, 4),
          ("coef", (6,), 1), ("yT", 12, 1), ("gate0", 4, 1), ("out0", 6, 1), ("norm0b", 6, 1), ("wk0", 32, 1),
          ("sel0", 9, 3), ("hot0", 6, 1), ("gate0b", (6, 7, 14, 15), 1),
          ("norm1", 6, 1), ("in1", 24, 1), ("hid", 2, 1), ("filt", 12, 1), ("norm_f", 4, 1),
          ("filtF", 12, 1), ("zT", 6, 1), ("zF", 12, 1), ("conv", 8, 1), ("gate1", 4, 1), ("out1", 6, 1),
          ("norm1b", 6, 1), ("wk1", 32, 1), ("sel1", 1, 3), ("hot1", 6, 1), ("gate1b", (6, 7, 14, 15), 1)]


def plan_banks():
    used, first, groups = [0] * 8, {}, {}
    for stage, gs, n in STAGES:
        first[stage], groups[stage] = list(used), range(gs) if isinstance(gs, int) else gs
        for q in groups[stage]:
            used[q % 8] += n
    return first, groups


FIRST, GROUPS = plan_banks()


def use_of(stage, q, i=0):
    same = [g for g in GROUPS[stage] if g % 8 == q % 8]
    before = FIRST[stage][q % 8] + same.index(q)
    if isinstance(i, int):
        return before + len(same) * i
    return i * len(same) + before


def sg(d, g):
    return 8 * (g // 4) + 4 * d + g % 4


WQ = [max(0, 2 * _a - 1) for _a in range(SIDES)]
KEYG = [min(2 * _a + 2, 2 * SIDES - 1) for _a in range(SIDES)]
SELG = [8, 0]
SPLIT = {"norm0": 0, "norm0b": 1, "norm1": 2, "norm1b": 3}
W_BASE = {"in0": 0, "wk0": 14, "in1": 30, "wk1": 54}
NORM_NO = {"norm0": 0, "norm0b": 1, "norm1": 2, "norm1b": 3}
GATE_NO = {"gate0": 0, "gate0b": 1, "gate1": 2, "gate1b": 3}

COLS = {}
N_COLS = 0
for _name, _n in [("mu", 14), ("k_k", 4), ("k_a", 4), ("r_k", 4), ("w0", 8), ("a0", 8), ("g", 32), ("b_mod", 96),
                  ("b_in", 24), ("conv_w", 72), ("conv_b", 24), ("bias", 8), ("f_b1", 1), ("f_b2", 1), ("freq", 1),
                  ("cond", 16)]:
    COLS[_name] = N_COLS
    N_COLS += _n
ROWS = {"q_norm": (0, 256), "kv_norm": (256, 128), "qn": (384, 192), "kn": (576, 192)}
N_ROWS = 768


def build(nc, io):
    with ExitStack() as ctx:
        def sb(name, shape, dt=F32):
            return ctx.enter_context(nc.sbuf_tensor(name, shape, dt))

        sems = {}

        def s(name):
            if name not in sems:
                sems[name] = ctx.enter_context(nc.semaphore(name))
            return sems[name]

        ring = sb("ring", [P, RING, SLOT])
        x = sb("x", [P, TILES, D])
        cols = sb("cols", [P, N_COLS])
        modc = sb("modc", [P, 2, 48, 2])
        gsc = sb("gsc", [P, KD, 2])
        condT = sb("condT", [P, KD, 2])
        ident = sb("ident", [P, P])
        stacked = sb("stacked", [P, CH])
        iota = sb("iota", [P, P])
        rep16 = sb("rep16", [P, P * BUILD], BF16)
        ones = sb("ones", [P, P])
        headones = sb("headones", [P, P])
        stat = sb("stat", [P, 64])
        elast = sb("elast", [P, 2, PAIRS, NCH])
        coef = sb("coef", [P, PAIRS, NCH])
        row2 = sb("row2", [P, 512])
        shared = sb("shared", [P, 4480])
        masks = shared[:, 0:2048].rearrange("p (m c) -> p m c", m=16)
        ST = shared[:, 2048:3072].rearrange("p (s d m v) -> p s d m v", s=2, d=2, m=PAIRS)
        s0 = shared[0:64, 3072:4096].rearrange("v (d h k) -> v d h k", d=2, h=HEADS)
        scanmask = shared[:, 4096:4480]
        sel = shared[:, 0:3 * T].rearrange("p (m t) -> p m t", m=3)
        sel16 = shared[:, 3 * T:11 * T // 2].bitcast(BF16).rearrange("p (m t) -> p m t", m=5)
        gel = shared[:, 6 * T:8 * T].rearrange("p (b t) -> p b t", b=2)
        gw = shared[:, 8 * T:10 * T].rearrange("p (b t) -> p b t", b=2)
        with nc.sbuf_tensor("arena", [P, 27648], F32) as arena, nc.sbuf_tensor("hT", [P, KD, T], F32) as hT:
            pass
        wd = sb("wd", [P, 2, T, SLICE])
        xs = sb("xs", [P, 2, KD, T], F32R)
        us = sb("us", [P, 2, 2, D], F32R)
        vs = sb("vs", [P, 2, 2, D], F32R)
        gs = sb("gs", [P, 2, 2, T], F32R)
        ohA = sb("ohA", [P, 2, P, BUILD], BF16)
        ohE = sb("ohE", [P, 2, SLICE, BUILD], BF16)
        ohB = sb("ohB", [P, 2, 3, SLICE, BUILD], BF16)
        psum = ctx.enter_context(nc.psum_tensor("psum", [P, 8, 512], F32))

        def area(off, *shape):
            n = 1
            for d in shape:
                n *= d
            assert off + n <= 27648, (off, shape)
            a = arena[:, off:off + n]
            if len(shape) == 1:
                return a
            names = "abcd"[:len(shape)]
            return a.rearrange("p (%s) -> p %s" % (" ".join(names), " ".join(names)),
                               **{names[k]: shape[k] for k in range(len(shape) - 1)})

        rkv = area(0, 12, T)
        wdad = area(4608, T)
        gd = area(4992, T)
        mla0 = 5376
        mla = area(mla0, 3, 448)
        ckv = area(mla0 + 1344, KEYTILES, 128)
        kpe = area(mla0 + 1856, KEYTILES, 64)
        qc = area(mla0 + 2112, 3, 256)
        qcT = area(mla0 + 2880, 2, T)
        ckvT = area(mla0 + 3648, KEYTILES * P)
        q = area(mla0 + 4160, 3, MLA_HEADS, QK)
        kx = area(mla0 + 6464, KEYTILES, MLA_HEADS, QK)
        vx = area(mla0 + 9536, KEYTILES, MLA_HEADS, P)
        qTn = area(mla0 + 11584, MLA_HEADS, T)
        qTr = area(mla0 + 13120, MLA_HEADS, T)
        kTn = area(mla0 + 14656, MLA_HEADS, 4 * P)
        kTr = area(mla0 + 16704, MLA_HEADS, 4 * P)
        sq = area(mla0 + 14656, 3072)
        prob = area(mla0 + 0, 7, P)
        probT = area(mla0 + 2112, 7, P)
        rows = area(mla0 + 18752, N_ROWS)
        rope = area(mla0 + 19520, 2, 2, 32)
        rtmp = area(mla0 + 19648, 4, 2, MLA_HEADS, 32)
        assert mla0 + 19648 + 1024 <= 27648
        tilde = area(5376, 8, PAIRS, T)
        ksum = area(17664, PAIRS, T)
        kk = area(19200, PAIRS, T)
        ld = area(20736, PAIRS, T)
        cum = area(22272, PAIRS, T)
        cumx = area(23808, PAIRS, T)
        lr = area(25344, PAIRS, T)
        tr0 = 19200
        flat = ring[:, 0:2, :].rearrange("p s n -> p (s n)")
        assert [SLOT_OF[j] for j in SCRATCH] == [0, 1]

        def transients(base, sa):
            m = [base[:, 2560 + 512 * n:3072 + 512 * n] for n in range(10)]
            return [base[:, 0:2560].rearrange("p (n m c) -> p n m c", n=5, m=PAIRS)] + m + [
                base[:, 7680:7936], base[:, 7936:8192], sa]
        scan_mem = [transients(arena[:, tr0:tr0 + 8192], area(tr0 + 8192, 256)), transients(flat, area(4608, 256))]
        y = area(1536, NCH, PAIRS, CH)
        lora_rhs = area(26880, 2, T)
        bexp = row2[:, 0:256].rearrange("p (b n) -> p b n", b=2)
        bonus_w = area(0, PAIRS, T)
        lnx = area(tr0, 2, PAIRS, CH)
        yc = area(tr0 + 512, NCH, PAIRS, CH)
        ysq = area(tr0 + 2048, NCH, PAIRS, CH)
        zexp = area(tr0 + 3584, 2, PAIRS, P)
        vtok = area(tr0 + 4608, NCH, PAIRS, CH)
        pad = area(mla0 + 20736, 2, 388)
        padt = area(mla0 + 21512, 388)
        xn = area(24576, 1024)
        xn2 = area(25600, 1024)
        junk = area(26624, 1024)
        gate_row = area(20480, 2, D)
        x0T = area(0, KD, T)
        zinT = area(3072, KD, T)
        filtF = area(6144, 6, D)
        zF = area(12288, 6, D)
        filt = area(12288, 3, 2 * D)
        z = area(18432, 3, D)
        absf = area(6144, 12, 512)
        rnorm = area(18432, 2, D)
        hid = area(22528, 2, T)
        htmp = area(23296, 2, T)
        prod = area(21504, 2, D)
        pad1 = area(24576, 2, 388)
        padt1 = area(25352, 388)
        vtmp = area(25740, T)
        gate_bc = area(9216, 16, P)
        qT = area(0, SIDES, T)
        sc = area(6144, SIDES, TILES, P)
        top = area(24576, TILES, SIDES, TOPK)
        topi = area(25344, TILES, SIDES, TOPK)
        topif = area(26112, TILES, SIDES, TOPK)
        cand = area(0, HEADS, CANDS)
        dec = area(1024, 4, P)
        mix = area(1536, 2, P)
        tops = area(2048, HEADS, TOPK)
        posu = area(2176, HEADS, TOPK)
        oh = [area(o, 1024).bitcast(BF16).rearrange("p (m k h) -> p m k h", m=TOPK, k=TOPK) for o in (2560, 3584)]
        pick = area(4608, 3, P)
        pos16 = [area(o, 64).bitcast(BF16).rearrange("p (k h) -> p k h", k=TOPK) for o in (4992, 5056)]
        key16 = [area(o, 64).bitcast(BF16).rearrange("p (m h) -> p m h", m=TOPK) for o in (5120, 5184)]
        places = area(18432, 1024).bitcast(BF16)
        subkeys = area(22528, SIDES, P)
        modrow = area(22528, 2, 512)

        MODROW = {"mod0": (modrow[:, 0], modrow[:, 1]), "sel0": (modrow[:, 0], modrow[:, 1]),
                  "mod0b": (area(26880, 512), row2[:])}

        block = ctx.enter_context(nc.Block())

        def slot(job):
            return ring[:, SLOT_OF[job], :]

        def landed(eng, job):
            eng.wait_ge(s("landed%d" % SLOT_OF[job]), 16 * LANDING[job])

        def bank_free(eng, stage, g, i=0):
            u = use_of(stage, g, i)
            if not (isinstance(u, int) and u == 0):
                eng.wait_ge(s("bank_free%d" % (g % 8)), u)
            return psum[:, g % 8, :]

        def bank_full(eng, stage, g, i=0):
            eng.wait_ge(s("bank_full%d" % (g % 8)), use_of(stage, g, i) + 1)
            return psum[:, g % 8, :]

        def full(ins, g):
            ins.then_inc(s("bank_full%d" % (g % 8)), 1)

        def copied(eng, stage, g, i=0):
            eng.wait_ge(s("bank_free%d" % (g % 8)), use_of(stage, g, i) + 1)

        def free(ins, g):
            ins.then_inc(s("bank_free%d" % (g % 8)), 1)

        def chain(eng, name):
            at = {"base": 0, "n": 0}

            def link(ins):
                ins.then_inc(s(name), 1)
                at["n"] += 1
                eng.wait_ge(s(name), at["base"] + at["n"])

            def enter(base):
                done = at["n"]
                at["base"], at["n"] = base, 0
                return done

            return link, enter

        def tell(eng, ins, name, value):
            ins.then_inc(s(name), 1)
            eng.wait_ge(s(name), value)

        def expert_steps(eng, step):
            def block(lin, sl, j, par, start=False, end=False):
                for u in range(STEPS):
                    last = end and u == STEPS - 1
                    step(lin, sl, j, u, par, "first" if start and u == 0 else "end" if last else "")

            block(lambda k, c: c, lambda k, c: c, 0, 0, start=True)
            with eng.Fori(1, BLOCKS) as j:
                block(lambda k, c: j * k + c, lambda k, c: c, j, 0)
            with eng.Fori(0, SLICES // 2 - 1) as i:
                for n in (1, 2):
                    with eng.Fori(0, BLOCKS) as j:
                        block(lambda k, c: i * (2 * BLOCKS * k) + j * k + (n * BLOCKS * k + c),
                              lambda k, c: i * (2 * k) + (n * k + c), j, n % 2)
            m = BLOCKS * (SLICES - 1)
            with eng.Fori(0, BLOCKS - 1) as j:
                block(lambda k, c: j * k + (m * k + c), None, j, 1)
            block(lambda k, c: (m + BLOCKS - 1) * k + c, None, BLOCKS - 1, 1, end=True)

        def weight_part(n, part):
            return us[:, n % 2, part, :].rearrange("p (k n) -> p k n", k=KD)

        def weight_columns(name, l, n):
            w = slot(JOB[(name, l)] + n // 4).rearrange("p (k n) -> p k n", k=KD)
            return w[:, :, n % 4 * P:(n % 4 + 1) * P]

        def table(j0, n):
            d = ring[:, SLOT_OF[j0 + n // 2], :].rearrange("p (m c d) -> p m c d", m=2, c=2)
            return d[:, 0, n % 2, :], d[:, 1, n % 2, :]

        def both(items):
            for _parts in zip_longest(*items):
                pass

        def at_least(eng, name, value):
            if not isinstance(value, int) or value > 0:
                eng.wait_ge(s(name), value)

        def bc(ap, n):
            return ap.unsqueeze(2).to_broadcast([ap.shape[0], ap.shape[1], n])

        def head_bc(ap, n, k):
            return ap.unsqueeze(1).to_broadcast([ap.shape[0], k, n])

        def blocks(ap):
            return ap.rearrange("p (m c) -> p m c", m=PAIRS)

        def col(name, k=0):
            return cols[:, COLS[name] + k:COLS[name] + k + 1]

        @block.sync
        def _(sp):
            for ap, src in [(x[:, 0, :], io["x_prompt"][0]),
                            (x[:, 1:3, :], io["x_sample"][0].rearrange("(a p) d -> p a d", p=P)),
                            (cols[:], io["cols"]), (ident[:], io["consts"][:, 0:128]),
                            (headones[:], io["consts"][:, 128:256]), (stacked[:], io["consts"][:, 256:320]),
                            (scanmask, io["consts"][:, 320:704]), (iota[:], io["consts"][:, 704:832])]:
                sp.dma_start(ap, src).then_inc(s("inputs"), 16)

            def job_load(j, k, used):
                if used is not None:
                    sp.wait_ge(s("slot_used"), used)
                sp.dma_start(ring[:, k, :], io["stream"][j]).then_inc(s("landed%d" % k), 16)

            def load_plain(first, last):
                for j in sorted(set(range(first, last)) - set(SCRATCH)):
                    job_load(j, SLOT_OF[j], BEFORE[j] + 1 if BEFORE[j] >= 0 else None)
            load_plain(0, RING)
            m = SCRATCH[0] // RING
            n = JOB[("uv", 0)] // RING
            for first, last in ((1, m), (m + 1, n)):
                with sp.Fori(first, last) as i:
                    for k in range(RING):
                        job_load(i * RING + k, k, i * RING + (k - RING + 1))
                load_plain(last * RING, last * RING + RING if last == m else JOB[("uv", 0)])
            for l in range(2):
                first = JOB[("uv", l)]
                load_plain(first, first + UVRING)
                with sp.Fori(1, UVJOBS // UVRING) as i:
                    for k in range(UVRING):
                        job_load(i * UVRING + (first + k), k, i * UVRING + (first + k - UVRING + 1))
                load_plain(first + UVJOBS, JOB[("uv", 1)] if l == 0 else N_JOBS)

        @block.gpsimd
        def _(pool):
            bank_full(pool, "norm0", 5)
            for ap, src in [(masks, io["masks"]), (rows, io["rows"].to_broadcast([P, N_ROWS])),
                            (rope[:, 0], io["rope"][0].rearrange("(a p) f -> p a f", p=P)),
                            (rope[:, 1], io["rope"][1].rearrange("(a p) f -> p a f", p=P)),
                            (ckv[:, 1, :], io["cache_mla_ckv"][0, 0]), (kpe[:, 1, :], io["cache_mla_kpe"][0, 0]),
                            (s0[:, 0], io["state_rwkv_fwd"][0, 0].rearrange("h v k -> v h k")),
                            (s0[:, 1], io["state_rwkv_bwd"][0, 0].rearrange("h v k -> v h k"))]:
                pool.dma_start(ap, src).then_inc(s("mixer_params"), 16)
            def weight_lo(name, l, stage, n):
                pool.wait_ge(s("w_hi"), W_BASE[stage] + n + 1)
                nc.gpsimd.tensor_tensor(weight_part(n, 1), weight_columns(name, l, n),
                                        weight_part(n, 0).bitcast(F32), ALU.subtract).then_inc(s("w_lo"), 1)
            for n in range(14):
                weight_lo("in", 0, "in0", n)
            pool.wait_ge(s("latents"), 1)
            pool.dma_start(io["o_ckv"][0, 0], ckv[:, 0, :]).then_inc(s("stored"), 16)
            pool.dma_start(io["o_kpe"][0, 0], kpe[:, 0, :]).then_inc(s("stored"), 16)

            def block_masks(stage, i):
                for lev, d in [(lev, d) for lev in range(1, 6) for d in range(2)]:
                    ex, NT, NTm, Tm, TT, Pm, KT, RkT, RbT, ktok, btok, Vt, Xt, SA = scan_mem[d]
                    if lev == 1:
                        copied(pool, stage, sg(d, 1), i)
                    else:
                        bank_full(pool, stage, sg(d, 8 + 3 * (lev - 2)), i)
                    m = masks[:, lev + 6 * d, :].unsqueeze(1).to_broadcast([P, PAIRS, P])
                    nc.gpsimd.tensor_tensor(blocks(NTm), blocks(NT), m, ALU.mult).then_inc(s("ntm_ready%d" % d), 1)
            with pool.Fori(0, 2) as i:
                block_masks("scanp", i)
            pool.wait_ge(s("state_copied"), 2)
            for d, name in enumerate(("o_fwd", "o_bwd")):
                pool.dma_start(io[name][0, 0].rearrange("h v k -> v h k"), s0[:, d]).then_inc(s("stored"), 16)
            with pool.Fori(0, 4) as i:
                block_masks("scans", i)
            pool.wait_ge(s("scan_done"), 1)
            for h in range(2):
                for m, name in enumerate(("lnx_g", "lnx_b")):
                    pool.dma_start(lnx[64 * h:64 * h + 64, m],
                                   io[name][h:h + 1].to_broadcast([64, PAIRS, CH])).then_inc(s("lnx_loaded"), 16)
            for l in range(2):
                if l == 1:
                    for n in range(24):
                        weight_lo("in", 1, "in1", n)
                for n in range(SIDES):
                    weight_lo("wq", l, "wk%d" % l, n)

                def step(lin, sl, j, u, par, where):
                    n = lin(STEPS, P * l + u)
                    pool.wait_ge(s("v_hi"), n + 1)
                    nc.gpsimd.tensor_tensor(vs[:, u % 2, 1, :], table(JOB[("uv", l)], u)[1],
                                            vs[:, u % 2, 0, :].bitcast(F32), ALU.subtract).then_inc(s("v_lo"), 1)
                expert_steps(pool, step)
            pool.wait_ge(s("y_done"), 1)
            pool.dma_start(io["o_prompt"][0], x[:, 0, :]).then_inc(s("stored"), 16)
            pool.dma_start(io["o_sample"][0].rearrange("(a p) d -> p a d", p=P), x[:, 1:3, :]).then_inc(s("stored"), 16)
            pool.wait_ge(s("stored"), 16 * 6)

        @block.tensor
        def _(pe):
            mm = nc.tensor.matmul

            def hand_back(ins, jobs=1):
                ins.then_inc(s("slot_used"), jobs)

            def adaln_jobs(stage, i):
                def row(n):
                    job = JOB[(stage, 0)] + 4 * i + n
                    w = slot(job).rearrange("p (k n) -> p k n", k=KD)
                    landed(pe, job)
                    b = bank_free(pe, stage, n, i)
                    for k in range(KD):
                        ins = mm(b[0:2, :], condT[:, k, :], w[:, k, :], start=k == 0, stop=k == KD - 1)
                        if k == 0 and job > 0:
                            hand_back(ins)
                    full(ins, n)

                def columns(n):
                    copied(pe, stage, n, i)
                    b = bank_free(pe, stage, 4 + n, i)
                    for m in range(4):
                        ins = nc.tensor.transpose(b[:, 2 * m:2 * m + 2],
                                                  MODROW[stage][n % 2][0:2, m * P:(m + 1) * P], ident[0:2, 0:2])
                        if (stage, i, n, m) == ("mod0b", 1, 3, 0):
                            hand_back(ins)
                    full(ins, 4 + n)
                for n in range(4):
                    row(n)
                    if n > 0:
                        columns(n - 1)
                columns(3)

            def norm_transposes(stage):
                for t in range(TILES):
                    pe.wait_ge(s("normed"), NORM_NO[stage] * TILES + t + 1)
                    for h in range(2):
                        b = bank_free(pe, stage, 2 * t + h)
                        for k in range(4):
                            ins = nc.tensor.transpose(b[:, k * P:(k + 1) * P],
                                                      (xn, xn2)[t % 2][:, (4 * h + k) * P:(4 * h + k + 1) * P], ident[:])
                            if stage != "norm1" and t == 0 and h == 0 and k == 0:
                                hand_back(ins)
                        full(ins, 2 * t + h)

            def split_product(stage, g, n, back=False):
                pe.wait_ge(s("w_lo"), W_BASE[stage] + n + 1)
                b = bank_free(pe, stage, g)
                w = [weight_part(n, part) for part in range(2)]
                for k in range(KD):
                    for c, (kw, kx) in enumerate(((0, 0), (0, 1), (1, 0))):
                        ins = mm(b[:, 0:T], w[kw][:, k, :], xs[:, kx, k, :], start=k == 0 and c == 0,
                                 stop=k == KD - 1 and c == 2)
                        if back and k == 0 and c == 0:
                            hand_back(ins)
                full(ins, g)

            def token_product(stage, g, w, n, t, back=False):
                b = bank_free(pe, stage, g)
                for k in range(KD):
                    ins = mm(b[:, 0:n], hT[:, k, t * P:(t + 1) * P], w[:, k, 0:n], start=k == 0, stop=k == KD - 1)
                    if back and k == 0:
                        hand_back(ins)
                full(ins, g)

            def out_product(l):
                for j in range(2):
                    job = JOB[("out", l)] + j
                    landed(pe, job)
                    w = slot(job).rearrange("p (k n) -> p k n", k=KD)
                    for t in range(TILES):
                        token_product("out%d" % l, 3 * j + t, w, 512, t, back=j == 1 and t == 0)

            def gate_rows(stage, l):
                pe.wait_ge(s("gate_cols"), GATE_NO[stage] + 1)
                for c in range(2):
                    for h in range(2):
                        g = GROUPS[stage][2 * c + h]
                        b = bank_free(pe, stage, g)
                        for k in range(4):
                            ins = mm(b[:, k * P:(k + 1) * P], gate_bc[:, 8 * c + 4 * h + k, :], ident[:],
                                     start=True, stop=True)
                            if (c, h, k) == (0, 0, 0) and (stage[-1] == "b" or stage == "gate1"):
                                hand_back(ins)
                        full(ins, g)

            pe.wait_ge(s("inputs"), 16 * 8)
            pe.wait_ge(s("cond_ready"), 1)
            adaln_jobs("mod0", 0)
            norm_transposes("norm0")
            pe.wait_ge(s("x_parts"), 3)
            for j in range(4):
                for m in range(4 if j < 3 else 2):
                    split_product("in0", 4 * j + m, 4 * j + m, back=j > 0 and m == 0)
            job = JOB[("in", 0)] + 4
            landed(pe, job)
            for t in range(TILES):
                token_product("in0", 14 + t, slot(job).rearrange("p (k n) -> p k n", k=KD), 448, t, back=t == 0)

            small = slot(JOB[("small", 0)])
            q_up = small[:, 0:1536].rearrange("p (k n) -> p k n", k=2)
            kv_up = small[:, 1536:2560]
            w2a2 = small[:, 2560:3584].rearrange("p (d n) -> p d n", d=2)
            g2 = small[:, 3584:4096]
            pe.wait_ge(s("latents"), 1)
            for k in range(2):
                b = bank_free(pe, "qkvT", k)
                for t in range(TILES):
                    ins = nc.tensor.transpose(b[:, t * P:(t + 1) * P], qc[:, t, k * P:(k + 1) * P], ident[:])
                    if k == 0 and t == 0:
                        hand_back(ins)
                full(ins, k)
            b = bank_free(pe, "qkvT", 2)
            for t in range(KEYTILES):
                ins = nc.tensor.transpose(b[:, t * P:(t + 1) * P], ckv[:, t, :], ident[:])
            full(ins, 2)
            landed(pe, JOB[("small", 0)])
            for g in range(3):
                copied(pe, "qkvT", g)
            for t in range(TILES):
                for h in range(2):
                    b = bank_free(pe, "up", 2 * t + h)
                    for k in range(2):
                        ins = mm(b[:, 0:384], qcT[:, k, t * P:(t + 1) * P], q_up[:, k, 384 * h:384 * h + 384],
                                 start=k == 0, stop=k == 1)
                    full(ins, 2 * t + h)
            for t in range(KEYTILES):
                for h in range(2):
                    b = bank_free(pe, "up", 6 + 2 * t + h)
                    full(mm(b, ckvT[:, t * P:(t + 1) * P], kv_up[:, 512 * h:512 * h + 512], start=True, stop=True),
                         6 + 2 * t + h)
            pe.wait_ge(s("heads_ready"), 1)
            for h in range(MLA_HEADS):
                for part, (src, n) in enumerate(((q, TILES), (q, TILES), (kx, KEYTILES), (kx, KEYTILES))):
                    g = 4 * h + part
                    b = bank_free(pe, "headT", g)
                    for t in range(n):
                        if part % 2 == 0:
                            ins = nc.tensor.transpose(b[:, t * P:(t + 1) * P], src[:, t, h, 0:P], ident[:])
                        else:
                            ins = nc.tensor.transpose(b[0:64, t * P:(t + 1) * P], src[:, t, h, P:QK], ident[:])
                    full(ins, g)
            for h in range(MLA_HEADS):
                if h == 0:
                    for g in range(8, 16):
                        copied(pe, "headT", g)
                for t in range(TILES):
                    keys = slice(0, P) if t == 0 else slice(P, 4 * P)
                    n = keys.stop - keys.start
                    b = bank_free(pe, "att", t, h)
                    mm(b[:, 0:n], qTn[:, h, t * P:(t + 1) * P], kTn[:, h, keys], start=True, stop=False)
                    full(mm(b[:, 0:n], qTr[0:64, h, t * P:(t + 1) * P], kTr[0:64, h, keys], start=False, stop=True), t)
                pe.wait_ge(s("probs"), h + 1)
                b = bank_free(pe, "att", 3, h)
                for n in range(4):
                    ins = nc.tensor.transpose(b[:, n * P:(n + 1) * P], prob[:, n, :], ident[:])
                full(ins, 3)
                b = bank_free(pe, "att", 4, h)
                for n in range(3):
                    ins = nc.tensor.transpose(b[:, n * P:(n + 1) * P], prob[:, 4 + n, :], ident[:])
                full(ins, 4)
                copied(pe, "att", 3, h)
                copied(pe, "att", 4, h)
                b = bank_free(pe, "att", 5, h)
                mm(b[:, 0:P], vx[:, 0, h, :], probT[:, 0, :], start=True, stop=True)
                for t in range(1, 3):
                    for n in range(3):
                        ins = mm(b[:, t * P:(t + 1) * P], vx[:, 1 + n, h, :], probT[:, 3 * t - 2 + n, :],
                                 start=n == 0, stop=n == 2)
                full(ins, 5)

            pe.wait_ge(s("kk_squares"), 1)
            for m in range(PAIRS):
                b = bank_free(pe, "knorm", m)
                full(mm(b[:, 0:T], headones[:], ld[:, m, :], start=True, stop=True), m)
            pe.wait_ge(s("lora_in"), 3)
            for d in range(2):
                for part in range(2):
                    for m in range(PAIRS):
                        g = 8 * d + 4 * part + m
                        b = bank_free(pe, "lora", g)
                        full(mm(b[:, 0:T], w2a2[:, d, m * P:(m + 1) * P], lora_rhs[:, part, :],
                                start=True, stop=True), g)
            for m in range(PAIRS):
                b = bank_free(pe, "lora", 16 + m)
                full(mm(b[:, 0:T], g2[:, m * P:(m + 1) * P], gd, start=True, stop=True), 16 + m)
            for i in range(2):
                adaln_jobs("mod0b", i)
            pe.wait_ge(s("mixer_params"), 16 * 8)
            for d in range(2):
                for h in range(2):
                    b = bank_free(pe, "state_in", 2 * d + h)
                    for n in range(2):
                        m = 2 * h + n
                        ins = nc.tensor.transpose(b[:, n * 64:(n + 1) * 64],
                                                  s0[:, d, 2 * m:2 * m + 2, :].rearrange("v h k -> v (h k)"),
                                                  ident[0:64, 0:64])
                    full(ins, 2 * d + h)
            def scan_item(stage, i, d, base):
                ex, NT, NTm, Tm, TT, Pm, KT, RkT, RbT, ktok, btok, Vt, Xt, SA = scan_mem[d]
                r_, a_, b_, k_, v_ = (ex[:, n] for n in range(5))
                S = ST[:, 0 if stage == "scanp" else 1, d]

                def pairs(g, lhsT, rhs, n=P):
                    b = bank_free(pe, stage, sg(d, g), i)
                    for m in range(PAIRS):
                        ins = mm(b[:, m * n:(m + 1) * n], lhsT(m), rhs(m), start=True, stop=True)
                    full(ins, sg(d, g))

                def sl(ap, n=P):
                    return lambda m: ap[:, m * n:(m + 1) * n]

                def pr(ap):
                    return lambda m: ap[:, m, :]
                pe.wait_ge(s("expanded%d" % d), i * 5 + (5 * base + 5))
                pairs(0, pr(a_), pr(b_))
                pairs(1, pr(b_), pr(a_))
                pairs(2, pr(k_), pr(a_))
                pairs(3, pr(k_), pr(r_))
                pairs(4, pr(b_), pr(r_))
                b = bank_free(pe, stage, sg(d, 5), i)
                for m in range(PAIRS):
                    ins = nc.tensor.transpose(b[:, m * P:(m + 1) * P], k_[:, m, :], ident[:])
                full(ins, sg(d, 5))
                b = bank_free(pe, stage, sg(d, 6), i)
                for m in range(PAIRS):
                    ins = nc.tensor.transpose(b[:, m * P:(m + 1) * P], b_[:, m, :], ident[:])
                full(ins, sg(d, 6))
                pairs(7, pr(v_), lambda m: stacked[:], CH)
                yield
                g = 8
                for lev in range(1, 6):
                    pe.wait_ge(s("ntm_ready%d" % d), i * 5 + (5 * base + lev))
                    pe.wait_ge(s("t_ready%d" % d), i * 6 + (6 * base + lev))
                    pairs(g, sl(NTm), sl(Tm))
                    yield
                    copied(pe, stage, sg(d, g), i)
                    if lev < 5:
                        pairs(g + 1, sl(TT), sl(Pm))
                        pairs(g + 2, sl(Pm), sl(TT))
                    else:
                        pairs(g + 1, sl(Pm), sl(TT))
                    g += 3
                    yield
                pe.wait_ge(s("state_ready%d" % d), i + (base + 1))
                if d == 1:
                    pe.wait_ge(s("state_scaled"), i + (base + 1))
                copied(pe, stage, sg(d, 7), i)
                copied(pe, stage, sg(d, 2), i)
                b = bank_free(pe, stage, sg(d, 22), i)
                for m in range(PAIRS):
                    o = b[:, m * CH:(m + 1) * CH]
                    mm(o, a_[:, m, :], S[:, m, :], start=True, stop=False)
                    ins = mm(o, KT[:, m * P:(m + 1) * P], Vt[:, m * CH:(m + 1) * CH], start=False, stop=True)
                full(ins, sg(d, 22))
                yield
                pe.wait_ge(s("t_ready%d" % d), i * 6 + (6 * base + 6))
                copied(pe, stage, sg(d, 22), i)
                pairs(23, sl(TT), sl(Xt, CH), CH)
                yield
                copied(pe, stage, sg(d, 23), i)
                for g in range(3, 7):
                    copied(pe, stage, sg(d, g), i)
                b = bank_free(pe, stage, sg(d, 24), i)
                for m in range(PAIRS):
                    o = b[:, m * CH:(m + 1) * CH]
                    mm(o, r_[:, m, :], S[:, m, :], start=True, stop=False)
                    mm(o, RkT[:, m * P:(m + 1) * P], Vt[:, m * CH:(m + 1) * CH], start=False, stop=False)
                    ins = mm(o, RbT[:, m * P:(m + 1) * P], SA[:, m * CH:(m + 1) * CH], start=False, stop=True)
                full(ins, sg(d, 24))
                b = bank_free(pe, stage, sg(d, 25), i)
                for m in range(PAIRS):
                    o = b[:, m * CH:(m + 1) * CH]
                    mm(o, ktok[:, m * P:(m + 1) * P], Vt[:, m * CH:(m + 1) * CH], start=True, stop=False)
                    ins = mm(o, btok[:, m * P:(m + 1) * P], SA[:, m * CH:(m + 1) * CH], start=False, stop=True)
                full(ins, sg(d, 25))

            for d in range(2):
                pe.wait_ge(s("state_ready%d" % d), 1)
            with pe.Fori(0, 2) as i:
                both(scan_item("scanp", i, d, 0) for d in range(2))
            for d in range(2):
                pe.wait_ge(s("state_ready%d" % d), 3)
                b = bank_free(pe, "state_out", d)
                for m in range(PAIRS):
                    ins = nc.tensor.transpose(b[0:64, m * P:(m + 1) * P], ST[:, 0, d, m, :], ident[:])
                full(ins, d)
            with pe.Fori(0, 4) as i:
                both(scan_item("scans", i, d, 2) for d in range(2))
            b = bank_free(pe, "coef", 6)
            for n in range(PAIRS * NCH):
                pe.wait_ge(s("bonus_exp"), n + 1)
                ins = mm(b[:, n:n + 1], bexp[:, n % 2, :], ones[:, 0:1], start=True, stop=True)
                if n < PAIRS * NCH - 1:
                    ins.then_inc(s("bonus_mm"), 1)
            full(ins, 6)

            for part, name in enumerate(("vexp_ready", "yexp_ready")):
                for c in range(NCH):
                    pe.wait_ge(s(name), c + 1)
                    b = bank_free(pe, "yT", NCH * part + c)
                    for m in range(PAIRS):
                        ins = mm(b[:, m * CH:(m + 1) * CH], zexp[:, c % 2, m, :], stacked[:], start=True, stop=True)
                        if (part, c, m) == (0, 0, 0):
                            hand_back(ins, len(SCRATCH))
                    full(ins, NCH * part + c)
            gate_rows("gate0", 0)
            for g in range(NCH, 2 * NCH):
                copied(pe, "yT", g)
            copied(pe, "att", 5, MLA_HEADS - 1)
            out_product(0)

            def peer(l):
                norm_transposes("norm%db" % l)
                pe.wait_ge(s("x_parts"), 3 * SPLIT["norm%db" % l] + 3)
                pe.wait_ge(s("subkeys_in"), l + 1)
                for j in range(4):
                    for m in range(4):
                        a = 4 * j + m
                        split_product("wk%d" % l, WQ[a], a, back=m == 0)
                        if a > 0:
                            key_products(l, a - 1)
                key_products(l, SIDES - 1)
                for t in range(TILES):
                    if l == 0:
                        adaln_jobs("sel0", t)
                    pe.wait_ge(s("picked%d" % l), t + 1)
                    b = bank_free(pe, "sel%d" % l, SELG[l], t)
                    for n in range(3):
                        ins = nc.tensor.transpose(b[:, n * P:(n + 1) * P], pick[:, n, :], ident[:])
                        if n == 0 and t == (TILES - 1, 0)[l]:
                            hand_back(ins)
                    full(ins, SELG[l])
                for g in range(6):
                    bank_free(pe, "hot%d" % l, g)
                for g in (6, 7):
                    pe.wait_ge(s("bank_free%d" % g), FIRST["hot%d" % l][g])
                hot(l)

            def key_products(l, a):
                copied(pe, "wk%d" % l, WQ[a])
                b = bank_free(pe, "wk%d" % l, KEYG[a])
                for t in range(TILES):
                    ins = mm(b[:, t * P:(t + 1) * P], qT[:, a, t * P:(t + 1) * P], subkeys[:, a, :],
                             start=True, stop=True)
                full(ins, KEYG[a])

            def hot(l):
                j0 = JOB[("uv", l)]
                c0 = P * l
                g0 = SLICES * NG * l

                def group(g, par):
                    pe.wait_ge(s("onehots"), g + 1)
                    at_least(pe, "w_copied", g)
                    for t in range(BUILD):
                        ins = mm(psum[:, 7, 3 * SLICE * t:3 * SLICE * (t + 1)], ohA[:, par, :, t],
                                 ohB[:, par].rearrange("p m n t -> p (m n) t")[:, :, t], start=True, stop=True)
                    ins.then_inc(s("w_ready"), 1)

                def products(out, a, b, start, stop, used=False):
                    for n, (ka, kb) in enumerate(((0, 0), (0, 1), (1, 0))):
                        ins = mm(out, a[ka], b[kb], start=start and n == 0, stop=stop and n == 2,
                                 skip_group_check=True)
                        if used and n == 0:
                            ins.then_inc(s("slot_used"), 1)
                    return ins

                def v_tile(par, t, start=False, stop=False, used=False):
                    for h in range(2):
                        ins = products(psum[:, 2 * t + h, :], [gs[:, par, a, t * P:(t + 1) * P] for a in range(2)],
                                       [vs[:, par, b, 512 * h:512 * h + 512] for b in range(2)],
                                       start, stop, used and h == 0)
                        if stop:
                            full(ins, 2 * t + h)
                    return ins

                def v_waits(n):
                    pe.wait_ge(s("g_lo"), n + 1)
                    pe.wait_ge(s("v_lo"), n + 1)

                def step(lin, sl, j, u, par, where):
                    n = lin(STEPS, c0 + u)
                    g = lin(STEPS * PER_STEP, g0 + NG + PER_STEP * u)
                    build = sl is not None
                    pe.wait_ge(s("u_lo"), n + 1)
                    at_least(pe, "gelu_done", n)
                    for k in range(KD):
                        ins = products(psum[:, 6, 0:T], [us[:, u % 2, a, k * P:(k + 1) * P] for a in range(2)],
                                       [xs[:, b, k, :] for b in range(2)], k == 0, k == KD - 1)
                        if k == KD // 2 - 1 and build:
                            group(g, u % 2)
                    ins.then_inc(s("h_ready"), 1)
                    if where != "first":
                        v_waits(n - 1)
                    for t in range(TILES):
                        used = t == 1 and u % 2 == 1 and where != "end"
                        if used:
                            pe.wait_ge(s("v_lo"), n + 1)
                        if where != "first":
                            ins = v_tile((u + 1) % 2, t, start=isinstance(n, int) and n == c0 + 1, used=used)
                            if t == TILES - 1:
                                ins.then_inc(s("v_done"), 1)
                        if build and t != 1:
                            group(g + (1 if t == 0 else 2), (u + 1 + t // 2) % 2)

                def first_group(g, par):
                    pe.wait_ge(s("onehots"), g + 1)
                    at_least(pe, "w_copied", g - 1)
                    for t in range(BUILD):
                        for m in range(3):
                            ins = mm(psum[:, 6 + par, SLICE * t:SLICE * (t + 1)], ohA[:, par, :, t],
                                     ohB[:, par, m, :, t], start=m == 0, stop=m == 2)
                    ins.then_inc(s("w_ready"), 1)
                first_group(g0, 0)
                first_group(g0 + 1, 1)
                with pe.Fori(1, NG // 2) as i:
                    for par in range(2):
                        first_group(i * 2 + (g0 + par), par)
                pe.wait_ge(s("w_copied"), g0 + NG)
                expert_steps(pe, step)
                v_waits(c0 + P - 1)
                for t in range(TILES):
                    v_tile(1, t, stop=True)

            peer(0)
            gate_rows("gate0b", 0)

            norm_transposes("norm1")
            pe.wait_ge(s("x_parts"), 3 * SPLIT["norm1"] + 3)
            for j in range(6):
                for m in range(4):
                    split_product("in1", 4 * j + m, 4 * j + m, back=j > 0 and m == 0)
            job_f, job_d = JOB[("filter", 1)], JOB[("dft", 1)]
            fw = slot(job_f)
            w3, zpos, w1, w2 = fw[0:64, 0:2048], fw[0:33, 2048:2432], fw[0:33, 2432:2496], fw[0:64, 2496:2560]
            landed(pe, job_f)
            b = bank_free(pe, "hid", 0)
            full(mm(b[0:64, 0:T], w1, zpos, start=True, stop=True), 0)
            pe.wait_ge(s("hid_ready"), 1)
            b = bank_free(pe, "hid", 1)
            full(mm(b[0:64, 0:T], w2, hid[0:64, 0, :], start=True, stop=True), 1)
            pe.wait_ge(s("hid_ready"), 2)
            for t in range(TILES):
                for n in range(4):
                    b = bank_free(pe, "filt", 4 * t + n)
                    full(mm(b, hid[0:64, 1, t * P:(t + 1) * P], w3[:, 512 * n:512 * n + 512], start=True, stop=True),
                         4 * t + n)
            na = 0
            pe.wait_ge(s("abs_ready"), 12)
            for seq, tiles in ((0, (1, 2)), (1, (0,))):
                for h in range(2):
                    b = bank_free(pe, "norm_f", 2 * seq + h)
                    n = 2 * len(tiles)
                    for m in range(n):
                        ins = mm(b, ones[:], absf[:, na, :], start=m == 0, stop=m == n - 1)
                        na += 1
                    full(ins, 2 * seq + h)
            dft = slot(job_d)
            landed(pe, job_d)
            Fz = [dft[:, 0:1024].rearrange("p (a f) -> p a f", a=2), dft[:, 3072:3328].rearrange("p (a f) -> p a f", a=1)]
            Fb = [dft[:, 1024:2048].rearrange("p (a f) -> p a f", a=2), dft[:, 3328:3584].rearrange("p (a f) -> p a f", a=1)]
            Gi = [dft[:, 2048:3072].rearrange("p (a f) -> p a f", a=4), dft[:, 3584:3840].rearrange("p (a f) -> p a f", a=2)]
            SEQ = ((0, (1, 2), 0, 4), (1, (0,), 4, 2))

            def transform(stage, parts):
                for sq_, tiles, f0, nf in SEQ:
                    for f in range(nf):
                        for h in range(2):
                            g = 2 * (f0 + f) + h
                            b = bank_free(pe, stage, g)
                            todo = [(mat[sq_][:, a, f * P:(f + 1) * P], src(t, h)) for mat, src in parts
                                    for a, t in enumerate(tiles)]
                            for n, (lhsT, rhs) in enumerate(todo):
                                ins = mm(b, lhsT, rhs, start=n == 0, stop=n == len(todo) - 1)
                                if stage == "filtF" and g == 0 and n == 0:
                                    hand_back(ins, 2)
                            full(ins, g)
            transform("filtF", [(Fz, lambda t, h: filt[:, t, 512 * h:512 * h + 512]),
                                (Fb, lambda t, h: filt[:, t, D + 512 * h:D + 512 * h + 512])])
            pe.wait_ge(s("zin_ready"), KD)
            copied(pe, "filtF", 11)
            for t in range(TILES):
                for h in range(2):
                    b = bank_free(pe, "zT", 2 * t + h)
                    for k in range(4):
                        ins = nc.tensor.transpose(b[:, k * P:(k + 1) * P], zinT[:, 4 * h + k, t * P:(t + 1) * P], ident[:])
                    full(ins, 2 * t + h)
            for g in range(6):
                copied(pe, "zT", g)
            transform("zF", [(Fz, lambda t, h: z[:, t, 512 * h:512 * h + 512])])
            for k in range(KD):
                pe.wait_ge(s("spectra_ready"), 1 + k // 4)
                b = bank_free(pe, "conv", k)
                for sq_, tiles, f0, nf in SEQ:
                    n = len(tiles) * P
                    o = tiles[0] * P
                    for f in range(nf):
                        ins = mm(b[:, o:o + n], zF[:, f0 + f, k * P:(k + 1) * P], Gi[sq_][:, f, :],
                                 start=f == 0, stop=f == nf - 1)
                full(ins, k)
            gate_rows("gate1", 1)
            pe.wait_ge(s("conv_out"), KD)
            out_product(1)
            peer(1)
            gate_rows("gate1b", 1)

        @block.vector
        def _(dve):
            V = nc.vector
            L, enter = chain(dve, "dve_chain")
            normed = [0]
            x_new = [0]

            def rms(ss, n, count, eps=EPS):
                a = stat[:, ss:ss + n]
                V.tensor_scalar(a, a, 1.0 / count, eps, ALU.mult, ALU.add).then_inc(s("to_root"), 1)
                roots[0] += 1
                dve.wait_ge(s("rooted"), roots[0])
                L(V.reciprocal(a, a))
            roots = [0]

            def norm(stage, l, part):
                no = NORM_NO[stage]
                o = COLS["g"] + 8 * (2 * l + part)
                L(V.tensor_scalar(gsc[:], modc[:, l, 24 * part + 8:24 * part + 16, :], 1.0, None, ALU.add))
                tell(dve, V.tensor_tensor(gsc[:], gsc[:], bc(cols[:, o:o + 8], 2), ALU.mult), "gsc_ready", no + 1)
                dve.wait_ge(s("x_squares"), no + 1)
                rms(0, 3, D)
                for t in range(TILES):
                    if t == 2:
                        bank_full(dve, stage, 1)
                    tell(dve, V.tensor_scalar((xn, xn2)[t % 2], x[:, t, :], stat[:, t:t + 1], None, ALU.mult),
                              "normed", no * TILES + t + 1)
                def x_lo(t):
                    c = slice(t * P, (t + 1) * P)
                    dve.wait_ge(s("x_hi"), 3 * SPLIT[stage] + t + 1)
                    tell(dve, V.tensor_tensor(xs[:, 1, :, c], hT[:, :, c], xs[:, 0, :, c].bitcast(F32),
                                              ALU.subtract), "x_parts", 3 * SPLIT[stage] + t + 1)
                for t in range(TILES):
                    b = bank_full(dve, stage, 2 * t + 1)
                    c = 0 if t == 0 else 1
                    for j in range(4):
                        ins = V.tensor_scalar(hT[:, 4 + j, t * P:(t + 1) * P], b[:, j * P:(j + 1) * P],
                                              gsc[:, 4 + j, c:c + 1], modc[:, l, 24 * part + 4 + j, c:c + 1],
                                              ALU.mult, ALU.add)
                    free(ins, 2 * t + 1)
                    if t > 0:
                        x_lo(t - 1)
                x_lo(TILES - 1)

            def gate_columns(stage, l, part):
                for c in range(2):
                    ins = V.tensor_copy(gate_bc[:, 8 * c:8 * c + 8, :], bc(modc[:, l, 8 * part:8 * part + 8, c], P))
                    if c == 0:
                        L(ins)
                    else:
                        tell(dve, ins, "gate_cols", GATE_NO[stage] + 1)

            def add_out(stage, gate, order):
                for n in (1, 3):
                    copied(dve, gate, GROUPS[gate][n])
                for g, t, h in order:
                    b = bank_full(dve, stage, g)
                    c = 0 if t == 0 else 1
                    tmp = (xn, xn2)[g % 2][:, 0:512]
                    ins = V.tensor_tensor(tmp, b, gate_row[:, c, 512 * h:512 * h + 512], ALU.mult)
                    free(ins, g)
                    copied(dve, stage, g)
                    xs = x[:, t, 512 * h:512 * h + 512]
                    ins = V.tensor_tensor(xs, xs, tmp, ALU.add)
                    if g == 5:
                        x_new[0] += 1
                        tell(dve, ins, "x_new", x_new[0])
                    else:
                        L(ins)

            dve.wait_ge(s("inputs"), 16 * 8)
            L(V.memset(ones[:], 1.0))
            dve.wait_ge(s("cond_sig"), 1)
            cond = cols[:, COLS["cond"]:COLS["cond"] + 16].rearrange("p (k c) -> p k c", k=KD)
            tell(dve, V.tensor_tensor(condT[:], condT[:], cond, ALU.mult), "cond_ready", 1)
            L(V.tensor_copy(rep16.rearrange("p (n t) -> p n t", t=BUILD), bc(iota[:], BUILD)))
            for n in range(4, 8):
                copied(dve, "mod0", n)
            norm("norm0", 0, 0)

            bank_full(dve, "norm0", 5)
            tell(dve, V.memset(pad, 0.0), "pad_zero", 1)
            mu = cols[:, COLS["mu"]:COLS["mu"] + 14]
            L(V.tensor_scalar(stat[:, 32:46], mu, 0.5, None, ALU.mult))
            L(V.tensor_scalar(stat[:, 46:60], mu, -1.0, 1.0, ALU.mult, ALU.add))
            for g in range(14):
                dst = rkv[:, g, :] if g < 12 else (wdad, gd)[g - 12]
                pd = pad[:, g % 2, :]
                dve.wait_ge(s("bank_free%d" % (g % 8)), use_of("in0", g) + 1)
                L(V.tensor_tensor(padt[:, 1:386], pd[:, 0:385], pd[:, 2:387], ALU.add))
                L(V.tensor_scalar(padt[:, 1:386], padt[:, 1:386], stat[:, 32 + g:33 + g], None, ALU.mult))
                om = stat[:, 46 + g:47 + g]
                L(V.scalar_tensor_tensor(dst[:, 0:P], pd[:, 1:129], om, padt[:, 1:129], ALU.mult, ALU.add))
                tell(dve, V.scalar_tensor_tensor(dst[:, P:T], pd[:, 130:386], om, padt[:, 130:386], ALU.mult, ALU.add),
                          "shifted", g + 1)

            dve.wait_ge(s("mixer_params"), 16 * 8)
            dve.wait_ge(s("latent_squares"), 1)
            L(V.tensor_scalar(stat[:, 3:6], stat[:, 3:6], 256.0 / 128.0, None, ALU.mult))
            rms(0, 6, 256)
            for t, kt in enumerate((0, 2, 3)):
                L(V.tensor_copy(kpe[:, kt, :], mla[:, t, 384:448]))
                L(V.scalar_tensor_tensor(ckv[:, kt, :], mla[:, t, 256:384], stat[:, 3 + t:4 + t], rows[:, 256:384],
                                         ALU.mult, ALU.mult))
                ins = V.scalar_tensor_tensor(qc[:, t, :], mla[:, t, 0:256], stat[:, t:t + 1], rows[:, 0:256],
                                             ALU.mult, ALU.mult)
                if t < 2:
                    L(ins)
            tell(dve, ins, "latents", 1)
            for t in range(KEYTILES):
                L(V.tensor_copy(kx[:, t, :, P:QK], head_bc(kpe[:, t, :], 64, MLA_HEADS)))
                for h in range(2):
                    g = 6 + 2 * t + h
                    b = bank_full(dve, "up", g).rearrange("p (h n) -> p h n", h=2)
                    L(V.tensor_copy(kx[:, t, 2 * h:2 * h + 2, 0:P], b[:, :, 0:P]))
                    free(V.tensor_copy(vx[:, t, 2 * h:2 * h + 2, :], b[:, :, P:2 * P]), g)
                    copied(dve, "up", g)
            for g in range(6):
                copied(dve, "up", g)
            for buf, n, o, row in ((q, 12, 6, "qn"), (kx, 16, 6, "kn")):
                a = buf.rearrange("p t h c -> p (t h) c")
                sv = sq[:, 0:n * QK].rearrange("p (r c) -> p r c", r=n)
                L(V.tensor_tensor(sv, a, a, ALU.mult))
                L(V.tensor_reduce(stat[:, o:o + n], sv, AX.X, ALU.add))
                rms(o, n, QK)
                L(V.tensor_tensor(a, a, bc(stat[:, o:o + n], QK), ALU.mult))
                r0 = ROWS[row][0]
                L(V.tensor_tensor(a, a, head_bc(rows[:, r0:r0 + QK], QK, n), ALU.mult))
            for n_, (buf, t0) in enumerate(((q, 1), (kx, 2))):
                x1, x2 = (buf[:, t0:t0 + 2, :, P + e:QK:2] for e in range(2))
                cs, sn = (rope[:, e].unsqueeze(2).to_broadcast([P, 2, MLA_HEADS, 32]) for e in range(2))
                for n, (a, w) in enumerate(((x1, cs), (x2, sn), (x1, sn), (x2, cs))):
                    L(V.tensor_tensor(rtmp[:, n], a, w, ALU.mult))
                L(V.tensor_tensor(x1, rtmp[:, 0], rtmp[:, 1], ALU.subtract))
                ins = V.tensor_tensor(x2, rtmp[:, 2], rtmp[:, 3], ALU.add)
                if n_ == 0:
                    L(ins)
            tell(dve, ins, "heads_ready", 1)
            for h in range(MLA_HEADS):
                for part in (2, 3):
                    g = 4 * h + part
                    b = bank_full(dve, "headT", g)
                    if part == 2:
                        free(V.tensor_copy(kTn[:, h, :], b), g)
                    else:
                        free(V.tensor_copy(kTr[0:64, h, :], b[0:64, :]), g)
            scale = float(QK) ** -0.5
            for h in range(MLA_HEADS):
                for t in range(TILES):
                    n = P if t == 0 else 3 * P
                    b = bank_full(dve, "att", t, h)
                    m = stat[:, 3 * h + t:3 * h + t + 1]
                    L(V.tensor_reduce(m, b[:, 0:n], AX.X, ALU.max, negate=True))
                    tell(dve, V.tensor_scalar(m, m, scale, None, ALU.mult), "row_max", 3 * h + t + 1)
                dve.wait_ge(s("exps"), 3 * h + 3)
                r = stat[:, 12 + 3 * h:15 + 3 * h]
                L(V.reciprocal(r, r))
                for t, (o, n) in enumerate(((0, 1), (1, 3), (4, 3))):
                    ins = V.tensor_scalar(prob[:, o:o + n, :], prob[:, o:o + n, :], r[:, t:t + 1], None, ALU.mult)
                    if t < 2:
                        L(ins)
                tell(dve, ins, "probs", h + 1)
                b = bank_full(dve, "att", 4, h)
                free(V.tensor_copy(probT[:, 4:7, :], b[:, 0:384].rearrange("p (n c) -> p n c", n=3)), 4)
                copied(dve, "att", 4, h)

            copied(dve, "att", 5, MLA_HEADS - 1)
            tell(dve, V.memset(lora_rhs, 0.0), "lora_zero", 1)
            for m in range(PAIRS):
                L(V.tensor_scalar(kk[:, m, :], rkv[:, 4 + m, :], col("k_k", m), None, ALU.mult))
            tell(dve, V.tensor_tensor(ld, kk, kk, ALU.mult), "kk_squares", 1)
            for m in range(PAIRS):
                copied(dve, "knorm", m)
            L(V.tensor_scalar(cum, cum, 1e-12, None, ALU.max))
            L(V.reciprocal(cum, cum))
            tell(dve, V.tensor_tensor(kk, kk, cum, ALU.mult), "kk_ready", 1)
            decay = -float(np.exp(np.float64(-0.5)))
            for d in range(2):
                for m in range(PAIRS):
                    copied(dve, "lora", 8 * d + m)
                    copied(dve, "lora", 8 * d + 4 + m)
                L(V.tensor_scalar(ld, ld, decay, None, ALU.mult))
                for m in range(PAIRS):
                    L(V.tensor_tensor_scan(cum[:, m, :], scanmask, ld[:, m, :], 0.0, ALU.mult, ALU.add))
                tell(dve, V.tensor_tensor(cumx, cum, ld, ALU.subtract), "cums", d + 1)
                dve.wait_ge(s("decays"), d + 1)
                tr, ta, tb, tk = (tilde[:, 4 * d + n] for n in range(4))
                L(V.tensor_tensor(tr, tr, rkv[:, 0:4, :], ALU.mult))
                L(V.scalar_tensor_tensor(ta, ta, -1.0, kk, ALU.mult, ALU.mult))
                L(V.tensor_copy(tk, tb))
                L(V.tensor_tensor(tb, tb, kk, ALU.mult))
                L(V.tensor_tensor(tb, tb, lr, ALU.mult))
                for m in range(PAIRS):
                    L(V.tensor_scalar(lr[:, m, :], lr[:, m, :], -1.0, col("k_a", m), ALU.add, ALU.mult))
                kd = cum
                L(V.scalar_tensor_tensor(kd, lr, 1.0, rkv[:, 4:8, :], ALU.add, ALU.mult))
                L(V.tensor_tensor(tk, tk, kd, ALU.mult))
                if d == 0:
                    tell(dve, V.tensor_copy(ksum, kd), "dir_done", 1)
                else:
                    L(V.tensor_tensor(ksum, ksum, kd, ALU.add))
            L(V.tensor_tensor(bonus_w, ksum, rkv[:, 0:4, :], ALU.mult))
            for m in range(PAIRS):
                ins = V.tensor_scalar(bonus_w[:, m, :], bonus_w[:, m, :], col("r_k", m), None, ALU.mult)
                if m < PAIRS - 1:
                    L(ins)
            L(ins)
            L(V.memset(ST[:, 0], 0.0))
            L(V.memset(y, 0.0))
            tell(dve, V.memset(scan_mem[0][0], 0.0), "state_ready0", 1)
            for g in range(4):
                d, h = g // 2, g % 2
                b = bank_full(dve, "state_in", g)
                free(V.tensor_copy(ST[:, 1, d, 2 * h:2 * h + 2, :], b[:, 0:2 * CH].rearrange("p (m c) -> p m c", m=2)), g)
                copied(dve, "state_in", g)
            dve.wait_ge(s("slot_used"), SCRATCH[1] - RING + 1)
            tell(dve, V.memset(scan_mem[1][0], 0.0), "state_ready1", 1)
            def scan_item(stage, i, d, base, chunk, seq):
                ex, NT, NTm, Tm, TT, Pm, KT, RkT, RbT, ktok, btok, Vt, Xt, SA = scan_mem[d]
                S = ST[:, seq, d]
                c = chunk

                def expand(n):
                    src = tilde[:, 4 * d + n]
                    L(V.tensor_copy(ex[0:64, n, :, 0:CH], src[0:64, :, bass.ts(c, CH)]))
                    V.tensor_copy(ex[64:P, n, :, CH:P], src[64:P, :, bass.ts(c, CH)]).then_inc(s("expanded%d" % d), 1)
                el = elast[:, d, :, bass.ts(c, 1)].to_broadcast([P, PAIRS, CH])
                for n in range(3):
                    expand(n)
                yield
                dve.wait_ge(s("state_ready%d" % d), i + (base + 1))
                if d == 1:
                    V.tensor_tensor(S, S, el, ALU.mult).then_inc(s("state_scaled"), 1)
                    dve.wait_ge(s("state_scaled"), i + (base + 1))
                m0 = head_bc(masks[:, (6, 0)[d], :], P, PAIRS)
                m0T = head_bc(masks[:, (0, 6)[d], :], P, PAIRS)
                eye = head_bc(ident[:], P, PAIRS)
                b = bank_full(dve, stage, sg(d, 0), i)
                free(V.tensor_tensor(blocks(Tm), blocks(b), m0, ALU.mult), sg(d, 0))
                copied(dve, stage, sg(d, 1), i)
                L(V.tensor_tensor(blocks(TT), blocks(NT), m0T, ALU.mult))
                copied(dve, stage, sg(d, 0), i)
                L(V.tensor_tensor(blocks(Tm), blocks(Tm), eye, ALU.add))
                V.tensor_tensor(blocks(TT), blocks(TT), eye, ALU.add).then_inc(s("t_ready%d" % d), 1)
                for n, (dst, m) in enumerate(((KT, 12 + 2 * d), (RkT, 13 + 2 * d), (RbT, 13 + 2 * d))):
                    b = bank_full(dve, stage, sg(d, 2 + n), i)
                    free(V.tensor_tensor(blocks(dst), blocks(b), head_bc(masks[:, m, :], P, PAIRS), ALU.mult), sg(d, 2 + n))
                dve.wait_ge(s("t_ready%d" % d), i * 6 + (6 * base + 1))
                g = 9
                for lev in range(1, 6):
                    yield
                    if lev < 5:
                        b = bank_full(dve, stage, sg(d, g), i)
                        free(V.tensor_tensor(Tm, Tm, b, ALU.add), sg(d, g))
                        copied(dve, stage, sg(d, g), i)
                        g += 1
                    b = bank_full(dve, stage, sg(d, g), i)
                    free(V.tensor_tensor(TT, TT, b, ALU.add), sg(d, g))
                    copied(dve, stage, sg(d, g), i)
                    g += 2
                    V.tensor_copy(stat[:, 62:63], ones[:, 0:1]).then_inc(s("t_ready%d" % d), 1)
                    dve.wait_ge(s("t_ready%d" % d), i * 6 + (6 * base + lev + 1))
                yield
                b = bank_full(dve, stage, sg(d, 24), i)
                yv = y[:, bass.ts(c, 1)].rearrange("p o m v -> p (o m v)")
                free(V.tensor_tensor(yv, yv, b[:, 0:256], ALU.add), sg(d, 24))
                b = bank_full(dve, stage, sg(d, 25), i)
                Sf = S.rearrange("p m v -> p (m v)")
                copied(dve, stage, sg(d, 24), i)
                ins = V.tensor_tensor(Sf, Sf, b[:, 0:256], ALU.add)
                free(ins, sg(d, 25))
                copied(dve, stage, sg(d, 25), i)
                if d == 0:
                    ins = V.tensor_tensor(S, S, el, ALU.mult)
                else:
                    ins = V.tensor_copy(stat[:, 61:62], ones[:, 0:1])
                ins.then_inc(s("state_ready%d" % d), 1)

            c0, per = enter(0), 2 * (3 + 2)
            with dve.Fori(0, 2) as i:
                back = dve.snap(1 - i)
                enter(i * per + c0)
                both(scan_item("scanp", i, d, 0, (i, back)[d], 0) for d in range(2))
            with dve.Fori(0, 4) as i:
                back = dve.snap(5 - i)
                enter(i * per + (c0 + 2 * per))
                both(scan_item("scans", i, d, 2, (i + 2, back)[d], 1) for d in range(2))
            enter(c0 + 6 * per)

            bank_full(dve, "scans", sg(1, 25), 3)
            L(V.memset(bexp, 0.0))
            tell(dve, V.memset(zexp, 0.0), "scan_done", 1)
            yr = y.rearrange("p c m v -> p (c m) v")
            ycr, ysr = (a.rearrange("p c m v -> p (c m) v") for a in (yc, ysq))
            n = NCH * PAIRS
            mean, var = stat[:, 0:n], stat[:, n:2 * n]
            L(V.tensor_reduce(mean, yr, AX.X, ALU.add))
            L(V.tensor_scalar(mean, mean, 1.0 / CH, None, ALU.mult))
            L(V.tensor_tensor(ycr, yr, bc(mean, CH), ALU.subtract))
            L(V.tensor_tensor(ysr, ycr, ycr, ALU.mult))
            L(V.tensor_reduce(var, ysr, AX.X, ALU.add))
            rms(n, n, CH, LNX_EPS)
            L(V.tensor_tensor(ycr, ycr, bc(var, CH), ALU.mult))
            dve.wait_ge(s("lnx_loaded"), 16 * 4)
            for m, op in ((0, ALU.mult), (1, ALU.add)):
                L(V.tensor_tensor(yc, yc, lnx[:, m].unsqueeze(1).to_broadcast([P, NCH, PAIRS, CH]), op))

            bank_full(dve, "coef", 6)
            free(V.tensor_copy(coef[:].rearrange("p m c -> p (m c)"), psum[:, 6, 0:PAIRS * NCH]), 6)
            copied(dve, "coef", 6)
            for c in range(NCH):
                b = bank_full(dve, "yT", c)
                cf = coef[:, :, c:c + 1].to_broadcast([P, PAIRS, CH])
                free(V.tensor_tensor(vtok[:, c], b[:, 0:256].rearrange("p (m v) -> p m v", m=PAIRS), cf, ALU.mult), c)
                copied(dve, "yT", c)
                L(V.tensor_tensor(yc[:, c], yc[:, c], vtok[:, c], ALU.add))
            copied(dve, "lora", 19)

            def expand_y(c):
                if c > 1:
                    bank_full(dve, "yT", NCH + c - 2)
                L(V.tensor_copy(zexp[0:64, c % 2, :, 0:CH], yc[0:64, c]))
                tell(dve, V.tensor_copy(zexp[64:P, c % 2, :, CH:P], yc[64:P, c]), "yexp_ready", c + 1)
            expand_y(0)
            for c in range(NCH):
                if c < NCH - 1:
                    expand_y(c + 1)
                g = NCH + c
                b = bank_full(dve, "yT", g)
                free(V.tensor_tensor(hT[:, 0:4, c * CH:(c + 1) * CH], b[:, 0:256].rearrange("p (m v) -> p m v", m=PAIRS),
                                     hT[:, 0:4, c * CH:(c + 1) * CH], ALU.mult), g)
            for n in range(4, 8):
                copied(dve, "mod0b", n, 1)
            gate_columns("gate0", 0, 2)
            add_out("out0", "gate0", [(3 * j + t, t, j) for j in range(2) for t in range(TILES)])

            def peer(l):
                norm("norm%db" % l, l, 1)
                def best16(lists):
                    for v, o, oi in lists:
                        ins = V.max(o[:, 0:8], v)
                    L(ins)
                    for v, o, oi in lists:
                        ins = V.max_index(oi[:, 0:8], o[:, 0:8], v)
                    L(ins)
                    for v, o, oi in lists:
                        ins = V.match_replace(v, o[:, 0:8], v, -3.0e38)
                    L(ins)
                    for v, o, oi in lists:
                        ins = V.max(o[:, 8:16], v)
                    L(ins)
                    for v, o, oi in lists:
                        ins = V.max_index(oi[:, 8:16], o[:, 8:16], v)
                    L(ins)

                for a in range(SIDES):
                    copied(dve, "wk%d" % l, KEYG[a])
                    best16([(sc[:, a, t, :], top[:, t, a, :], topi[:, t, a, :].bitcast(U32)) for t in range(TILES)])
                L(V.tensor_copy(places.rearrange("p (m n) -> p m n", m=TOPK), bc(iota[:, 0:TOPK], P)))
                for t in range(TILES):
                    L(V.tensor_copy(topif[:, t], topi[:, t].bitcast(U32)))
                    tv = top[:, t].rearrange("p (h e) k -> p h e k", e=2)
                    ti = topif[:, t].rearrange("p (h e) k -> p h e k", e=2)
                    for i0, ni, nj, o in ((0, NEAR, TOPK, 0), (NEAR, TOPK - NEAR, NEAR, NEAR * TOPK)):
                        sh = [P, HEADS, ni, nj]
                        ins = V.tensor_tensor(cand[:, :, o:o + ni * nj].rearrange("p h (i j) -> p h i j", i=ni),
                                              tv[:, :, 0, i0:i0 + ni].unsqueeze(3).to_broadcast(sh),
                                              tv[:, :, 1, 0:nj].unsqueeze(2).to_broadcast(sh), ALU.add)
                    L(ins)
                    best16([(cand[:, h, :], tops[:, h, :], posu[:, h, :].bitcast(U32)) for h in range(HEADS)])
                    un, ud = posu.rearrange("p h k -> p (h k)").bitcast(U32), dec.bitcast(U32)
                    V.tensor_scalar(ud[:, 0], un, 4, None, ALU.logical_shift_right)
                    V.tensor_scalar(ud[:, 1], un, 2, None, ALU.logical_shift_right)
                    V.tensor_scalar(ud[:, 2], un, 12, None, ALU.bitwise_and)
                    L(V.tensor_scalar(ud[:, 3], un, 3, None, ALU.bitwise_and))
                    L(V.tensor_copy(dec, ud))
                    V.scalar_tensor_tensor(mix[:, 1], dec[:, 0], float(NEAR), dec[:, 2], ALU.is_lt, ALU.mult)
                    L(V.scalar_tensor_tensor(mix[:, 0], dec[:, 1], -12.0, dec[:, 0], ALU.add, ALU.subtract))
                    L(V.scalar_tensor_tensor(mix[:, 0], dec[:, 0], float(NEAR), mix[:, 0], ALU.is_ge, ALU.mult))
                    if t > 0:
                        bank_full(dve, "sel%d" % l, SELG[l], t - 1)
                    for e in range(2):
                        V.tensor_tensor(pos16[e], mix[:, e].rearrange("p (h k) -> p k h", h=HEADS),
                                        dec[:, 3 * e].rearrange("p (h k) -> p k h", h=HEADS), ALU.add)
                        ins = V.tensor_copy(key16[e], ti[:, :, e, :].rearrange("p h m -> p m h"))
                    L(ins)
                    sh4 = [P, TOPK, TOPK, HEADS]
                    for e in range(2):
                        ins = V.tensor_tensor(oh[e], pos16[e].unsqueeze(1).to_broadcast(sh4),
                                              places.rearrange("p (m k h) -> p m k h", m=TOPK, k=TOPK), ALU.is_equal)
                    L(ins)
                    for e in range(2):
                        ins = V.tensor_tensor(oh[e], oh[e], key16[e].unsqueeze(2).to_broadcast(sh4), ALU.mult)
                    L(ins)
                    for n in (8, 4, 2):
                        for e in range(2):
                            ins = V.tensor_tensor(oh[e][:, 0:n], oh[e][:, 0:n], oh[e][:, n:2 * n], ALU.add)
                        L(ins)
                    for e in range(2):
                        ins = V.tensor_tensor(pick[:, e, :].rearrange("p (h k) -> p k h", h=HEADS), oh[e][:, 0],
                                              oh[e][:, 1], ALU.add)
                    L(ins)
                    gt = pick[:, 2, :].rearrange("p (h k) -> p h k", h=HEADS)
                    tell(dve, V.tensor_tensor(gt, tops, tops[:, :, 0:1].to_broadcast([P, HEADS, TOPK]), ALU.subtract),
                              "shifted_tops", 3 * l + t + 1)
                    dve.wait_ge(s("tops_exp"), 3 * l + t + 1)
                    L(V.tensor_reduce(stat[:, 0:8], gt, AX.X, ALU.add))
                    L(V.reciprocal(stat[:, 0:8], stat[:, 0:8]))
                    tell(dve, V.tensor_tensor(gt, gt, bc(stat[:, 0:8], TOPK), ALU.mult), "picked%d" % l, t + 1)
                for t in range(TILES):
                    copied(dve, "sel%d" % l, SELG[l], t)
                L(V.tensor_copy(sel16[:, 0:2, :], sel[:, 0:2, :]))
                rest = sel[:, 2, :]
                for n in range(2, 5):
                    L(V.tensor_copy(sel16[:, n, :], rest))
                    if n < 4:
                        L(V.tensor_tensor(sel[:, 0, :], rest, sel16[:, n, :], ALU.subtract))
                        rest = sel[:, 0, :]
                j0 = JOB[("uv", l)]
                c0 = P * l
                g0 = SLICES * NG * l

                def onehots(g, tok, first, par):
                    at_least(dve, "w_ready", g - 1)
                    sh = [P, SLICE, BUILD]
                    V.tensor_tensor(ohE[:, par], rep16[:, bass.ds(first, SLICE * BUILD)].rearrange(
                        "p (n t) -> p n t", t=BUILD), sel16[:, 1, bass.ds(tok, BUILD)].unsqueeze(1).to_broadcast(sh),
                        ALU.is_equal).then_inc(s("onehot_i2"), 1)
                    sh = [P, P, BUILD]
                    V.tensor_tensor(ohA[:, par], rep16.rearrange("p (n t) -> p n t", t=BUILD),
                                    sel16[:, 0, bass.ds(tok, BUILD)].unsqueeze(1).to_broadcast(sh), ALU.is_equal)
                    dve.wait_ge(s("onehot_i2"), g + 1)
                    sh = [P, 3, SLICE, BUILD]
                    V.tensor_tensor(ohB[:, par], ohE[:, par].unsqueeze(1).to_broadcast(sh),
                                    sel16[:, 2:5, bass.ds(tok, BUILD)].unsqueeze(2).to_broadcast(sh),
                                    ALU.mult).then_inc(s("onehots"), 1)

                def dense(g, tok, par):
                    dve.wait_ge(s("w_ready"), g + 1)
                    V.tensor_reduce(wd[:, par, bass.ds(tok, BUILD), :], psum[:, 7, 0:3 * SLICE * BUILD].rearrange(
                        "p (t m n) -> p t n m", t=BUILD, m=3), AX.X, ALU.add).then_inc(s("w_copied"), 1)

                def step(lin, sl, j, u, par, where):
                    n = lin(STEPS, c0 + u)
                    g = lin(STEPS * PER_STEP, g0 + NG + PER_STEP * u)
                    tok = j * (STEPS * PER_STEP * BUILD) + PER_STEP * BUILD * u
                    build = sl is not None
                    if build:
                        first = sl(SLICE * BUILD, SLICE * BUILD)
                        for k in range(2):
                            onehots(g + k, tok + BUILD * k, first, (u + k) % 2)
                    if build:
                        at_least(dve, "g_made", n)
                        dense(g, tok, 1 - par)
                    if where != "end":
                        u_part(u + 1, n + 1)
                    dve.wait_ge(s("gelu_done"), n + 1)
                    dve.wait_ge(s("w_copied"), sl(NG, g0 + NG) if build else g0 + SLICES * NG)
                    at_least(dve, "g_lo", n - 1)
                    V.tensor_tensor(gw[:, u % 2, :], gel[:, u % 2, :],
                                    wd[:, par, :, bass.ds(j * STEPS + u, 1)].rearrange("p t o -> p (t o)"),
                                    ALU.mult).then_inc(s("g_made"), 1)
                    if build:
                        onehots(g + 2, tok + 2 * BUILD, first, u % 2)
                    dve.wait_ge(s("g_hi"), n + 1)
                    V.tensor_tensor(gs[:, u % 2, 1, :], gw[:, u % 2, :], gs[:, u % 2, 0, :].bitcast(F32),
                                    ALU.subtract).then_inc(s("g_lo"), 1)
                    if build:
                        for k in (1, 2):
                            dense(g + k, tok + BUILD * k, 1 - par)

                def u_part(u, n):
                    dve.wait_ge(s("u_hi"), n + 1)
                    V.tensor_tensor(us[:, u % 2, 1, :], table(j0, u)[0], us[:, u % 2, 0, :].bitcast(F32),
                                    ALU.subtract).then_inc(s("u_lo"), 1)

                onehots(g0, 0, 0, 0)
                onehots(g0 + 1, BUILD, 0, 1)
                with dve.Fori(1, NG // 2) as i:
                    for k in range(2):
                        onehots(i * 2 + (g0 + k), i * (2 * BUILD) + k * BUILD, 0, k)
                u_part(0, c0)
                expert_steps(dve, step)
                dve.wait_ge(s("g_lo"), P * (l + 1))
                gate_columns("gate%db" % l, l, 5)
                add_out("hot%d" % l, "gate%db" % l, [(2 * t + h, t, h) for t in range(TILES) for h in range(2)])

            bank_full(dve, "out0", 5)
            peer(0)

            norm("norm1", 1, 0)
            bank_full(dve, "norm1", 5)
            tell(dve, V.memset(pad1, 0.0), "pad_zero", 2)
            for g in range(24):
                pd = pad1[:, g % 2, :]
                dve.wait_ge(s("bank_free%d" % (g % 8)), use_of("in1", g) + 1)
                k = g % 8
                dst = (x0T[:, k, :], zinT[:, k, :], vtmp)[g // 8]
                L(V.tensor_scalar(padt1[:, 1:386], pd[:, 0:385], col("conv_w", g), col("conv_b", g), ALU.mult, ALU.add))
                L(V.scalar_tensor_tensor(padt1[:, 1:386], pd[:, 1:386], col("conv_w", 24 + g), padt1[:, 1:386],
                                         ALU.mult, ALU.add))
                for (a, b_), o in (((1, 129), 0), ((130, 386), P)):
                    ins = V.scalar_tensor_tensor(dst[:, o:o + b_ - a], pd[:, a + 1:b_ + 1], col("conv_w", 48 + g),
                                                 padt1[:, a:b_], ALU.mult, ALU.add)
                    if o == 0:
                        L(ins)
                tell(dve, ins, "shifted", 14 + g + 1)
                if g >= 16:
                    tell(dve, V.tensor_tensor(zinT[:, k, :], zinT[:, k, :], vtmp, ALU.mult), "zin_ready", k + 1)
            V.tensor_copy(stat[:, 62:63], ones[:, 0:1]).then_inc(s("slot_used"), 1)
            dve.wait_ge(s("slot_used"), JOB[("in", 1)] + 6)

            magic, two_pi = 12582912.0, 2 * np.pi
            c1 = float(np.float32(6.28125))
            c2 = float(np.float32(round((two_pi - c1) * 2 ** 20) / 2 ** 20))
            c3 = float(np.float32(two_pi - c1 - c2))
            for n in range(2):
                b = bank_full(dve, "hid", n)
                a, k_ = htmp[0:64, 0, :], htmp[0:64, 1, :]
                free(V.tensor_scalar(a, b[0:64, 0:T], col("f_b1" if n == 0 else "f_b2")[0:64], col("freq")[0:64],
                                     ALU.add, ALU.mult), n)
                copied(dve, "hid", n)
                L(V.tensor_scalar(k_, a, float(1 / two_pi), magic, ALU.mult, ALU.add))
                L(V.tensor_scalar(k_, k_, -magic, None, ALU.add))
                for c in (c1, c2, c3):
                    L(V.scalar_tensor_tensor(a, k_, -c, a, ALU.mult, ALU.add))
                tell(dve, V.tensor_scalar(a, a, 3.1415925, -3.1415925, ALU.min, ALU.max), "sin_in", n + 1)
            job_w = JOB[("window", 1)]
            landed(dve, job_w)
            win = slot(job_w)[:, 0:3072].rearrange("p (t c) -> p t c", t=3)
            for t in range(TILES):
                for n in range(4):
                    g = 4 * t + n
                    b = bank_full(dve, "filt", g)
                    h = n % 2
                    free(V.tensor_tensor(filt[:, t, 512 * n:512 * n + 512], b, win[:, t, 512 * h:512 * h + 512],
                                         ALU.mult), g)
                    copied(dve, "filt", g)
            L(V.memset(filt[0:1, 0, D:2 * D], 0.0))
            tell(dve, V.memset(filt[0:1, 1, D:2 * D], 0.0), "filters", 1)
            for g in range(4):
                b = bank_full(dve, "norm_f", g)
                free(V.reciprocal(rnorm[:, g // 2, 512 * (g % 2):512 * (g % 2) + 512], b), g)
                copied(dve, "norm_f", g)
            for g in range(12):
                f, h = g // 2, g % 2
                b = bank_full(dve, "filtF", g)
                seq = 0 if f < 4 else 1
                free(V.tensor_tensor(filtF[:, f, 512 * h:512 * h + 512], b, rnorm[:, seq, 512 * h:512 * h + 512],
                                     ALU.mult), g)
                copied(dve, "filtF", g)
            for h in range(2):
                c = slice(512 * h, 512 * h + 512)
                for n, (re, im, special) in enumerate(((0, 2, True), (1, 3, False), (4, 5, True))):
                    copied(dve, "zF", 2 * re + h)
                    copied(dve, "zF", 2 * im + h)
                    zr, zi, hr, hi_ = zF[:, re, c], zF[:, im, c], filtF[:, re, c], filtF[:, im, c]
                    p0, p1 = prod[:, 0, c], prod[:, 1, c]
                    V.tensor_tensor(p0, zr, hr, ALU.mult)
                    L(V.tensor_tensor(p1, zi, hi_, ALU.mult))
                    V.tensor_tensor(zr, zr, hi_, ALU.mult)
                    L(V.tensor_tensor(zi, zi, hr, ALU.mult))
                    L(V.tensor_tensor(zi, zi, zr, ALU.add))
                    ins = V.tensor_tensor(zr, p0, p1, ALU.subtract)
                    if special:
                        L(ins)
                        V.tensor_copy(zr[0:1, :], p0[0:1, :])
                        ins = V.tensor_copy(zi[0:1, :], p1[0:1, :])
                    if n < 2:
                        L(ins)
                tell(dve, ins, "spectra_ready", h + 1)
            for k in range(KD):
                b = bank_full(dve, "conv", k)
                free(V.scalar_tensor_tensor(zinT[:, k, :], zinT[:, k, :], col("bias", k), b[:, 0:T], ALU.mult, ALU.add), k)
                copied(dve, "conv", k)
                tell(dve, V.tensor_tensor(hT[:, k, :], zinT[:, k, :], x0T[:, k, :], ALU.mult), "conv_out", k + 1)
            gate_columns("gate1", 1, 2)
            add_out("out1", "gate1", [(3 * j + t, t, j) for j in range(2) for t in range(TILES)])
            bank_full(dve, "out1", 5)
            peer(1)
            V.tensor_copy(stat[:, 62:63], ones[:, 0:1]).then_inc(s("y_done"), 1)

        @block.scalar
        def _(act):
            A = nc.scalar.activation
            L, enter = chain(act, "act_chain")
            roots = [0]

            def root(ss, n):
                roots[0] += 1
                act.wait_ge(s("to_root"), roots[0])
                A(stat[:, ss:ss + n], stat[:, ss:ss + n], ACT.Sqrt).then_inc(s("rooted"), 1)

            def norm(stage, l, part):
                no = NORM_NO[stage]
                if no > 0:
                    act.wait_ge(s("x_new"), no)
                for t in range(TILES):
                    ins = A(junk, x[:, t, :], ACT.Square, accum_out=stat[:, t:t + 1])
                    if t < 2:
                        L(ins)
                tell(act, ins, "x_squares", no + 1)
                root(0, 3)
                for n in range(2):
                    weight_hi(("in", "wq")[part], l, n)
                if part == 1:
                    landed(act, JOB[("keys", l)])
                    A(subkeys.rearrange("p a n -> p (a n)"), slot(JOB[("keys", l)])[:, 0:2048],
                      ACT.Copy).then_inc(s("subkeys_in"), 1)
                act.wait_ge(s("gsc_ready"), no + 1)
                for t in range(TILES):
                    c = 0 if t == 0 else 1
                    b = bank_full(act, stage, 2 * t)
                    for k in range(4):
                        ins = A(hT[:, k, t * P:(t + 1) * P], b[:, k * P:(k + 1) * P], ACT.Identity,
                                bias=modc[:, l, 24 * part + k, c:c + 1], scale=gsc[:, k, c:c + 1])
                    free(ins, 2 * t)
                    copied(act, stage, 2 * t)
                    copied(act, stage, 2 * t + 1)
                    A(xs[:, 0, :, t * P:(t + 1) * P], hT[:, :, t * P:(t + 1) * P],
                      ACT.Copy).then_inc(s("x_hi"), 1)

            def weight_hi(name, l, n):
                if n % 4 == 0:
                    landed(act, JOB[(name, l)] + n // 4)
                A(weight_part(n, 0), weight_columns(name, l, n), ACT.Copy).then_inc(s("w_hi"), 1)

            def adaln_jobs(l, stage, i, first):
                def row(n):
                    if n > 1:
                        bank_full(act, stage, 2 + n, i)
                    b = bank_full(act, stage, n, i)
                    free(A(MODROW[stage][n % 2][0:2, :], b[0:2, :], ACT.Copy), n)

                def columns(n):
                    b = bank_full(act, stage, 4 + n, i)
                    for m in range(4):
                        j = 4 * (first + n) + m
                        ins = A(modc[:, l, j, :], b[:, 2 * m:2 * m + 2], ACT.Identity, bias=col("b_mod", 48 * l + j))
                    free(ins, 4 + n)
                for n in range(4):
                    row(n)
                    if n > 0:
                        columns(n - 1)
                columns(3)

            def gate_rows(stage):
                for c in range(2):
                    for h in range(2):
                        g = GROUPS[stage][2 * c + h]
                        b = bank_full(act, stage, g)
                        free(A(gate_row[:, c, 512 * h:512 * h + 512], b, ACT.Copy), g)

            act.wait_ge(s("inputs"), 16 * 8)
            cond = cols[:, COLS["cond"]:COLS["cond"] + 16].rearrange("p (k c) -> p k c", k=KD)
            A(condT[:], cond, ACT.Sigmoid).then_inc(s("cond_sig"), 1)
            adaln_jobs(0, "mod0", 0, 0)
            norm("norm0", 0, 0)
            act.wait_ge(s("pad_zero"), 1)
            for g in range(14):
                if g >= 2:
                    act.wait_ge(s("shifted"), g - 1)
                b = bank_full(act, "in0", g)
                L(A(pad[:, g % 2, 1:129], b[:, 0:P], ACT.Copy))
                free(A(pad[:, g % 2, 130:386], b[:, P:T], ACT.Copy), g)
                if g + 2 < 14:
                    weight_hi("in", 0, g + 2)
            for t in range(TILES):
                b = bank_full(act, "in0", 14 + t)
                free(A(mla[:, t, :], b[:, 0:448], ACT.Copy), 14 + t)
            for t in range(TILES):
                copied(act, "in0", 14 + t)
            act.wait_ge(s("shifted"), 14)
            for t in range(TILES):
                L(A(padt[:, 0:256], mla[:, t, 0:256], ACT.Square, accum_out=stat[:, t:t + 1]))
                ins = A(padt[:, 0:128], mla[:, t, 256:384], ACT.Square, accum_out=stat[:, 3 + t:4 + t])
                if t < 2:
                    L(ins)
            tell(act, ins, "latent_squares", 1)
            root(0, 6)
            for g in range(3):
                b = bank_full(act, "qkvT", g)
                if g < 2:
                    free(A(qcT[:, g, :], b[:, 0:T], ACT.Copy), g)
                else:
                    free(A(ckvT, b, ACT.Copy), g)
            for t in range(TILES):
                for h in range(2):
                    b = bank_full(act, "up", 2 * t + h)
                    free(A(q[:, t, 2 * h:2 * h + 2, :], b[:, 0:384].rearrange("p (h c) -> p h c", h=2), ACT.Copy), 2 * t + h)
            root(6, 12)
            root(6, 16)
            for h in range(MLA_HEADS):
                b = bank_full(act, "headT", 4 * h)
                free(A(qTn[:, h, :], b[:, 0:T], ACT.Copy), 4 * h)
                b = bank_full(act, "headT", 4 * h + 1)
                free(A(qTr[0:64, h, :], b[0:64, 0:T], ACT.Copy), 4 * h + 1)
            scale = float(QK) ** -0.5
            for h in range(MLA_HEADS):
                if h > 0:
                    bank_full(act, "att", 4, h - 1)
                for t, (o, n) in enumerate(((0, 1), (1, 3), (4, 3))):
                    act.wait_ge(s("row_max"), 3 * h + t + 1)
                    b = bank_full(act, "att", t, h)
                    ins = A(prob[:, o:o + n, :], b[:, 0:n * P].rearrange("p (n c) -> p n c", n=n), ACT.Exp,
                            bias=stat[:, 3 * h + t:3 * h + t + 1], scale=scale,
                            accum_out=stat[:, 12 + 3 * h + t:13 + 3 * h + t])
                    free(ins, t)
                    copied(act, "att", t, h)
                    A(stat[:, 60:61], ones[:, 0:1], ACT.Copy).then_inc(s("exps"), 1)
                    act.wait_ge(s("exps"), 3 * h + t + 1)
                b = bank_full(act, "att", 3, h)
                free(A(probT[:, 0:4, :], blocks(b), ACT.Copy), 3)
                b = bank_full(act, "att", 5, h)
                free(A(hT[:, 4 + h, :], b[:, 0:T], ACT.Copy), 5)
            act.wait_ge(s("lora_zero"), 1)
            A(lora_rhs[0:64, 0, :], wdad[0:64, :], ACT.Tanh).then_inc(s("lora_in"), 1)
            A(lora_rhs[64:P, 1, :], wdad[64:P, :], ACT.Copy).then_inc(s("lora_in"), 1)
            A(gd, gd, ACT.Sigmoid).then_inc(s("lora_in"), 1)
            for m in range(PAIRS):
                b = bank_full(act, "knorm", m)
                free(A(cum[:, m, :], b[:, 0:T], ACT.Sqrt), m)
            for d in range(2):
                if d == 0:
                    act.wait_ge(s("kk_ready"), 1)
                else:
                    act.wait_ge(s("dir_done"), 1)
                for part, (dst, name) in enumerate(((ld, "w0"), (lr, "a0"))):
                    for m in range(PAIRS):
                        g = 8 * d + 4 * part + m
                        b = bank_full(act, "lora", g)
                        free(A(dst[:, m, :], b[:, 0:T], ACT.Sigmoid, bias=col(name, 4 * d + m)), g)
                act.wait_ge(s("cums"), d + 1)
                if d == 0:
                    act.wait_ge(s("stored"), 16 * 2)
                L(A(elast[:, d], cum[:, :, CH - 1:T:CH], ACT.Exp))
                tr, ta, tb = (tilde[:, 4 * d + n] for n in range(3))
                for n, (dst, src, sign) in enumerate((((tr, cum, 1.0), (ta, cumx, 1.0), (tb, cum, -1.0)),
                                                      ((tr, cumx, -1.0), (ta, cum, -1.0), (tb, cumx, 1.0)))[d]):
                    ins = A(dst, src, ACT.Exp, scale=sign)
                    if n < 2:
                        L(ins)
                tell(act, ins, "decays", d + 1)
            for m in range(PAIRS):
                b = bank_full(act, "lora", 16 + m)
                free(A(hT[:, m, :], b[:, 0:T], ACT.Copy), 16 + m)
            for i in range(2):
                if i > 0:
                    bank_full(act, "mod0b", 7, i - 1)
                adaln_jobs(0, "mod0b", i, 4 + 4 * i)

            def scan_item(stage, i, d, base, chunk):
                ex, NT, NTm, Tm, TT, Pm, KT, RkT, RbT, ktok, btok, Vt, Xt, SA = scan_mem[d]
                for n, src in ((3, tilde[:, 4 * d + 3]), (4, rkv[:, 8:12, :])):
                    L(A(ex[0:64, n, :, 0:CH], src[0:64, :, bass.ts(chunk, CH)], ACT.Copy))
                    A(ex[64:P, n, :, CH:P], src[64:P, :, bass.ts(chunk, CH)], ACT.Copy).then_inc(s("expanded%d" % d), 1)
                yield
                for g, dst in ((1, NT), (5, ktok), (6, btok), (7, Vt)):
                    b = bank_full(act, stage, sg(d, g), i)
                    free(A(dst, b[:, 0:dst.shape[1]], ACT.Copy), sg(d, g))
                g = 8
                for lev in range(1, 6):
                    yield
                    b = bank_full(act, stage, sg(d, g), i)
                    free(A(Pm, b, ACT.Copy), sg(d, g))
                    g += 3
                for g, dst in ((22, Xt), (23, SA)):
                    yield
                    b = bank_full(act, stage, sg(d, g), i)
                    free(A(dst, b[:, 0:256], ACT.Copy), sg(d, g))

            for d in range(2):
                act.wait_ge(s("state_ready%d" % d), 1)
            c0, per = enter(0), 4
            with act.Fori(0, 2) as i:
                back = act.snap(1 - i)
                enter(i * per + c0)
                both(scan_item("scanp", i, d, 0, (i, back)[d]) for d in range(2))
            for d in range(2):
                b = bank_full(act, "state_out", d)
                free(A(s0[:, d].rearrange("v h k -> v (h k)"), b[0:64, :], ACT.Copy), d)
                copied(act, "state_out", d)
                A(stat[:, 60:61], ones[:, 0:1], ACT.Copy).then_inc(s("state_copied"), 1)
                act.wait_ge(s("state_copied"), d + 1)
            with act.Fori(0, 4) as i:
                back = act.snap(5 - i)
                enter(i * per + (c0 + 2 * per))
                both(scan_item("scans", i, d, 2, (i + 2, back)[d]) for d in range(2))
            enter(c0 + 6 * per)
            act.wait_ge(s("scan_done"), 1)
            for n in range(PAIRS * NCH):
                m, c = n // NCH, n % NCH
                if n >= 2:
                    act.wait_ge(s("bonus_mm"), n - 1)
                L(A(bexp[0:64, n % 2, 0:CH], bonus_w[0:64, m, c * CH:(c + 1) * CH], ACT.Copy))
                A(bexp[64:P, n % 2, CH:P], bonus_w[64:P, m, c * CH:(c + 1) * CH], ACT.Copy).then_inc(s("bonus_exp"), 1)
                if n == 10:
                    root(24, 24)
            for c in range(NCH):
                if c > 1:
                    bank_full(act, "yT", c - 2)
                for h in range(2):
                    ins = A(zexp[64 * h:64 * h + 64, c % 2, :, CH * h:CH * h + CH],
                            rkv[64 * h:64 * h + 64, 8:12, c * CH:(c + 1) * CH], ACT.Copy)
                    if h == 0:
                        L(ins)
                ins.then_inc(s("vexp_ready"), 1)
            gate_rows("gate0")

            def peer(l):
                norm("norm%db" % l, l, 1)

                def scores(a):
                    b = bank_full(act, "wk%d" % l, KEYG[a])
                    free(A(sc[:, a, :, :], b[:, 0:T].rearrange("p (t c) -> p t c", t=TILES), ACT.Copy), KEYG[a])
                for a in range(SIDES):
                    b = bank_full(act, "wk%d" % l, WQ[a])
                    free(A(qT[:, a, :], b[:, 0:T], ACT.Copy), WQ[a])
                    if a + 2 < SIDES:
                        weight_hi("wq", l, a + 2)
                    if a > 0:
                        scores(a - 1)
                scores(SIDES - 1)
                for t in range(TILES):
                    if l == 0:
                        adaln_jobs(1, "sel0", t, 4 * t)
                    act.wait_ge(s("shifted_tops"), 3 * l + t + 1)
                    A(pick[:, 2, :], pick[:, 2, :], ACT.Exp).then_inc(s("tops_exp"), 1)
                    b = bank_full(act, "sel%d" % l, SELG[l], t)
                    free(A(sel[:, 0:3, t * P:(t + 1) * P], b[:, 0:384].rearrange("p (n c) -> p n c", n=3), ACT.Copy),
                         SELG[l])
                j0 = JOB[("uv", l)]
                c0 = P * l

                def u_part(u):
                    A(us[:, u % 2, 0, :], table(j0, u)[0], ACT.Copy).then_inc(s("u_hi"), 1)

                def step(lin, sl, j, u, par, where):
                    n = lin(STEPS, c0 + u)
                    if where != "end":
                        if u % 2 == 1:
                            job = j0 + (u + 1) // 2
                            act.wait_ge(s("landed%d" % SLOT_OF[job]), lin(16, 16 * LANDING[job]))
                        at_least(act, "h_ready", n)
                        u_part(u + 1)
                    at_least(act, "v_done", lin(STEPS, (P - 1) * l + u - 1))
                    A(vs[:, u % 2, 0, :], table(j0, u)[1], ACT.Copy).then_inc(s("v_hi"), 1)
                    act.wait_ge(s("h_ready"), n + 1)
                    at_least(act, "g_made", n - 1)
                    A(gel[:, u % 2, :], psum[:, 6, 0:T], ACT.Gelu_apprx_tanh).then_inc(s("gelu_done"), 1)
                    act.wait_ge(s("g_made"), n + 1)
                    A(gs[:, u % 2, 0, :], gw[:, u % 2, :], ACT.Copy).then_inc(s("g_hi"), 1)
                landed(act, j0)
                u_part(0)

                def first_dense(g, tok, par):
                    act.wait_ge(s("w_ready"), g + 1)
                    A(wd[:, 0, bass.ds(tok, BUILD), :], psum[:, 6 + par, 0:SLICE * BUILD].rearrange(
                        "p (t n) -> p t n", t=BUILD), ACT.Copy).then_inc(s("w_copied"), 1)
                with act.Fori(0, NG // 2) as i:
                    for par in range(2):
                        first_dense(i * 2 + (SLICES * NG * l + par), i * (2 * BUILD) + par * BUILD, par)
                expert_steps(act, step)
                gate_rows("gate%db" % l)
            peer(0)

            norm("norm1", 1, 0)
            act.wait_ge(s("pad_zero"), 2)
            for g in range(24):
                if g >= 2:
                    act.wait_ge(s("shifted"), 14 + g - 1)
                b = bank_full(act, "in1", g)
                L(A(pad1[:, g % 2, 1:129], b[:, 0:P], ACT.Identity, bias=col("b_in", g)))
                free(A(pad1[:, g % 2, 130:386], b[:, P:T], ACT.Identity, bias=col("b_in", g)), g)
                if g + 2 < 24:
                    weight_hi("in", 1, g + 2)
            for n in range(2):
                act.wait_ge(s("sin_in"), n + 1)
                A(hid[0:64, n, :], htmp[0:64, 0, :], ACT.Sin).then_inc(s("hid_ready"), 1)
            act.wait_ge(s("filters"), 1)
            na = 0
            for tiles in ((1, 2), (0,)):
                for h in range(2):
                    for t in tiles:
                        for part in range(2):
                            o = part * D + 512 * h
                            A(absf[:, na, :], filt[:, t, o:o + 512], ACT.Abs).then_inc(s("abs_ready"), 1)
                            na += 1
            copied(act, "filtF", 11)
            for g in range(6):
                b = bank_full(act, "zT", g)
                free(A(z[:, g // 2, 512 * (g % 2):512 * (g % 2) + 512], b, ACT.Copy), g)
            for g in range(12):
                b = bank_full(act, "zF", g)
                free(A(zF[:, g // 2, 512 * (g % 2):512 * (g % 2) + 512], b, ACT.Copy), g)
            gate_rows("gate1")
            peer(1)

    return nc


def weight_jobs(w):
    n = -(-w.shape[1] // 512)
    out = np.zeros((n, P, KD, 512), np.float32)
    for j in range(n):
        part = w[:, 512 * j:512 * (j + 1)]
        out[j, :, :, :part.shape[1]] = part.reshape(KD, P, -1).transpose(1, 0, 2)
    return out.reshape(n, P, SLOT)


def uv_jobs(u, v):
    out = np.empty((UVJOBS, P, 2, 2 * D), np.float32)
    out[:, :, 0, :] = u.reshape(P, UVJOBS, 2, KD, P).transpose(1, 4, 2, 3, 0).reshape(UVJOBS, P, 2 * D)
    out[:, :, 1, :] = v.reshape(P, UVJOBS, 2 * D).transpose(1, 0, 2)
    return out.reshape(UVJOBS, P, SLOT)


def column(v):
    return v.reshape(-1, P).T


def dft_tables(L):
    t, f = np.arange(L)[:, None], np.arange(L)[None, :]
    ang = 2 * np.pi * ((t * f) % (2 * L)) / (2 * L)
    re, im = np.cos(ang), -np.sin(ang)
    ny = np.cos(np.pi * t[:, 0])
    im[:, 0] = ny
    fwd = np.concatenate([re, im], 1)
    imb = np.sin(ang)
    imb[:, 0] = ny
    bwd = np.concatenate([re, imb], 1)
    bwd[0] = 0
    w = np.full(L, 2.0)
    w[0] = 1.0
    inv_re = (w[:, None] * np.cos(ang.T)) / (2 * L)
    inv_im = (-2.0 * np.sin(ang.T)) / (2 * L)
    inv_im[0] = ny / (2 * L)
    inv = np.concatenate([inv_re, inv_im], 0)
    return [a.astype(np.float32) for a in (fwd, bwd, inv)]


def hyena_constants():
    zpos, window = np.zeros((33, T), np.float32), np.zeros((P, 3, D), np.float32)
    f = np.float32
    deltas = np.linspace(np.log(1e-2) / 0.3, np.log(1e-2) / 1.5, D).astype(f)
    bands = np.linspace(1e-4, 15, 16).astype(f)
    for L, o in ((P, 0), (2 * P, P)):
        t = np.arange(L, dtype=f)[:, None]
        unit = t / f(L - 1)
        ang = (f(2.0 * np.pi) * t * bands / f(L)).astype(f)
        zpos[:, o:o + L] = np.concatenate([unit, np.cos(ang), -np.sin(ang)], 1).T
        win = np.exp(-unit * np.abs(deltas))
        window[:, o // P:(o + L) // P, :] = win.reshape(-1, P, D).transpose(1, 0, 2)
    return zpos, window


def scan_masks():
    j, t = np.arange(P)[:, None] % CH, np.arange(P)[None, :] % CH
    out = []
    for d in range(2):
        for lev in range(6):
            b = 1 << lev
            m = (t // (2 * b) == j // (2 * b)) & ((t // b) % 2 == 1) & ((j // b) % 2 == 0)
            if d == 1:
                m = (t // (2 * b) == j // (2 * b)) & ((j // b) % 2 == 1) & ((t // b) % 2 == 0)
            out.append(m)
    out += [j < t, j <= t, j > t, j >= t]
    return np.stack(out, 1).astype(np.float32)


def fill(n):
    return np.zeros((P, n), np.float32)


def kernel(**inputs):
    import concourse.bacc as bacc
    from concourse.bass_utils import run_bass_kernel_spmd

    a = {k: np.ascontiguousarray(v) for k, v in inputs.items()}
    f = np.float32
    zpos, window = hyena_constants()
    jobs = []
    for l in range(2):
        if l == 0:
            mod = weight_jobs(a["w_mod"][0])
            jobs.append(mod[0:4])
            w = a["ab_w_in"][0]
            jobs += [weight_jobs(w[:, :1792]), weight_jobs(w[:, 1792:])]
            small = fill(SLOT)
            small[:, 0:1536] = a["mla_q_up"][0].reshape(2, P, 768).transpose(1, 0, 2).reshape(P, 1536)
            small[:, 1536:2560] = a["mla_kv_up"][0]
            small[0:64, 2560:3584] = a["rw_w2"][0].transpose(1, 0, 2).reshape(64, 1024)
            small[64:P, 2560:3584] = a["rw_a2"][0].transpose(1, 0, 2).reshape(64, 1024)
            small[:, 3584:4096] = a["rw_g2"][0]
            jobs += [small[None], mod[4:12], np.zeros((2, P, SLOT), np.float32), weight_jobs(a["ab_w_out"][0])]
        else:
            jobs.append(weight_jobs(a["hy_w_in"][0]))
            win, flt, dft = fill(SLOT), fill(SLOT), fill(SLOT)
            win[:, 0:3072] = window.reshape(P, 3072)
            flt[0:64, 0:2048] = a["hy_f_w3"][0]
            flt[0:33, 2048:2432] = zpos
            flt[0:33, 2432:2496] = a["hy_f_w1"][0]
            flt[0:64, 2496:2560] = a["hy_f_w2"][0]
            o = 0
            for L in (2 * P, P):
                for m in dft_tables(L):
                    n = m.size // P
                    dft[:, o:o + n] = m.reshape(-1, P, m.shape[1]).transpose(1, 0, 2).reshape(P, n)
                    o += n
            jobs += [win[None], flt[None], dft[None], weight_jobs(a["hy_w_out"][0])]
        keys = fill(SLOT)
        keys[:, 0:2048] = a["peer_keys"][l].reshape(SIDES, P, P).transpose(2, 0, 1).reshape(P, 2048)
        jobs += [keys[None], weight_jobs(a["peer_w_q"][l])]
        if l == 0:
            jobs.append(weight_jobs(a["w_mod"][1]))
        jobs.append(uv_jobs(a["peer_u"][l], a["peer_v"][l]))
    stream = np.concatenate(jobs)
    assert len(stream) == N_JOBS

    cols = fill(N_COLS)

    def put(name, block):
        cols[:block.shape[0], COLS[name]:COLS[name] + block.shape[1]] = block
    put("mu", column(a["rw_mu"][0]))
    put("k_k", column(a["rw_k_k"][0]))
    put("k_a", column(a["rw_k_a"][0]))
    put("r_k", column(a["rw_r_k"][0]))
    put("w0", column(a["rw_w0"][0]))
    put("a0", column(a["rw_a0"][0]))
    put("g", column(a["norm_g"]))
    put("b_mod", column(a["b_mod"]))
    put("b_in", column(a["hy_b_in"][0]))
    put("conv_w", column(a["hy_conv_w"][0]))
    put("conv_b", column(a["hy_conv_b"][0]))
    put("bias", column(a["hy_bias"][0]))
    put("f_b1", a["hy_f_b1"][0][:, None])
    put("f_b2", a["hy_f_b2"][0][:, None])
    put("freq", a["hy_f_freq"][0][:, None])
    put("cond", np.stack([a["c_ctx"], a["c"][0]], 1).reshape(KD, P, 2).transpose(1, 0, 2).reshape(P, 16))

    consts = fill(832)
    i = np.arange(P)
    consts[:, 0:128] = np.eye(P)
    consts[:, 128:256] = i[:, None] // 64 == i[None, :] // 64
    consts[:, 256:320] = i[:, None] % 64 == np.arange(64)[None, :]
    consts[:, 320:704] = (np.arange(T) % CH != 0)[None, :]
    consts[:, 704:832] = i[None, :]

    pos = np.arange(2 * P)
    inv = (f(10000.0) ** (-np.arange(16, dtype=f) / f(16))).astype(f)
    ang = np.concatenate([(pos // 64)[:, None].astype(f) * inv, (pos % 64)[:, None].astype(f) * inv], 1)
    rope = np.stack([np.cos(ang), np.sin(ang)]).astype(f)

    arrays = {
        "x_prompt": a["x_prompt"], "x_sample": a["x_sample"], "cols": cols, "consts": consts,
        "masks": scan_masks(), "rope": rope, "stream": stream,
        "rows": np.concatenate([a["mla_q_norm"][0], a["mla_kv_norm"][0], a["mla_qn"][0], a["mla_kn"][0]])[None],
        "cache_mla_ckv": a["cache_mla_ckv"], "cache_mla_kpe": a["cache_mla_kpe"],
        "state_rwkv_fwd": a["state_rwkv_fwd"], "state_rwkv_bwd": a["state_rwkv_bwd"],
        "lnx_g": a["rw_lnx_g"][0].reshape(PAIRS, 2, CH).transpose(1, 0, 2).copy(),
        "lnx_b": a["rw_lnx_b"][0].reshape(PAIRS, 2, CH).transpose(1, 0, 2).copy(),
    }
    outs = {"o_prompt": (1, P, D), "o_sample": (1, 2 * P, D), "o_fwd": (1, 1, HEADS, 64, 64),
            "o_bwd": (1, 1, HEADS, 64, 64), "o_ckv": (1, 1, P, 128), "o_kpe": (1, 1, P, 64)}
    nc = bacc.Bacc("TRN2", target_bir_lowering=False, num_devices=1)
    io = {}
    for k, v in arrays.items():
        io[k] = nc.dram_tensor("in_" + k, v.shape, F32, kind="ExternalInput").ap()
    for k, shape in outs.items():
        io[k] = nc.dram_tensor(k, shape, F32, kind="ExternalOutput").ap()
    build(nc, io)
    r = run_bass_kernel_spmd(nc, [{"in_" + k: v for k, v in arrays.items()}], core_ids=[0]).results[0]
    return tuple(r[k] for k in outs)
```
